# Optimizing a Trainium2 kernel written in Bass

```python
import jax, jax.numpy as jnp
from jax import lax
import numpy as np

D_MODEL = 1024
BATCH = 1
SEQ = 512
DEPTH = 1

MEM_LEN = 256
MIX_W = D_MODEL // 2
N_BRANCH = 4
CONV_W = MIX_W
CONV_K = 31
DN_HEADS = 4
DN_HEAD_DIM = MIX_W // DN_HEADS
DN_CONV_K = 4
DN_CHUNK = 64
GM_W = MIX_W
GM_GROUPS = 4
GM_CHUNK = 128
POOL_W = MIX_W
POOL_WINDOWS = (2, 4, 8, 16)
POOL_GROUPS = len(POOL_WINDOWS)
XA_HEADS = 4
XA_HEAD_DIM = D_MODEL // XA_HEADS
FFN_W = 4 * D_MODEL
IN_W = 2 * CONV_W + 4 * MIX_W + 2 * DN_HEADS + 2 * GM_W + POOL_W + N_BRANCH * D_MODEL

kernel_name = 'hybrid_gated_conv_deltanet_gmlp_pool_trunk'

def rmsnorm(x, g, eps=1e-6):
    xf = x.astype(jnp.float32)
    y = xf * lax.rsqrt(jnp.mean(xf * xf, axis=-1, keepdims=True) + eps)
    return (y * g.astype(jnp.float32)).astype(x.dtype)

def layernorm(x, g, b, eps=1e-5):
    xf = x.astype(jnp.float32)
    mu = jnp.mean(xf, axis=-1, keepdims=True)
    var = jnp.mean(jnp.square(xf - mu), axis=-1, keepdims=True)
    y = (xf - mu) * lax.rsqrt(var + eps)
    return (y * g.astype(jnp.float32) + b.astype(jnp.float32)).astype(x.dtype)

def causal_dwconv(x, w):
    K, C = w.shape
    return lax.conv_general_dilated(x, w[:, None, :].astype(x.dtype), window_strides=(1,),
                                    padding=[(K - 1, 0)],
                                    dimension_numbers=('NWC', 'WIO', 'NWC'),
                                    feature_group_count=C)

def gated_delta_rule(q, k, v, g, beta):
    B, S, H, Dk = q.shape
    Dv = v.shape[-1]
    C = DN_CHUNK
    N = S // C
    f32 = jnp.float32
    q = q.astype(f32)
    k = k.astype(f32)
    q = q * lax.rsqrt(jnp.sum(q * q, -1, keepdims=True) + 1e-6) * (Dk ** -0.5)
    k = k * lax.rsqrt(jnp.sum(k * k, -1, keepdims=True) + 1e-6)

    def chunks(t):
        t = t.astype(f32).reshape((B, N, C, H) + t.shape[3:])
        return jnp.moveaxis(t, 3, 2)

    q, k, v, g, beta = chunks(q), chunks(k), chunks(v), chunks(g), chunks(beta)
    gam = jnp.cumsum(g, axis=-1)
    causal = jnp.tril(jnp.ones((C, C), bool))
    strict = jnp.tril(jnp.ones((C, C), bool), -1)
    decay = jnp.exp(jnp.where(causal, gam[..., :, None] - gam[..., None, :], -jnp.inf))
    kb = k * beta[..., None]
    a = jnp.where(strict, jnp.einsum('bnhid,bnhjd->bnhij', kb, k) * decay, 0.0)
    rhs = jnp.concatenate([v * beta[..., None], kb * jnp.exp(gam)[..., None]], axis=-1)
    sol = lax.linalg.triangular_solve(a + jnp.eye(C, dtype=f32), rhs, left_side=True,
                                      lower=True, unit_diagonal=True)
    u, w = sol[..., :Dv], sol[..., Dv:]
    attn = jnp.einsum('bnhid,bnhjd->bnhij', q, k) * decay
    q_dec = q * jnp.exp(gam)[..., None]
    g_last = gam[..., -1]
    k_dec = k * jnp.exp(g_last[..., None] - gam)[..., None]

    def step(state, xs):
        u_n, w_n, attn_n, qd_n, kd_n, gl_n = xs
        v_new = u_n - jnp.einsum('bhck,bhkv->bhcv', w_n, state)
        o_n = (jnp.einsum('bhck,bhkv->bhcv', qd_n, state)
               + jnp.einsum('bhij,bhjv->bhiv', attn_n, v_new))
        state = (state * jnp.exp(gl_n)[..., None, None]
                 + jnp.einsum('bhck,bhcv->bhkv', kd_n, v_new))
        return state, o_n

    xs = tuple(jnp.moveaxis(t, 1, 0) for t in (u, w, attn, q_dec, k_dec, g_last))
    state0 = jnp.zeros((B, H, Dk, Dv), f32)
    _, o = lax.scan(step, state0, xs)
    return jnp.transpose(o, (1, 0, 3, 2, 4)).reshape(B, S, H, Dv)

def multiscale_pool(x):
    B, S, C = x.shape
    Cg = C // POOL_GROUPS
    xf = x.astype(jnp.float32).reshape(B, S, POOL_GROUPS, Cg)
    cs = jnp.cumsum(xf, axis=1)
    cs_pad = jnp.concatenate([jnp.zeros((B, 1, POOL_GROUPS, Cg), jnp.float32), cs], axis=1)
    t = jnp.arange(S)
    outs = []
    for gi, win in enumerate(POOL_WINDOWS):
        upper = cs[:, :, gi]
        lower = jnp.concatenate([jnp.zeros((B, win - 1, Cg), jnp.float32),
                                 cs_pad[:, :S - win + 1, gi]], axis=1)
        count = jnp.minimum(t + 1, win).astype(jnp.float32)[None, :, None]
        outs.append((upper - lower) / count)
    return (jnp.stack(outs, axis=2) - xf).astype(x.dtype)

def hybrid_mixer(h, w_in, conv_a_w, conv_a_b, ln_a_g, ln_a_b, dn_conv_w, dn_a_log, dn_dt_bias,
                 dn_norm_g, gm_ln_g, gm_ln_b, gm_ws, gm_bs, pool_w, pool_scale, w_branch, w_out):
    B, S, _ = h.shape
    f32 = jnp.float32
    z = h @ w_in
    sizes = [2 * CONV_W, MIX_W, MIX_W, MIX_W, MIX_W, DN_HEADS, DN_HEADS, 2 * GM_W, POOL_W,
             N_BRANCH * D_MODEL]
    idx = np.cumsum(sizes)[:-1].tolist()
    a_in, dq, dk, dv, dgate, dbeta, da, gm_in, pool_in, gate_in = jnp.split(z, idx, axis=-1)

    a1, a2 = jnp.split(a_in, 2, axis=-1)
    a = a1 * jax.nn.sigmoid(a2)
    a = causal_dwconv(a, conv_a_w) + conv_a_b
    a = jax.nn.silu(layernorm(a, ln_a_g, ln_a_b))

    qkv = jax.nn.silu(causal_dwconv(jnp.concatenate([dq, dk, dv], axis=-1), dn_conv_w))
    q, k, v = jnp.split(qkv, 3, axis=-1)
    heads = lambda t: t.reshape(B, S, DN_HEADS, DN_HEAD_DIM)
    beta = jax.nn.sigmoid(dbeta.astype(f32))
    g = -jnp.exp(dn_a_log.astype(f32)) * jax.nn.softplus(da.astype(f32) + dn_dt_bias.astype(f32))
    o = gated_delta_rule(heads(q), heads(k), heads(v), g, beta)
    o = rmsnorm(o, dn_norm_g) * jax.nn.silu(heads(dgate).astype(f32))
    o = o.reshape(B, S, MIX_W).astype(h.dtype)

    u, vg = jnp.split(jax.nn.gelu(gm_in, approximate=False), 2, axis=-1)
    vg = layernorm(vg, gm_ln_g, gm_ln_b)
    vc = vg.reshape(B, S // GM_CHUNK, GM_CHUNK, GM_GROUPS, GM_W // GM_GROUPS)
    ws = gm_ws * jnp.tril(jnp.ones((GM_CHUNK, GM_CHUNK), gm_ws.dtype))
    mixed = jnp.einsum('gts,bnsgc->bntgc', ws, vc) + gm_bs.T[:, :, None]
    c = u * mixed.reshape(B, S, GM_W)

    p = multiscale_pool(pool_in)
    p = jnp.einsum('bsgc,gcd->bsgd', p, pool_w).reshape(B, S, POOL_W) * pool_scale

    gates = jax.nn.sigmoid(gate_in).reshape(B, S, N_BRANCH, D_MODEL)
    br = jnp.stack([a, o, c, p], axis=2)
    proj = jnp.einsum('bsnc,ncd->bsnd', br, w_branch)
    merged = jnp.sum(gates * proj, axis=2)
    return merged @ w_out

def memory_cross_attention(h, mem, norm_mem, wq, wkv, wo):
    B, S, _ = h.shape
    M = mem.shape[1]
    m = rmsnorm(mem, norm_mem)
    q = (h @ wq).reshape(B, S, XA_HEADS, XA_HEAD_DIM)
    k, v = jnp.split(m @ wkv, 2, axis=-1)
    k = k.reshape(B, M, XA_HEADS, XA_HEAD_DIM)
    v = v.reshape(B, M, XA_HEADS, XA_HEAD_DIM)
    s = jnp.einsum('bshd,bmhd->bhsm', q, k).astype(jnp.float32) * (XA_HEAD_DIM ** -0.5)
    pr = jax.nn.softmax(s, axis=-1).astype(v.dtype)
    o = jnp.einsum('bhsm,bmhd->bshd', pr, v).reshape(B, S, D_MODEL)
    return o @ wo

def squared_relu_mlp(h, w1, w2):
    return jnp.square(jax.nn.relu(h @ w1)) @ w2

def setup_inputs(seed: int = 0) -> dict:
    key = jax.random.key(seed)
    ks = jax.random.split(key, 40)
    f32 = jnp.float32
    L, D = DEPTH, D_MODEL
    nrm = lambda i, shape, scale: jax.random.normal(ks[i], shape, f32) * scale
    gain = lambda i, shape: 1.0 + 0.1 * jax.random.normal(ks[i], shape, f32)
    dt = jnp.exp(jax.random.uniform(ks[10], (L, DN_HEADS), f32) * (np.log(0.1) - np.log(0.001))
                 + np.log(0.001))
    return {
        'x': nrm(0, (BATCH, SEQ, D), 1.0),
        'mem': nrm(1, (BATCH, MEM_LEN, D), 1.0),
        'norm_mix': gain(2, (L, D)),
        'w_in': nrm(3, (L, D, IN_W), D ** -0.5),
        'conv_a_w': nrm(4, (L, CONV_K, CONV_W), CONV_K ** -0.5),
        'conv_a_b': nrm(5, (L, CONV_W), 0.02),
        'ln_a_g': gain(6, (L, CONV_W)),
        'ln_a_b': nrm(7, (L, CONV_W), 0.02),
        'dn_conv_w': nrm(8, (L, DN_CONV_K, 3 * MIX_W), DN_CONV_K ** -0.5),
        'dn_a_log': jnp.log(jax.random.uniform(ks[9], (L, DN_HEADS), f32, 1.0, 16.0)),
        'dn_dt_bias': dt + jnp.log(-jnp.expm1(-dt)),
        'dn_norm_g': gain(11, (L, DN_HEAD_DIM)),
        'gm_ln_g': gain(12, (L, GM_W)),
        'gm_ln_b': nrm(13, (L, GM_W), 0.02),
        'gm_ws': nrm(14, (L, GM_GROUPS, GM_CHUNK, GM_CHUNK), GM_CHUNK ** -0.5),
        'gm_bs': gain(15, (L, GM_GROUPS, GM_CHUNK)),
        'pool_w': nrm(16, (L, POOL_GROUPS, POOL_W // POOL_GROUPS, POOL_W // POOL_GROUPS),
                      (POOL_W // POOL_GROUPS) ** -0.5),
        'pool_scale': gain(17, (L, POOL_W)),
        'w_branch': nrm(18, (L, N_BRANCH, MIX_W, D), MIX_W ** -0.5),
        'w_out': nrm(19, (L, D, D), D ** -0.5),
        'norm_xa': gain(20, (L, D)),
        'norm_mem': gain(21, (L, D)),
        'xa_wq': nrm(22, (L, D, D), D ** -0.5),
        'xa_wkv': nrm(23, (L, D, 2 * D), D ** -0.5),
        'xa_wo': nrm(24, (L, D, D), D ** -0.5),
        'norm_mlp': gain(25, (L, D)),
        'mlp_w1': nrm(26, (L, D, FFN_W), D ** -0.5),
        'mlp_w2': nrm(27, (L, FFN_W, D), FFN_W ** -0.5),
        'norm_f': gain(28, (D,)),
    }

def reference(x, mem, norm_mix, w_in, conv_a_w, conv_a_b, ln_a_g, ln_a_b, dn_conv_w, dn_a_log,
              dn_dt_bias, dn_norm_g, gm_ln_g, gm_ln_b, gm_ws, gm_bs, pool_w, pool_scale, w_branch,
              w_out, norm_xa, norm_mem, xa_wq, xa_wkv, xa_wo, norm_mlp, mlp_w1, mlp_w2, norm_f):
    for l in range(DEPTH):
        x = x + hybrid_mixer(rmsnorm(x, norm_mix[l]), w_in[l], conv_a_w[l], conv_a_b[l], ln_a_g[l],
                             ln_a_b[l], dn_conv_w[l], dn_a_log[l], dn_dt_bias[l], dn_norm_g[l],
                             gm_ln_g[l], gm_ln_b[l], gm_ws[l], gm_bs[l], pool_w[l], pool_scale[l],
                             w_branch[l], w_out[l])
        x = x + memory_cross_attention(rmsnorm(x, norm_xa[l]), mem, norm_mem[l], xa_wq[l],
                                       xa_wkv[l], xa_wo[l])
        x = x + squared_relu_mlp(rmsnorm(x, norm_mlp[l]), mlp_w1[l], mlp_w2[l])
    return rmsnorm(x, norm_f)


_drawn_inputs = setup_inputs


def setup_inputs(seed=0):
    import zlib

    import numpy as np

    out = dict(_drawn_inputs(seed))
    spreads = {}
    factors = {'conv_a_b': 4.802,
     'ln_a_b': 8.0,
     'gm_ln_g': 2.718,
     'gm_ln_b': 8.0,
     'norm_xa': 6.385,
     'norm_mem': 4.121}
    for name, (base, spread) in spreads.items():
        noise = np.random.default_rng([zlib.crc32(name.encode()), seed]).standard_normal(out[name].shape)
        drawn = base * np.exp(spread * noise) if base else spread * noise
        out[name] = __import__('jax').numpy.asarray(drawn.astype(out[name].dtype))
    for name, factor in factors.items():
        out[name] = (out[name] * factor).astype(out[name].dtype)
    return out
```

```python
from contextlib import ExitStack

import numpy as np

import concourse.bass as bass
from concourse import mybir

P = 128
D = 1024
T = 512
MEM = 256
KT = D // P
NT = T // P
MIX = D // 2
MT = MIX // P
HEADS = 4
CK = 31
PADC = 32
FFN = 4 * D
RING = 3

F32 = mybir.dt.float32
F32R = mybir.dt.float32r
ACT = mybir.ActivationFunctionType
ALU = mybir.AluOpType
X = mybir.AxisListType.X

PHASES = [("pool", 4), ("gm", 8), ("qkv", 12), ("conv", 8), ("merge_p", 12), ("merge_c", 12),
          ("dgate", 4), ("merge_o", 12), ("merge_a", 12), ("out", 8), ("kv", 16), ("q", 8),
          ("wo", 8), ("w1", 32), ("w2", 32)]
FIRST = {}
NU = 0
for _name, _n in PHASES:
    FIRST[_name] = NU
    NU += _n

TAKE = {"dgate": 0, "out": 4, "kv": 12, "q": 28, "wo": 36, "w1": 44}

COLS = {}
_at = 0
for _name, _n in [("norm_mix", 8), ("norm_xa", 8), ("norm_mem", 8), ("norm_mlp", 8),
                  ("conv_w", 4 * PADC), ("conv_b", 4), ("ln_a_g", 4), ("ln_a_b", 4),
                  ("dn_w", 48), ("dn_g", 1), ("pool_s", 4), ("eps6", 1), ("eps5", 1)]:
    COLS[_name] = _at
    _at += _n
NCOLS = _at

CONST = {}
_at = 0
for _name, _n in [("ident", P), ("tri", P), ("strict", P), ("level0", P), ("levels", 6 * P),
                  ("ones", P), ("head", 64)]:
    CONST[_name] = _at
    _at += _n
NCONST = _at


def units(eng, first, count):
    n = count // RING
    with eng.Fori(0, n) as i:
        for j in range(RING):
            yield i * RING + j, (first + j) % RING, (first + j) // RING + i
    for k in range(n * RING, count):
        yield k, (first + k) % RING, (first + k) // RING


class Steps:

    def __init__(self, eng, sem):
        self.eng, self.sem, self.before, self.here, self.turn = eng, sem, 0, 0, None

    def value(self):
        return self.before + self.here + (0 if self.turn is None else self.turn)

    def done(self, ins):
        ins.then_inc(self.sem, 1)
        self.here += 1
        self.eng.wait_ge(self.sem, self.value())

    def enter(self, i, per):
        self.before += self.here
        self.here, self.turn, self.per = 0, i * per, per

    def leave(self, n):
        assert self.here == self.per
        self.before += n * self.per
        self.here, self.turn = 0, None


def trunk(nc, wall, x_t, mem_t, w_bd, cols_d, rows_d, gains_d, ws_t, pool_w, const_d, norm_f, out):
    with ExitStack() as ctx:
        def sb(name, shape, dt=F32):
            return ctx.enter_context(nc.sbuf_tensor(name, shape, dt))

        def sem(name):
            return ctx.enter_context(nc.semaphore(name))

        raw = sb("raw", [P, RING, 1024])
        whi = sb("whi", [P, RING, 1024], F32R)
        wlo = sb("wlo", [P, RING, 1024], F32R)
        ahi = sb("ahi", [P, KT, T], F32R)
        alo = sb("alo", [P, KT, T], F32R)
        bhi = sb("bhi", [P, MT, T], F32R)
        blo = sb("blo", [P, MT, T], F32R)
        bdhi = sb("bdhi", [P, KT * 8], F32R)
        bdlo = sb("bdlo", [P, KT * 8], F32R)
        stream = sb("stream", [P, KT, T])
        buf = sb("buf", [P, 8, 2048])
        conv = sb("conv", [P, 4 * (T + PADC) + 4 * T])
        sig = sb("sig", [P, 2, T])
        sq = sb("sq", [P, 2, T])
        rstd = sb("rstd", [P, T])
        state = sb("state", [P, 2, HEADS, P])
        vnew = sb("vnew", [P, HEADS, P])
        cols = sb("cols", [P, NCOLS])
        const = sb("const", [P, NCONST])
        rows = sb("rows", [P, 8])
        wbd = sb("wbd", [P, KT * 8])
        small = sb("small", [P, 16, 16])
        ps = ctx.enter_context(nc.psum_tensor("ps", [P, 8, T], F32))

        def col(name, k=0):
            return cols[:, COLS[name] + k:COLS[name] + k + 1]

        ident, tri, strict, level0 = (const[:, CONST[n]:CONST[n] + P] for n in ("ident", "tri", "strict", "level0"))
        ones = const[:, CONST["ones"]:CONST["ones"] + P]
        head_inv = const[:, CONST["head"]:CONST["head"] + 64].rearrange("p (g t) -> p g t", g=4)

        def tiles(k, n=1):
            return buf[:, k:k + n, :].rearrange("p a (t c) -> p (a t) c", c=T)

        def mats(k):
            return buf[:, k, :].rearrange("p (h c t) -> p h c t", h=HEADS, c=NT)

        z = buf[:, :, :].rearrange("p a (t c) -> p (a t) c", c=T)
        zflat = buf[:, :, :].rearrange("p a c -> p (a c)")
        xin = tiles(6, 2)
        a_pad = conv[:, 0:4 * (T + PADC)].rearrange("p (t c) -> p t c", t=4)
        a_acc = conv[:, 4 * (T + PADC):].rearrange("p (t c) -> p t c", t=4)
        tmp_a = conv[:, 0:2048].rearrange("p (t c) -> p t c", t=4)
        tmp_b = conv[:, 2048:4096].rearrange("p (t c) -> p t c", t=4)
        early = stream[:, :, :].rearrange("p a c -> p (a c)")
        gm_g, gm_b, gm_bias = early[:, 0:512], early[:, 512:1024], early[:, 1024:1536]
        ws, pw = early[:, 1536:2048], early[:, 2048:2560]
        gains = early[:, 0:1536]

        beta, g_col, gam, egl = (small[:, n, :] for n in range(4))
        kbe_s, kd_s, s5, s6, s7, s8 = (small[:, n, :] for n in range(4, 10))
        stat = small[:, 10:12, :].rearrange("p a b -> p (a b)")
        mv = small[:, 12, :]
        r_ln = small[:, 13, :]
        negmax, denom = small[:, 14, :], small[:, 15, :]

        raw_in = [sem(f"raw_in{s}") for s in range(RING)]
        hi_ready, lo_ready = sem("hi_ready"), sem("lo_ready")
        unit_done = sem("unit_done")
        z_free = sem("z_free")
        taken = sem("taken")
        gate_free = sem("gate_free")
        merged = sem("merged")
        dve_step, act_step = sem("dve_step"), sem("act_step")
        names = ("const_in params_in x_in x2_in mem_in early_in f_in out_sent sq_ready sq_added sum_ready std_ready "
                 "h_ready h_hi h_split bd_hi bd_split bd_ready bd_exp bd_act gelu_ready pooled pool_mm pool_scaled "
                 "p_hi p_split vt_ready vn_std vn_ready mix_ready c_ready c_hi c_split conv_q silu_ready "
                 "sig2_ready qkv_t qkv_tok qk_sq qk_std qk_norm qk_back qk_feat gamrow gb_ready gam_ready egr_ready "
                 "dec_pre dec_exp attn_mm a_mm x0_ready x0_done y0_mm y0_ready lv_t lv_masked lv_p lv_y lv_x lv_xt "
                 "v_tok o_sum vn_var ca_var x_mean kbe_ready wt_mm wt_ready v_mm v_ready s_mm s_ready o_mm o_tok o_sq o_std o_norm o_back "
                 "dg_silu o_feat o_hi o_split ca_ready ca_t ca_std ca_norm ca_back ca_silu a_hi a_split m_hi m_split "
                 "mem_sq mem_sum mem_std m_hi2 m_split2 x1_sq x1_sum x1_std x1_hi x1_split vt2 vt2_taken "
                 "score_mm nmax exp_done probs_ready pt_mm pt_ready pv_mm attn_o ao_hi ao_split x2_sq x2_sum x2_std "
                 "x2_hi x2_split x2t_mm x2t_ready h1_ready h1_hi h1_split fin_mm y_ready y_sq y_std y_out "
                 "gram_ready decay_ready mem_added x1_added x2_added mem_r x1_r x2_r").split()
        s = {n: sem(n) for n in names}

        block = ctx.enter_context(nc.Block())

        @block.sync
        def _(sp):
            for k in range(4):
                sp.dma_start(xin[:, 2 * k:2 * k + 2, :], x_t[:, 2 * k:2 * k + 2, :]).then_inc(s["x_in"], 16)
            for u in range(RING):
                sp.dma_start(raw[:, u, :], wall[u]).then_inc(raw_in[u], 16)
            for k, slot, _ in units(sp, RING, NU - RING):
                sp.wait_ge(lo_ready, k + 1)
                sp.dma_start(raw[:, slot, :], wall[k + RING]).then_inc(raw_in[slot], 16)
            out_v = out[0].rearrange("(t p) d -> p t d", p=P)
            y_out = conv[:, 0:4096].rearrange("p (t d) -> p t d", t=NT)
            for t in range(NT):
                sp.wait_ge(s["y_out"], t + 1)
                sp.dma_start(out_v[:, t, :], y_out[:, t, :]).then_inc(s["out_sent"], 16)
            sp.wait_ge(s["out_sent"], 16 * NT)

        @block.gpsimd
        def _(pool):
            for k, slot, _ in units(pool, 0, NU):
                pool.wait_ge(hi_ready, k + 1)
                nc.gpsimd.tensor_tensor(wlo[:, slot, :], raw[:, slot, :], whi[:, slot, :].bitcast(F32),
                                        ALU.subtract).then_inc(lo_ready, 1)

        @block.tensor
        def _(pe):
            def three(dst, st_hi, st_lo, mv_hi, mv_lo, first, last):
                nc.tensor.matmul(dst, st_hi, mv_hi, start=first, stop=False, skip_group_check=True)
                nc.tensor.matmul(dst, st_hi, mv_lo, start=False, stop=False, skip_group_check=True)
                return nc.tensor.matmul(dst, st_lo, mv_hi, start=False, stop=last, skip_group_check=True)

            def unit(slot, bank, ready, n=T, hi=ahi, lo=alo):
                fhi = hi[:, :, :].rearrange("p a c -> p (a c)")
                flo = lo[:, :, :].rearrange("p a c -> p (a c)")
                for k in range(KT):
                    pe.wait_ge(ready, k + 1)
                    last = three(ps[:, bank, 0:n], whi[:, slot, k * P:(k + 1) * P], wlo[:, slot, k * P:(k + 1) * P],
                                 fhi[:, k * n:(k + 1) * n], flo[:, k * n:(k + 1) * n], k == 0, k == KT - 1)
                last.then_inc(unit_done, 1)

            def z_units(first, count):
                for k, slot, _ in units(pe, first, count):
                    pe.wait_ge(lo_ready, k + first + 1)
                    pe.wait_ge(z_free, k + first + 1)
                    unit(slot, slot, s["h_split"])

            def taken_units(name, ready, count=None, skip=0, **how):
                first = FIRST[name] + skip
                for k, slot, _ in units(pe, first, count or dict(PHASES)[name]):
                    pe.wait_ge(lo_ready, k + first + 1)
                    pe.wait_ge(taken, k + TAKE[name] + skip + 1)
                    unit(slot, slot, ready, **how)

            def merge(name, n, ready):
                first = FIRST[name]
                with pe.Fori(0, 4) as i:
                    for j in range(2):
                        slot = (first + j) % RING
                        pe.wait_ge(lo_ready, i * 3 + first + j + 1)
                        pe.wait_ge(gate_free, i * 2 + 8 * n + j + 1)
                        unit(slot, j, s["h_split"])
                    slot = (first + 2) % RING
                    pe.wait_ge(lo_ready, i * 3 + first + 3)
                    pe.wait_ge(merged, i * 2 + 8 * n + 2)
                    pe.wait_ge(ready, MT)
                    for e in range(2):
                        for c in range(MT):
                            at = (c * 2 + e) * P
                            last = three(ps[:, 2 + e, :], whi[:, slot, at:at + P], wlo[:, slot, at:at + P],
                                         bhi[:, c, :], blo[:, c, :], c == 0, c == MT - 1)
                    last.then_inc(unit_done, 1)

            def mean_square(src, n, ready, tell):
                pe.wait_ge(ready, 1)
                nc.tensor.matmul(ps[:, 7, 0:n], ones, src, start=True, stop=True).then_inc(tell, 1)

            pe.wait_ge(s["const_in"], 16)
            mean_square(sq[:, 0, :], T, s["sum_ready"], s["x_mean"])
            pe.wait_ge(s["bd_split"], 1)
            pe.wait_ge(s["h_split"], KT)
            for t in range(NT):
                for k in range(KT):
                    last = three(ps[:, 4, t * 8:t * 8 + 8], ahi[:, k, t * P:(t + 1) * P], alo[:, k, t * P:(t + 1) * P],
                                 bdhi[:, k * 8:k * 8 + 8], bdlo[:, k * 8:k * 8 + 8], k == 0, k == KT - 1)
            last.then_inc(s["bd_ready"], 1)
            z_units(0, 24)
            pe.wait_ge(s["pooled"], 1)
            for g in range(4):
                nc.tensor.matmul(ps[:, 4 + g, :], pw[:, g * P:(g + 1) * P], z[:, g, :],
                                 start=True, stop=True).then_inc(s["pool_mm"], 1)
            pe.wait_ge(s["gelu_ready"], 2)
            pe.wait_ge(s["pool_scaled"], 4)
            for t in range(NT):
                for f in range(4):
                    last = nc.tensor.transpose(ps[:, 4 + t, f * P:(f + 1) * P], tiles(2)[:, f, t * P:(t + 1) * P], ident)
                last.then_inc(s["vt_ready"], 1)
            z_units(24, 8)
            pe.wait_ge(s["vn_ready"], 1)
            vn = tiles(2)
            for g in range(4):
                for n in range(NT):
                    last = nc.tensor.matmul(ps[:, 4 + g, n * P:(n + 1) * P], vn[:, n, g * P:(g + 1) * P],
                                            ws[:, g * P:(g + 1) * P], start=True, stop=True)
                last.then_inc(s["mix_ready"], 1)
            pe.wait_ge(z_free, 3 + 32)
            merge("merge_p", 0, s["p_split"])
            pe.wait_ge(s["silu_ready"], 3)
            pe.wait_ge(s["c_ready"], 4)
            for n in range(3):
                for h in range(HEADS):
                    if n:
                        pe.wait_ge(s["qkv_tok"], 4 * (n - 1) + h + 1)
                    for c in range(NT):
                        last = nc.tensor.transpose(ps[:, 4 + h, c * P:(c + 1) * P],
                                                   tiles(2 + n)[:, h, c * P:(c + 1) * P], ident)
                    last.then_inc(s["qkv_t"], 1)
            merge("merge_c", 1, s["c_split"])
            pe.wait_ge(s["qkv_tok"], 8)
            pe.wait_ge(s["v_tok"], 4)
            pe.wait_ge(s["gb_ready"], 1)
            nc.tensor.matmul(ps[:, 4, 0:16], tri, g_col, start=True, stop=True).then_inc(s["gamrow"], 1)
            pe.wait_ge(s["gam_ready"], 1)
            for h in range(HEADS):
                for c in range(NT):
                    n = h * NT + c
                    last = nc.tensor.matmul(ps[:, 4 + h, c * P:(c + 1) * P], g_col[:, n:n + 1].to_broadcast([P, P]),
                                            tri, start=True, stop=True)
                last.then_inc(s["gamrow"], 1)
            pe.wait_ge(gate_free, 2 + 16)
            pe.wait_ge(merged, 2 + 16)
            for n in range(2):
                pe.wait_ge(s["qk_norm"], n + 1)
                for h in range(HEADS):
                    if n:
                        pe.wait_ge(s["qk_feat"], h + 1)
                    for c in range(NT):
                        last = nc.tensor.transpose(ps[:, h, c * P:(c + 1) * P], mats(5 + n)[:, h, c, :], ident)
                    last.then_inc(s["qk_back"], 1)
            qn, kn = mats(2), mats(3)
            pe.wait_ge(s["qk_feat"], 8)
            for h in range(HEADS):
                for c in range(NT):
                    last = nc.tensor.matmul(ps[:, h, c * P:(c + 1) * P], kn[:, h, c, :], kn[:, h, c, :],
                                            start=True, stop=True)
                last.then_inc(s["a_mm"], 1)
            pe.wait_ge(s["dec_pre"], 8)
            for h in range(HEADS):
                for c in range(NT):
                    last = nc.tensor.matmul(ps[:, 4 + h, c * P:(c + 1) * P], kn[:, h, c, :], qn[:, h, c, :],
                                            start=True, stop=True)
                last.then_inc(s["attn_mm"], 1)
            a_m, x_m, y_m, t_m = mats(0), mats(2), mats(3), mats(1)
            for h in range(HEADS):
                pe.wait_ge(s["x0_ready"], h + 1)
                for c in range(NT):
                    last = nc.tensor.transpose(ps[:, h, c * P:(c + 1) * P], x_m[:, h, c, :], ident)
                last.then_inc(s["y0_mm"], 1)
            pe.wait_ge(s["gram_ready"], 4)
            with pe.Fori(0, 6) as lv:
                for h in range(HEADS):
                    pe.wait_ge(s["lv_y"], lv * 4 + h + 1)
                    pe.wait_ge(s["lv_x"], lv * 4 + h + 1)
                    for c in range(NT):
                        last = nc.tensor.matmul(ps[:, 4 + h, c * P:(c + 1) * P], a_m[:, h, c, :], y_m[:, h, c, :],
                                                start=True, stop=True)
                    last.then_inc(s["lv_t"], 1)
                for h in range(HEADS):
                    pe.wait_ge(s["lv_masked"], lv * 4 + h + 1)
                    for c in range(NT):
                        last = nc.tensor.matmul(ps[:, h, c * P:(c + 1) * P], x_m[:, h, c, :], t_m[:, h, c, :],
                                                start=True, stop=True)
                    last.then_inc(s["lv_p"], 1)
                for h in range(HEADS):
                    pe.wait_ge(s["lv_y"], lv * 4 + h + 5)
                    for c in range(NT):
                        last = nc.tensor.transpose(ps[:, 4 + h, c * P:(c + 1) * P], y_m[:, h, c, :], ident)
                    last.then_inc(s["lv_xt"], 1)
            kbe = mats(2)
            pe.wait_ge(s["kbe_ready"], 1)
            pe.wait_ge(s["lv_x"], 28)
            for h in range(HEADS):
                for c in range(NT):
                    last = nc.tensor.matmul(ps[:, 4 + h, c * P:(c + 1) * P], kbe[:, h, c, :], y_m[:, h, c, :],
                                            start=True, stop=True)
                last.then_inc(s["wt_mm"], 1)
            wt, qd, at_m, kd, vb = mats(1), mats(4), mats(5), mats(6), mats(7)
            for c in range(NT):
                old, new = state[:, (c + 1) % 2], state[:, c % 2]
                if c == 0:
                    pe.wait_ge(s["lv_y"], 28)
                if c == 1:
                    pe.wait_ge(s["wt_ready"], 4)
                if c:
                    pe.wait_ge(s["v_ready"], c)
                    pe.wait_ge(s["s_ready"], c)
                for h in range(HEADS):
                    last = nc.tensor.matmul(ps[:, 0, h * P:(h + 1) * P], y_m[:, h, c, :], vb[:, h, c, :],
                                            start=True, stop=c == 0)
                    if c:
                        last = nc.tensor.matmul(ps[:, 0, h * P:(h + 1) * P], wt[:, h, c, :], old[:, h, :],
                                                start=False, stop=True)
                last.then_inc(s["v_mm"], 1)
                pe.wait_ge(s["v_ready"], c + 1)
                if c < NT - 1:
                    if c == 0:
                        pe.wait_ge(s["kbe_ready"], 2)
                    for h in range(HEADS):
                        last = nc.tensor.matmul(ps[:, 1, h * P:(h + 1) * P], kd[:, h, c, :], vnew[:, h, :],
                                                start=True, stop=True)
                    last.then_inc(s["s_mm"], 1)
                ob = 2 + c % 2
                if c >= 2:
                    pe.wait_ge(s["o_tok"], c - 1)
                for h in range(HEADS):
                    if c:
                        nc.tensor.matmul(ps[:, ob, h * P:(h + 1) * P], qd[:, h, c, :], old[:, h, :],
                                         start=True, stop=False)
                    last = nc.tensor.matmul(ps[:, ob, h * P:(h + 1) * P], at_m[:, h, c, :], vnew[:, h, :],
                                            start=c == 0, stop=True)
                last.then_inc(s["o_mm"], 1)
            pe.wait_ge(s["o_tok"], NT)
            taken_units("dgate", s["h_split"])
            pe.wait_ge(s["ca_ready"], 1)
            pe.wait_ge(s["wt_ready"], 4)
            for t in range(NT):
                for f in range(4):
                    last = nc.tensor.transpose(ps[:, 4 + t, f * P:(f + 1) * P], a_acc[:, f, t * P:(t + 1) * P], ident)
                last.then_inc(s["ca_t"], 1)
            o_tok = buf[:, 0, :].rearrange("p (c h v) -> p c h v", c=NT, h=HEADS)
            pe.wait_ge(s["o_norm"], 1)
            pe.wait_ge(taken, 3 + 4)
            for h in range(HEADS):
                for c in range(NT):
                    last = nc.tensor.transpose(ps[:, h, c * P:(c + 1) * P], o_tok[:, c, h, :], ident)
                last.then_inc(s["o_back"], 1)
            pe.wait_ge(s["o_feat"], 4)
            merge("merge_o", 2, s["o_split"])
            pe.wait_ge(s["ca_norm"], 1)
            for f in range(4):
                for t in range(NT):
                    last = nc.tensor.transpose(ps[:, 4 + f, t * P:(t + 1) * P], tiles(2)[:, t, f * P:(f + 1) * P], ident)
                last.then_inc(s["ca_back"], 1)
            merge("merge_a", 3, s["a_split"])
            pe.wait_ge(gate_free, 2 + 32)
            pe.wait_ge(merged, 2 + 32)
            taken_units("out", s["m_split"])
            mean_square(sq[:, 0, 0:MEM], MEM, s["mem_added"], s["mem_sum"])
            taken_units("kv", s["m_split2"], n=MEM, hi=bhi, lo=blo)
            pe.wait_ge(s["mem_r"], 1)
            mean_square(sq[:, 0, :], T, s["x1_added"], s["x1_sum"])
            for m in range(2):
                for f in range(KT):
                    pe.wait_ge(taken, 3 + TAKE["kv"] + 8 + f + 1)
                    last = nc.tensor.transpose(ps[:, 3 + 2 * m + f // 4, (f % 4) * P:(f % 4 + 1) * P],
                                               buf[:, 3, f * MEM + m * P:f * MEM + (m + 1) * P], ident)
                last.then_inc(s["vt2"], 1)
            taken_units("q", s["x1_split"])
            q_t, k_t = tiles(0, 2), buf[:, 2, :]
            pe.wait_ge(taken, 3 + TAKE["q"] + 8)
            pe.wait_ge(s["vt2_taken"], 2)
            pe.wait_ge(s["x1_r"], 1)
            for h in range(HEADS):
                for pair in range(2):
                    for e in range(2):
                        t = 2 * pair + e
                        for d in range(2):
                            f = 2 * h + d
                            last = nc.tensor.matmul(ps[:, 2 * h + pair, e * MEM:(e + 1) * MEM],
                                                    q_t[:, f, t * P:(t + 1) * P], k_t[:, f * MEM:(f + 1) * MEM],
                                                    start=d == 0, stop=d == 1)
                    last.then_inc(s["score_mm"], 1)
            probs = buf[:, 5:7, :].rearrange("p a (b c) -> p (a b) c", c=T)
            for b in range(8):
                pe.wait_ge(s["probs_ready"], b + 1)
                for m in range(2):
                    for e in range(2):
                        last = nc.tensor.transpose(ps[:, b, (2 * m + e) * P:(2 * m + e + 1) * P],
                                                   probs[:, b, e * MEM + m * P:e * MEM + (m + 1) * P], ident)
                last.then_inc(s["pt_mm"], 1)
            v_tok = buf[:, 4, :].rearrange("p (m f) -> p m f", m=2)
            p_t = conv[:, 0:4096].rearrange("p (m h t) -> p m h t", m=2, h=HEADS)
            for f in range(KT):
                h = f // 2
                pe.wait_ge(s["pt_ready"], max(2 * h + 2, f + 1))
                for m in range(2):
                    last = nc.tensor.matmul(ps[:, f, :], v_tok[:, m, f * P:(f + 1) * P], p_t[:, m, h, :],
                                            start=m == 0, stop=m == 1)
                last.then_inc(s["pv_mm"], 1)
            pe.wait_ge(s["attn_o"], 8)
            taken_units("wo", s["ao_split"])
            mean_square(sq[:, 0, :], T, s["x2_added"], s["x2_sum"])

            def w1_unit(first, skip, count):
                for k, slot, _ in units(pe, first, count):
                    pe.wait_ge(lo_ready, k + first + 1)
                    pe.wait_ge(taken, k + TAKE["w1"] + skip + 1)
                    for kk in range(KT):
                        hi, lo = (bhi, blo) if kk < 4 else (ahi, alo)
                        pe.wait_ge(s["x2_split"], kk + 1)
                        last = three(ps[:, slot, :], whi[:, slot, kk * P:(kk + 1) * P], wlo[:, slot, kk * P:(kk + 1) * P],
                                     hi[:, kk, :], lo[:, kk, :], kk == 0, kk == KT - 1)
                    last.then_inc(unit_done, 1)

            w1 = FIRST["w1"]
            w1_unit(w1, 0, 12)
            for half in range(2):
                if half:
                    w1_unit(w1 + 12, 12, 12)
                    pe.wait_ge(s["x2t_ready"], 4)
                for t in range(NT):
                    for f in range(4):
                        last = nc.tensor.transpose(ps[:, 3 + t, f * P:(f + 1) * P],
                                                   stream[:, 4 * half + f, t * P:(t + 1) * P], ident)
                    last.then_inc(s["x2t_mm"], 1)
            w1_unit(w1 + 24, 24, 8)
            pe.wait_ge(taken, 3 + TAKE["w1"] + 32)
            pe.wait_ge(s["x2t_ready"], 8)
            pe.wait_ge(s["x2_r"], 1)

            def w2_unit(k, slot, start, stop):
                pe.wait_ge(lo_ready, k + FIRST["w2"] + 1)
                pe.wait_ge(s["h1_split"], k + 1)
                for t in range(NT):
                    for half in range(2):
                        last = three(ps[:, 2 * t + half, :], ahi[:, slot, t * P:(t + 1) * P],
                                     alo[:, slot, t * P:(t + 1) * P], whi[:, slot, half * T:(half + 1) * T],
                                     wlo[:, slot, half * T:(half + 1) * T], start, stop)
                last.then_inc(unit_done, 1)

            w2 = FIRST["w2"]
            w2_unit(0, w2 % RING, True, False)
            for k, slot, _ in units(pe, w2 + 1, 30):
                w2_unit(k + 1, slot, False, False)
            w2_unit(31, (w2 + 31) % RING, False, True)

        @block.scalar
        def _(act):
            steps = Steps(act, act_step)
            act.sem_inc(z_free, 3)
            act.sem_inc(gate_free, 2)
            act.dma_start(const[:, :], const_d).then_inc(s["const_in"], 16)
            act.dma_start(cols[:, :], cols_d).then_inc(s["params_in"], 16)
            act.dma_start(rows[:, :], rows_d.partition_broadcast(P)).then_inc(s["params_in"], 16)
            act.dma_start(wbd[:, :], w_bd).then_inc(s["params_in"], 16)
            act.dma_start(gains, gains_d.partition_broadcast(P)).then_inc(s["early_in"], 16)
            act.dma_start(ws, ws_t).then_inc(s["early_in"], 16)
            act.dma_start(pw, pool_w).then_inc(s["early_in"], 16)

            def high(slot, turn):
                act.wait_ge(raw_in[slot], (turn + 1) * 16)
                nc.scalar.activation(whi[:, slot, :], raw[:, slot, :], ACT.Copy).then_inc(hi_ready, 1)

            def feed(first, k, slot, turn):
                act.wait_ge(unit_done, k + first + 1)
                high(slot, turn + 1)

            def feed_units(first, count):
                for k, slot, turn in units(act, first, count):
                    feed(first, k, slot, turn)

            def z_units(first, count):
                for k, slot, turn in units(act, first, count):
                    act.wait_ge(unit_done, k + first + 1)
                    nc.scalar.activation(zflat[:, bass.ds((k + first) * T, T)], ps[:, slot, :],
                                         ACT.Copy).then_inc(z_free, 1)
                    high(slot, turn + 1)

            def merge(name, n):
                first = FIRST[name]
                with act.Fori(0, 4) as i:
                    for j in range(RING):
                        slot, turn = (first + j) % RING, i + (first + j) // RING
                        act.wait_ge(unit_done, i * 3 + first + j + 1)
                        if j < 2:
                            act.wait_ge(merged, i * 2 + 8 * n + 2)
                            nc.scalar.activation(sig[:, j, :], ps[:, j, :], ACT.Sigmoid).then_inc(gate_free, 1)
                        high(slot, turn + 1)

            def split_high(dst, src, tell, scale=1.0):
                nc.scalar.activation(dst, src, ACT.Copy, scale=scale).then_inc(tell, 1)

            for k in range(KT):
                act.wait_ge(s["x_in"], 64)
                if k >= 2:
                    act.wait_ge(s["sq_added"], k - 1)
                nc.scalar.activation(tmp_a[:, k % 2, :], xin[:, k, :], ACT.Square).then_inc(s["sq_ready"], 1)
            act.wait_ge(s["params_in"], 48)
            act.wait_ge(s["x_mean"], 1)
            nc.scalar.activation(rstd[:, :], ps[:, 7, :], ACT.Sqrt, bias=col("eps6"), scale=1.0 / D).then_inc(s["std_ready"], 1)
            nc.scalar.activation(bdhi[:, :], wbd[:, :], ACT.Copy).then_inc(s["bd_hi"], 1)
            for u in range(RING):
                high(u, 0)
            for k in range(KT):
                act.wait_ge(s["h_hi"], k + 1)
                split_high(ahi[:, k, :], xin[:, k, :], s["h_ready"])
            act.wait_ge(s["bd_exp"], 1)
            nc.scalar.activation(s5, s6, ACT.Exp, scale=-1.0).then_inc(s["bd_act"], 1)
            nc.scalar.activation(rows[:, 0:4], rows[:, 0:4], ACT.Exp).then_inc(s["bd_act"], 1)
            act.wait_ge(s["bd_exp"], 2)
            nc.scalar.activation(s6, s5, ACT.Ln).then_inc(s["bd_act"], 1)
            act.wait_ge(s["bd_ready"], 1)
            nc.scalar.activation(beta, ps[:, 4, 0:32].rearrange("p (t e) -> p e t", e=8)[:, 0:4, :],
                                 ACT.Sigmoid).then_inc(s["bd_act"], 1)
            z_units(0, 12)
            act.wait_ge(z_free, 3 + 12)
            for n in range(2):
                nc.scalar.activation(buf[:, 1 + n, :], buf[:, 1 + n, :], ACT.Gelu).then_inc(s["gelu_ready"], 1)
            z_units(12, 12)
            for g in range(4):
                act.wait_ge(s["pool_mm"], g + 1)
                if g == 0:
                    act.wait_ge(s["pool_mm"], 4)
                nc.scalar.activation(z[:, g, :], ps[:, 4 + g, :], ACT.Copy, scale=col("pool_s", g)).then_inc(s["pool_scaled"], 1)
            act.wait_ge(s["pool_scaled"], 4)
            for g in range(4):
                split_high(bhi[:, g, :], z[:, g, :], s["p_hi"])
            act.wait_ge(s["vn_var"], 1)
            nc.scalar.activation(r_ln[:, 0:4], r_ln[:, 0:4], ACT.Sqrt, bias=col("eps5")).then_inc(s["vn_std"], 1)
            z_units(24, 8)
            act.wait_ge(z_free, 3 + 32)
            nc.scalar.activation(buf[:, 6, :], buf[:, 6, :], ACT.Sigmoid).then_inc(s["sig2_ready"], 1)
            for n in range(3):
                act.wait_ge(s["conv_q"], n + 1)
                nc.scalar.activation(buf[:, 2 + n, :], buf[:, 2 + n, :], ACT.Silu).then_inc(s["silu_ready"], 1)
            merge("merge_p", 0)
            act.wait_ge(s["c_ready"], 8)
            act.wait_ge(unit_done, FIRST["merge_c"])
            for g in range(4):
                split_high(bhi[:, g, :], tiles(1)[:, g, :], s["c_hi"])
            for n in range(2):
                for h in range(HEADS):
                    act.wait_ge(s["qkv_t"], 4 * n + h + 1)
                    nc.scalar.activation(tiles(5 + n)[:, h, :], ps[:, 4 + h, :], ACT.Copy).then_inc(s["qkv_tok"], 1)
                act.wait_ge(s["qkv_tok"], 4 * n + 4)
                act.wait_ge(s["qkv_t"], 4 * n + 4)
                nc.scalar.activation(buf[:, 2 + n, :], buf[:, 5 + n, :], ACT.Square).then_inc(s["qk_sq"], 1)
            for n in range(2):
                act.wait_ge(s["qk_std"], n + 1)
                nc.scalar.activation((s7, s8)[n], (s7, s8)[n], ACT.Sqrt).then_inc(s["std_ready"], 1)
            merge("merge_c", 1)
            for h in range(HEADS):
                act.wait_ge(s["gamrow"], h + 2)
                nc.scalar.activation(tiles(4)[:, h, :], ps[:, 4 + h, :], ACT.Exp).then_inc(s["egr_ready"], 1)
                act.wait_ge(s["qk_back"], h + 1)
                nc.scalar.activation(tiles(2)[:, h, :], ps[:, h, :], ACT.Copy).then_inc(s["qk_feat"], 1)
            for h in range(HEADS):
                act.wait_ge(s["qk_back"], h + 5)
                nc.scalar.activation(tiles(3)[:, h, :], ps[:, h, :], ACT.Copy).then_inc(s["qk_feat"], 1)
            act.wait_ge(s["decay_ready"], 1)
            nc.scalar.activation(kbe_s, gam, ACT.Exp).then_inc(s["bd_act"], 1)
            nc.scalar.activation(kd_s, kd_s, ACT.Exp).then_inc(s["bd_act"], 1)
            nc.scalar.activation(egl, egl, ACT.Exp).then_inc(s["bd_act"], 1)
            for h in range(HEADS):
                act.wait_ge(s["dec_pre"], h + 5)
                nc.scalar.activation(tiles(0)[:, h, :], tiles(0)[:, h, :], ACT.Exp, scale=-1.0).then_inc(s["dec_exp"], 1)
            for h in range(HEADS):
                nc.scalar.activation(tiles(5)[:, h, :], tiles(5)[:, h, :], ACT.Exp).then_inc(s["dec_exp"], 1)
            act.sem_inc(s["lv_x"], 4)
            with act.Fori(0, 6) as lv:
                for h in range(HEADS):
                    act.wait_ge(s["lv_xt"], lv * 4 + h + 1)
                    nc.scalar.activation(tiles(2)[:, h, :], ps[:, 4 + h, :], ACT.Copy).then_inc(s["lv_x"], 1)
            for h in range(HEADS):
                act.wait_ge(s["wt_mm"], h + 1)
                nc.scalar.activation(tiles(1)[:, h, :], ps[:, 4 + h, :], ACT.Copy, scale=-1.0).then_inc(s["wt_ready"], 1)
            for c in range(NT):
                act.wait_ge(s["o_mm"], c + 1)
                nc.scalar.activation(tiles(0)[:, c, :], ps[:, 2 + c % 2, :], ACT.Copy).then_inc(s["o_tok"], 1)
            act.wait_ge(s["o_tok"], NT)
            nc.scalar.activation(buf[:, 3, :], buf[:, 0, :], ACT.Square).then_inc(s["o_sq"], 1)
            act.wait_ge(s["o_sum"], 1)
            nc.scalar.activation(s5, s5, ACT.Sqrt, bias=col("eps6"), scale=1.0 / P).then_inc(s["o_std"], 1)
            feed_units(FIRST["dgate"], 4)
            act.wait_ge(taken, 3 + 4)
            nc.scalar.activation(buf[:, 4, :], buf[:, 4, :], ACT.Silu).then_inc(s["dg_silu"], 1)
            for h in range(HEADS):
                act.wait_ge(s["o_feat"], h + 1)
                split_high(bhi[:, h, :], tiles(6)[:, h, :], s["o_hi"])
            act.wait_ge(s["ca_var"], 1)
            nc.scalar.activation(r_ln[:, 0:4], r_ln[:, 0:4], ACT.Sqrt, bias=col("eps5")).then_inc(s["ca_std"], 1)
            merge("merge_o", 2)
            for f in range(4):
                act.wait_ge(s["ca_back"], f + 1)
                nc.scalar.activation(tiles(3)[:, f, :], ps[:, 4 + f, :], ACT.Silu, bias=col("ln_a_b", f),
                                     scale=col("ln_a_g", f)).then_inc(s["ca_silu"], 1)
            act.wait_ge(s["ca_silu"], 4)
            for f in range(4):
                split_high(bhi[:, f, :], tiles(3)[:, f, :], s["a_hi"])
            act.wait_ge(s["o_split"], 4)
            act.dma_start(xin, x_t).then_inc(s["x2_in"], 16)
            act.wait_ge(s["dg_silu"], 1)
            act.wait_ge(s["o_feat"], 4)
            act.dma_start(buf[:, 4, :], mem_t).then_inc(s["mem_in"], 16)
            merge("merge_a", 3)
            act.wait_ge(merged, 2 + 32)
            act.dma_start(sig[:, :, :].rearrange("p a c -> p (a c)"), norm_f.partition_broadcast(P)).then_inc(s["f_in"], 16)
            act.wait_ge(unit_done, FIRST["out"])
            for k in range(KT):
                split_high(ahi[:, k, :], stream[:, k, :], s["m_hi"])
            act.wait_ge(s["mem_in"], 16)
            for k in range(KT):
                split_high(bhi[:, k // 2, (k % 2) * MEM:(k % 2 + 1) * MEM], buf[:, 4, k * MEM:(k + 1) * MEM],
                           s["m_hi2"], col("norm_mem", k))
            mem_sq = buf[:, 5, :]
            nc.scalar.activation(mem_sq, buf[:, 4, :], ACT.Square).then_inc(s["mem_sq"], 1)

            def taken_feed(name):
                first = FIRST[name]
                for k, slot, turn in units(act, first, 8):
                    feed(first, k, slot, turn)

            taken_feed("out")
            for k in range(KT):
                act.wait_ge(taken, 3 + TAKE["out"] + k + 1)
                split_high(ahi[:, k, :], stream[:, k, :], s["x1_hi"], col("norm_xa", k))
            act.wait_ge(s["mem_sum"], 1)
            nc.scalar.activation(sq[:, 1, 0:MEM], ps[:, 7, 0:MEM], ACT.Sqrt, bias=col("eps6"), scale=1.0 / D).then_inc(s["mem_std"], 1)

            def squares_of_stream(added, tell):
                for k in range(KT):
                    if k >= 2:
                        act.wait_ge(added, k - 1)
                    nc.scalar.activation(tmp_b[:, k % 2, :], stream[:, k, :], ACT.Square).then_inc(tell, 1)

            squares_of_stream(s["x1_sq"], s["x1_std"])
            feed_units(FIRST["kv"], 16)
            act.wait_ge(s["x1_sum"], 1)
            nc.scalar.activation(sq[:, 1, :], ps[:, 7, :], ACT.Sqrt, bias=col("eps6"), scale=1.0 / D).then_inc(s["x1_std"], 1)
            for m in range(2):
                act.wait_ge(s["vt2"], m + 1)
                nc.scalar.activation(buf[:, 4, m * 1024:(m + 1) * 1024].rearrange("p (a c) -> p a c", a=2),
                                     ps[:, 3 + 2 * m:5 + 2 * m, :], ACT.Copy).then_inc(s["vt2_taken"], 1)
            feed_units(FIRST["q"], 8)
            probs = buf[:, 5:7, :].rearrange("p a (b c) -> p (a b) c", c=T)
            p_t = conv[:, 0:4096].rearrange("p (m h t) -> p m h t", m=2, h=HEADS)
            for b in range(8):
                act.wait_ge(s["nmax"], b + 1)
                for e in range(2):
                    n = 2 * b + e
                    nc.scalar.activation(probs[:, b, e * MEM:(e + 1) * MEM], ps[:, b, e * MEM:(e + 1) * MEM], ACT.Exp,
                                         bias=negmax[:, n:n + 1], scale=1.0 / 16.0,
                                         accum_out=denom[:, n:n + 1]).then_inc(s["exp_done"], 1)
            for b in range(8):
                act.wait_ge(s["pt_mm"], b + 1)
                h, pair = b // 2, b % 2
                nc.scalar.activation(p_t[:, :, h, pair * MEM:(pair + 1) * MEM],
                                     ps[:, b, :].rearrange("p (m t) -> p m t", m=2), ACT.Copy).then_inc(s["pt_ready"], 1)
            for f in range(KT):
                act.wait_ge(s["attn_o"], f + 1)
                split_high(ahi[:, f, :], tiles(0, 2)[:, f, :], s["ao_hi"])
            feed_units(FIRST["wo"], 8)
            for k in range(KT):
                act.wait_ge(taken, 3 + TAKE["wo"] + k + 1)
                dst = bhi if k < 4 else ahi
                split_high(dst[:, k, :], stream[:, k, :], s["x2_hi"], col("norm_mlp", k))
            squares_of_stream(s["x2_sq"], s["x2_std"])
            act.wait_ge(s["x2_sum"], 1)
            nc.scalar.activation(sq[:, 1, :], ps[:, 7, :], ACT.Sqrt, bias=col("eps6"), scale=1.0 / D).then_inc(s["x2_std"], 1)
            w1 = FIRST["w1"]
            x2_tok = conv[:, 0:4096].rearrange("p (t d) -> p t d", t=NT)
            feed_units(w1, 12)
            for half in range(2):
                if half:
                    feed_units(w1 + 12, 12)
                for t in range(NT):
                    act.wait_ge(s["x2t_mm"], 4 * half + t + 1)
                    nc.scalar.activation(x2_tok[:, t, half * T:(half + 1) * T], ps[:, 3 + t, :],
                                         ACT.Copy).then_inc(s["x2t_ready"], 1)
            feed_units(w1 + 24, 8)
            w2 = FIRST["w2"]

            def h1_high(k, slot):
                act.wait_ge(s["h1_ready"], k + 1)
                nc.scalar.activation(ahi[:, slot, :], zflat[:, bass.ds(k * T, T)] if not isinstance(k, int) else z[:, k, :],
                                     ACT.Copy).then_inc(s["h1_hi"], 1)

            for k in range(RING):
                h1_high(k, (w2 + k) % RING)
            for k, slot, turn in units(act, w2, 27):
                act.wait_ge(unit_done, k + w2 + 1)
                high(slot, turn + 1)
                h1_high(k + RING, slot)
            for k in range(27, 29):
                slot = (w2 + k) % RING
                act.wait_ge(unit_done, w2 + k + 1)
                high(slot, (w2 + k) // RING + 1)
                h1_high(k + RING, slot)
            for t in range(NT):
                act.wait_ge(s["y_ready"], 2 * t + 2)
                nc.scalar.activation(stream[:, 2 * t:2 * t + 2, :], x2_tok[:, t, :].rearrange("p (a c) -> p a c", a=2),
                                     ACT.Square, accum_out=denom[:, t:t + 1]).then_inc(s["y_sq"], 1)
                act.wait_ge(s["y_sq"], t + 1)
                nc.scalar.activation(denom[:, 8 + t:9 + t], denom[:, t:t + 1], ACT.Sqrt, bias=col("eps6"),
                                     scale=1.0 / D).then_inc(s["y_std"], 1)

        @block.vector
        def _(dve):
            v = nc.vector
            steps = Steps(dve, dve_step)
            done = steps.done
            dve.sem_inc(taken, 3)
            dve.sem_inc(merged, 2)

            def split_low(dst, src, hi, tell, scale=None):
                if scale is None:
                    v.tensor_tensor(dst, src, hi.bitcast(F32), ALU.subtract).then_inc(tell, 1)
                else:
                    v.scalar_tensor_tensor(out=dst, in0=src, scalar=scale, in1=hi.bitcast(F32), op0=ALU.mult,
                                           op1=ALU.subtract).then_inc(tell, 1)

            def add_squares(src, ready, added, total):
                for k in range(KT):
                    dve.wait_ge(ready, k + 1)
                    if k == 0:
                        v.tensor_copy(sq[:, 0, :], src[:, 0, :]).then_inc(added, 1)
                    else:
                        dve.wait_ge(added, k)
                        v.tensor_tensor(sq[:, 0, :], sq[:, 0, :], src[:, k % 2, :], ALU.add).then_inc(
                            total if k == KT - 1 else added, 1)

            def take(name, fn):
                first = FIRST[name]
                for k, slot, _ in units(dve, first, dict(PHASES)[name]):
                    dve.wait_ge(unit_done, k + first + 1)
                    fn(k, slot).then_inc(taken, 1)

            dve.wait_ge(s["x_in"], 64)
            add_squares(tmp_a, s["sq_ready"], s["sq_added"], s["sum_ready"])
            dve.wait_ge(s["params_in"], 48)
            dve.wait_ge(s["std_ready"], 1)
            done(v.reciprocal(rstd[:, :], rstd[:, :]))
            for k in range(KT):
                v.scalar_tensor_tensor(out=xin[:, k, :], in0=xin[:, k, :], scalar=col("norm_mix", k), in1=rstd[:, :],
                                       op0=ALU.mult, op1=ALU.mult).then_inc(s["h_hi"], 1)
                if k >= 1:
                    dve.wait_ge(s["h_ready"], k)
                    split_low(alo[:, k - 1, :], xin[:, k - 1, :], ahi[:, k - 1, :], s["h_split"])
            dve.wait_ge(s["h_ready"], KT)
            split_low(alo[:, KT - 1, :], xin[:, KT - 1, :], ahi[:, KT - 1, :], s["h_split"])
            dve.wait_ge(s["bd_hi"], 1)
            split_low(bdlo[:, :], wbd[:, :], bdhi[:, :], s["bd_split"])
            dve.wait_ge(s["bd_ready"], 1)
            da = ps[:, 4, 0:32].rearrange("p (t e) -> p e t", e=8)[:, 4:8, :]
            v4 = lambda ap: ap.rearrange("p (h c) -> p h c", h=HEADS)
            done(v.tensor_tensor(v4(g_col), da, rows[:, 4:8].unsqueeze(2).to_broadcast([P, 4, 4]), ALU.add))
            v.scalar_tensor_tensor(out=s6, in0=g_col, scalar=-1.0, in1=g_col, op0=ALU.mult, op1=ALU.max).then_inc(s["bd_exp"], 1)
            done(v.tensor_scalar(g_col, g_col, 0.0, None, ALU.max))
            dve.wait_ge(s["bd_act"], 1)
            v.tensor_scalar(s5, s5, 1.0, None, ALU.add).then_inc(s["bd_exp"], 1)
            dve.wait_ge(s["bd_act"], 3)
            done(v.tensor_tensor(g_col, g_col, s6, ALU.add))
            v.scalar_tensor_tensor(out=v4(g_col), in0=v4(g_col), scalar=-1.0,
                                   in1=rows[:, 0:4].unsqueeze(2).to_broadcast([P, 4, 4]), op0=ALU.mult,
                                   op1=ALU.mult).then_inc(s["gb_ready"], 1)

            dve.wait_ge(z_free, 3 + 4)
            dve.wait_ge(s["early_in"], 48)
            src = z[:, 0:4, :]
            for lv, dst in enumerate((tmp_a, tmp_b, tmp_a, tmp_b)):
                sh = 1 << lv
                done(v.tensor_copy(dst[:, lv:4, 0:sh], src[:, lv:4, 0:sh]))
                done(v.tensor_tensor(dst[:, lv:4, sh:T], src[:, lv:4, sh:T], src[:, lv:4, 0:T - sh], ALU.add))
                src = dst
            first16 = small[:, 8:12, :]
            for g in range(4):
                sums = (tmp_a, tmp_b)[g % 2][:, g, :]
                done(v.tensor_tensor(first16[:, g, :], sums[:, 0:16], head_inv[:, g, :], ALU.mult))
                done(v.tensor_tensor(first16[:, g, :], first16[:, g, :], z[:, g, 0:16], ALU.subtract))
                done(v.scalar_tensor_tensor(out=z[:, g, :], in0=sums, scalar=1.0 / (2 << g), in1=z[:, g, :],
                                            op0=ALU.mult, op1=ALU.subtract))
                ins = v.tensor_copy(z[:, g, 0:16], first16[:, g, :])
                if g < 3:
                    done(ins)
                else:
                    ins.then_inc(s["pooled"], 1)
            done(v.tensor_tensor(ws.rearrange("p (g t) -> p g t", g=4), ws.rearrange("p (g t) -> p g t", g=4),
                                 tri.unsqueeze(1).to_broadcast([P, 4, P]), ALU.mult))

            def short_conv(dst, srcs, n, last_tell):
                for h in range(4):
                    w = lambda j: col("dn_w", (n * 4 + h) * 4 + j)
                    done(v.tensor_scalar(dst[:, h, :], srcs[:, h, :], w(3), None, ALU.mult))
                    for j in range(3):
                        sh = 3 - j
                        ins = v.scalar_tensor_tensor(out=dst[:, h, sh:T], in0=srcs[:, h, 0:T - sh], scalar=w(j),
                                                     in1=dst[:, h, sh:T], op0=ALU.mult, op1=ALU.add)
                        if last_tell is not None and h == 3 and j == 2:
                            ins.then_inc(last_tell, 1)
                        else:
                            done(ins)

            def layer_norm(ready, dst, var, std, tell=None):
                for t in range(NT):
                    dve.wait_ge(ready, t + 1)
                    done(v.bn_stats(stat[:, 0:6], ps[:, 4 + t, :]))
                    done(v.bn_aggr(mv[:, 2 * t:2 * t + 2], stat[:, 0:6]))
                v.tensor_copy(r_ln[:, 0:4], mv[:, 0:8].rearrange("p (t e) -> p t e", e=2)[:, :, 1]).then_inc(var, 1)
                dve.wait_ge(std, 1)
                done(v.reciprocal(r_ln[:, 0:4], r_ln[:, 0:4]))
                for t in range(NT):
                    ins = v.tensor_scalar(dst[:, t, :], ps[:, 4 + t, :], mv[:, 2 * t:2 * t + 1], r_ln[:, t:t + 1],
                                          ALU.subtract, ALU.mult)
                    if t == NT - 1 and tell is not None:
                        ins.then_inc(tell, 1)
                    else:
                        done(ins)

            dve.wait_ge(z_free, 3 + 16)
            short_conv(tmp_b, tiles(3), 0, None)
            for g in range(4):
                dve.wait_ge(s["p_hi"], g + 1)
                split_low(blo[:, g, :], z[:, g, :], bhi[:, g, :], s["p_split"])
            layer_norm(s["vt_ready"], tiles(2), s["vn_var"], s["vn_std"])
            b2 = tiles(2)
            done(v.tensor_tensor(b2, b2, gm_g.unsqueeze(1).to_broadcast([P, 4, T]), ALU.mult))
            v.tensor_tensor(b2, b2, gm_b.unsqueeze(1).to_broadcast([P, 4, T]), ALU.add).then_inc(s["vn_ready"], 1)
            dve.wait_ge(z_free, 3 + 24)
            short_conv(tiles(3), tiles(4), 1, None)
            short_conv(tiles(4), tiles(5), 2, None)
            for g in range(4):
                dve.wait_ge(s["mix_ready"], g + 1)
                bias = gm_bias[:, g * P:(g + 1) * P].unsqueeze(1).to_broadcast([P, 4, P])
                v.tensor_tensor(tmp_a[:, g, :].rearrange("p (n t) -> p n t", n=4),
                                ps[:, 4 + g, :].rearrange("p (n t) -> p n t", n=4), bias, ALU.add).then_inc(s["c_ready"], 1)
            dve.wait_ge(s["c_ready"], 4)
            for g in range(4):
                v.tensor_tensor(tiles(1)[:, g, :], tiles(1)[:, g, :], tmp_a[:, g, :], ALU.mult).then_inc(s["c_ready"], 1)
            v.tensor_copy(tiles(2), tmp_b).then_inc(s["conv_q"], 1)
            dve.wait_ge(s["conv_q"], 1)
            done(v.memset(a_pad[:, :, 0:PADC - 1], 0.0))
            dve.wait_ge(z_free, 3 + 32)
            v.memset(a_acc, 0.0).then_inc(s["conv_q"], 1)
            dve.wait_ge(s["sig2_ready"], 1)
            done(v.tensor_tensor(a_pad[:, :, PADC - 1:PADC - 1 + T], tiles(7), tiles(6), ALU.mult))
            dve.wait_ge(s["conv_q"], 2)
            for t in range(4):
                ins = v.tensor_scalar(a_acc[:, t, :], a_acc[:, t, :], col("conv_b", t), None, ALU.add)
                if t < 3:
                    done(ins)
                else:
                    ins.then_inc(s["conv_q"], 1)
            dve.wait_ge(s["conv_q"], 3)

            def merge(name, n, taps):
                first = FIRST[name]
                with dve.Fori(0, 4) as i:
                    per = 16 * taps + (0 if n == 0 else 2)
                    if per:
                        steps.enter(i, per)
                    for j in range(4 * taps):
                        for t in range(4):
                            tap = i * 4 + (16 * n + j)
                            ins = v.scalar_tensor_tensor(out=a_acc[:, t, :], in0=a_pad[:, t, bass.ds(tap, T)],
                                                         scalar=cols[:, bass.ds(tap + (COLS["conv_w"] + t * PADC), 1)],
                                                         in1=a_acc[:, t, :], op0=ALU.mult, op1=ALU.add)
                            done(ins)
                    dve.wait_ge(unit_done, i * 3 + first + 3)
                    dve.wait_ge(gate_free, i * 2 + 8 * n + 4)
                    for e in range(2):
                        dst = stream[:, :, :].rearrange("p a c -> p (a c)")[:, bass.ds(i * 2 * T + e * T, T)]
                        if n == 0:
                            v.tensor_tensor(dst, sig[:, e, :], ps[:, 2 + e, :], ALU.mult).then_inc(merged, 1)
                        else:
                            done(v.tensor_tensor(sq[:, e, :], sig[:, e, :], ps[:, 2 + e, :], ALU.mult))
                            v.tensor_tensor(dst, dst, sq[:, e, :], ALU.add).then_inc(merged, 1)
                    dve.wait_ge(merged, i * 2 + 8 * n + 4)
                if per:
                    steps.leave(4)

            merge("merge_p", 0, 1)
            for g in range(4):
                dve.wait_ge(s["c_hi"], g + 1)
                split_low(blo[:, g, :], tiles(1)[:, g, :], bhi[:, g, :], s["c_split"])
            bcol = lambda ap, h: ap[:, 4 * h:4 * h + 4].unsqueeze(2).to_broadcast([P, 4, P])
            b16 = lambda ap: ap.unsqueeze(2).to_broadcast([P, 16, P])
            m3 = lambda k: buf[:, k, :].rearrange("p (n t) -> p n t", n=16)
            dve.wait_ge(s["bd_act"], 4)
            for h in range(HEADS):
                dve.wait_ge(s["qkv_t"], 8 + h + 1)
                v.tensor_tensor(mats(7)[:, h], ps[:, 4 + h, :].rearrange("p (c t) -> p c t", c=4), bcol(beta, h),
                                ALU.mult).then_inc(s["v_tok"], 1)
            for n, r in enumerate((s7, s8)):
                dve.wait_ge(s["qk_sq"], n + 1)
                done(v.tensor_reduce(r, m3(2 + n), X, ALU.add))
                v.tensor_scalar(r, r, 1e-6, None, ALU.add).then_inc(s["qk_std"], 1)
            for n, r in enumerate((s7, s8)):
                dve.wait_ge(s["std_ready"], 2 + n)
                done(v.reciprocal(r, r))
                if n == 0:
                    done(v.tensor_scalar(r, r, float(P) ** -0.5, None, ALU.mult))
                v.tensor_tensor(m3(5 + n), m3(5 + n), b16(r), ALU.mult).then_inc(s["qk_norm"], 1)
            merge("merge_c", 1, 1)
            dve.wait_ge(s["gamrow"], 1)
            v.tensor_copy(gam, ps[:, 4, 0:16]).then_inc(s["gam_ready"], 1)
            dve.wait_ge(s["gam_ready"], 1)
            dve.wait_ge(s["qk_norm"], 2)
            dve.wait_ge(s["qk_back"], 4)
            for h in range(HEADS):
                dve.wait_ge(s["egr_ready"], h + 1)
                row = ps[:, 4 + h, :].rearrange("p (c t) -> p c t", c=4)
                done(v.tensor_copy(egl[:, 4 * h:4 * h + 4], row[:, :, P - 1]))
                done(v.tensor_tensor(mats(5)[:, h], row, bcol(gam, h), ALU.subtract))
                ins = v.tensor_scalar(mats(0)[:, h], mats(5)[:, h], 0.0, None, ALU.max)
                done(ins)
                v.tensor_scalar(mats(5)[:, h], mats(5)[:, h], 0.0, None, ALU.min).then_inc(s["dec_pre"], 1)
            dve.wait_ge(s["dec_pre"], 4)
            v.tensor_tensor(kd_s, egl, gam, ALU.subtract).then_inc(s["decay_ready"], 1)
            dve.sem_inc(s["dec_pre"], 4)
            dve.wait_ge(s["bd_act"], 7)
            done(v.tensor_tensor(kbe_s, kbe_s, beta, ALU.mult))
            dve.wait_ge(s["qk_feat"], 4)
            done(v.tensor_tensor(buf[:, 4, :], buf[:, 4, :], buf[:, 2, :], ALU.mult))
            for h in range(HEADS):
                dve.wait_ge(s["dec_exp"], h + 1)
                done(v.tensor_tensor(mats(0)[:, h], mats(0)[:, h], strict.unsqueeze(1).to_broadcast([P, 4, P]), ALU.mult))
                done(v.tensor_tensor(mats(0)[:, h], mats(0)[:, h], bcol(beta, h), ALU.mult))
                dve.wait_ge(s["a_mm"], h + 1)
                done(v.tensor_tensor(mats(0)[:, h], mats(0)[:, h], ps[:, h, :].rearrange("p (c t) -> p c t", c=4), ALU.mult))
                dve.wait_ge(s["attn_mm"], 4)
                done(v.tensor_tensor(mats(2)[:, h], mats(0)[:, h], level0.unsqueeze(1).to_broadcast([P, 4, P]), ALU.mult))
                v.tensor_tensor(mats(2)[:, h], ident.unsqueeze(1).to_broadcast([P, 4, P]), mats(2)[:, h],
                                ALU.subtract).then_inc(s["x0_ready"], 1)
            for h in range(HEADS):
                dve.wait_ge(s["dec_exp"], 4 + h + 1)
                done(v.tensor_tensor(mats(5)[:, h], mats(5)[:, h], tri.unsqueeze(1).to_broadcast([P, 4, P]), ALU.mult))
                v.tensor_tensor(mats(5)[:, h], mats(5)[:, h], ps[:, 4 + h, :].rearrange("p (c t) -> p c t", c=4),
                                ALU.mult).then_inc(s["gram_ready"], 1)
            for h in range(HEADS):
                dve.wait_ge(s["y0_mm"], h + 1)
                v.tensor_copy(tiles(3)[:, h, :], ps[:, h, :]).then_inc(s["lv_y"], 1)
            with dve.Fori(0, 6) as lv:
                mask = const[:, bass.ds(lv * P + CONST["levels"], P)].unsqueeze(1).to_broadcast([P, 4, P])
                for h in range(HEADS):
                    dve.wait_ge(s["lv_t"], lv * 4 + h + 1)
                    v.tensor_tensor(mats(1)[:, h], ps[:, 4 + h, :].rearrange("p (c t) -> p c t", c=4), mask,
                                    ALU.mult).then_inc(s["lv_masked"], 1)
                for h in range(HEADS):
                    dve.wait_ge(s["lv_p"], lv * 4 + h + 1)
                    v.tensor_tensor(tiles(3)[:, h, :], tiles(3)[:, h, :], ps[:, h, :], ALU.subtract).then_inc(s["lv_y"], 1)
            dve.wait_ge(s["lv_x"], 28)
            v.tensor_tensor(m3(2), m3(6), b16(kbe_s), ALU.mult).then_inc(s["kbe_ready"], 1)
            v.tensor_tensor(m3(6), m3(6), b16(kd_s), ALU.mult).then_inc(s["kbe_ready"], 1)
            egl_hc = egl.rearrange("p (h c) -> p h c", h=HEADS)
            for c in range(NT):
                old, new = state[:, (c + 1) % 2], state[:, c % 2]
                dve.wait_ge(s["v_mm"], c + 1)
                if c:
                    dve.wait_ge(s["o_mm"], c)
                v.tensor_copy(vnew[:, :, :], ps[:, 0, :].rearrange("p (h t) -> p h t", h=4)).then_inc(s["v_ready"], 1)
                if c < NT - 1:
                    if c:
                        done(v.tensor_tensor(new, old, egl_hc[:, :, c:c + 1].to_broadcast([P, 4, P]), ALU.mult))
                    dve.wait_ge(s["s_mm"], c + 1)
                    upd = ps[:, 1, :].rearrange("p (h t) -> p h t", h=4)
                    if c:
                        v.tensor_tensor(new, new, upd, ALU.add).then_inc(s["s_ready"], 1)
                    else:
                        v.tensor_copy(new, upd).then_inc(s["s_ready"], 1)
            dve.sem_inc(s["ca_ready"], 1)
            dve.wait_ge(s["o_sq"], 1)
            done(v.tensor_reduce(s5, m3(3), X, ALU.add))
            dve.sem_inc(s["o_sum"], 1)
            dve.wait_ge(s["o_std"], 1)
            done(v.reciprocal(s5, s5))
            v.tensor_tensor(m3(0), m3(0), b16(s5), ALU.mult).then_inc(s["o_norm"], 1)
            take("dgate", lambda k, slot: v.tensor_copy(tiles(4)[:, k, :] if isinstance(k, int)
                                                       else buf[:, 4, bass.ds(k * T, T)], ps[:, slot, :]))
            dve.wait_ge(s["dg_silu"], 1)
            for h in range(HEADS):
                dve.wait_ge(s["o_back"], h + 1)
                v.scalar_tensor_tensor(out=tiles(6)[:, h, :], in0=ps[:, h, :], scalar=col("dn_g"), in1=tiles(4)[:, h, :],
                                       op0=ALU.mult, op1=ALU.mult).then_inc(s["o_feat"], 1)
            for h in range(HEADS):
                dve.wait_ge(s["o_hi"], h + 1)
                split_low(blo[:, h, :], tiles(6)[:, h, :], bhi[:, h, :], s["o_split"])
            layer_norm(s["ca_t"], tiles(2), s["ca_var"], s["ca_std"], s["ca_norm"])
            merge("merge_o", 2, 0)
            for f in range(4):
                dve.wait_ge(s["a_hi"], f + 1)
                split_low(blo[:, f, :], tiles(3)[:, f, :], bhi[:, f, :], s["a_split"])
            merge("merge_a", 3, 0)
            for k in range(KT):
                dve.wait_ge(s["m_hi"], k + 1)
                split_low(alo[:, k, :], stream[:, k, :], ahi[:, k, :], s["m_split"])
            for k in range(KT):
                dve.wait_ge(s["m_hi2"], k + 1)
                split_low(blo[:, k // 2, (k % 2) * MEM:(k % 2 + 1) * MEM], buf[:, 4, k * MEM:(k + 1) * MEM],
                          bhi[:, k // 2, (k % 2) * MEM:(k % 2 + 1) * MEM], s["m_split2"], col("norm_mem", k))
            dve.wait_ge(s["mem_sq"], 1)
            v.tensor_reduce(sq[:, 0, 0:MEM], buf[:, 5, :].rearrange("p (k t) -> p t k", k=KT), X,
                            ALU.add).then_inc(s["mem_added"], 1)
            dve.wait_ge(s["x2_in"], 16)
            dve.wait_ge(s["m_split"], KT)

            def at(ap, k, n=T):
                flat = ap[:, :, :].rearrange("p a c -> p (a c)")
                return flat[:, k * n:(k + 1) * n] if isinstance(k, int) else flat[:, bass.ds(k * n, n)]

            take("out", lambda k, slot: v.tensor_tensor(at(stream, k), ps[:, slot, :], at(buf[:, 6:8, :], k), ALU.add))
            for k in range(KT):
                dve.wait_ge(s["x1_hi"], k + 1)
                split_low(alo[:, k, :], stream[:, k, :], ahi[:, k, :], s["x1_split"], col("norm_xa", k))
            dve.wait_ge(s["mem_std"], 1)
            v.reciprocal(rstd[:, 0:MEM], sq[:, 1, 0:MEM]).then_inc(s["mem_r"], 1)
            dve.wait_ge(s["mem_r"], 1)
            add_squares(tmp_b, s["x1_std"], s["x1_sq"], s["x1_added"])
            take("kv", lambda k, slot: v.tensor_tensor(at(buf[:, 2:4, :], k, MEM), ps[:, slot, 0:MEM], rstd[:, 0:MEM], ALU.mult))
            dve.wait_ge(taken, 3 + TAKE["q"])
            dve.wait_ge(s["x1_std"], KT + 1)
            v.reciprocal(rstd[:, :], sq[:, 1, :]).then_inc(s["x1_r"], 1)
            dve.wait_ge(s["x1_r"], 1)
            take("q", lambda k, slot: v.tensor_tensor(at(buf[:, 0:2, :], k), ps[:, slot, :], rstd[:, :], ALU.mult))
            probs = buf[:, 5:7, :].rearrange("p a (b c) -> p (a b) c", c=T)
            for b in range(8):
                dve.wait_ge(s["score_mm"], b + 1)
                done(v.reduce_max(negmax[:, 2 * b:2 * b + 2], ps[:, b, :].rearrange("p (e m) -> p e m", e=2), X))
                v.tensor_scalar(negmax[:, 2 * b:2 * b + 2], negmax[:, 2 * b:2 * b + 2], -1.0 / 16.0, None,
                                ALU.mult).then_inc(s["nmax"], 1)
            for b in range(8):
                dve.wait_ge(s["exp_done"], 2 * b + 2)
                done(v.reciprocal(denom[:, 2 * b:2 * b + 2], denom[:, 2 * b:2 * b + 2]))
                pb = probs[:, b, :].rearrange("p (e m) -> p e m", e=2)
                v.tensor_tensor(pb, pb, denom[:, 2 * b:2 * b + 2].unsqueeze(2).to_broadcast([P, 2, MEM]),
                                ALU.mult).then_inc(s["probs_ready"], 1)
            for f in range(KT):
                dve.wait_ge(s["pv_mm"], f + 1)
                v.tensor_copy(tiles(0, 2)[:, f, :], ps[:, f, :]).then_inc(s["attn_o"], 1)
            for f in range(KT):
                dve.wait_ge(s["ao_hi"], f + 1)
                split_low(alo[:, f, :], tiles(0, 2)[:, f, :], ahi[:, f, :], s["ao_split"])
            take("wo", lambda k, slot: v.tensor_tensor(at(stream, k), at(stream, k), ps[:, slot, :], ALU.add))
            for k in range(KT):
                dve.wait_ge(s["x2_hi"], k + 1)
                hi, lo = (bhi, blo) if k < 4 else (ahi, alo)
                split_low(lo[:, k, :], stream[:, k, :], hi[:, k, :], s["x2_split"], col("norm_mlp", k))
            add_squares(tmp_b, s["x2_std"], s["x2_sq"], s["x2_added"])
            dve.wait_ge(s["x2_std"], KT + 1)
            v.reciprocal(rstd[:, :], sq[:, 1, :]).then_inc(s["x2_r"], 1)
            dve.wait_ge(s["x2_r"], 1)
            w1 = FIRST["w1"]
            for k, slot, _ in units(dve, w1, 32):
                dve.wait_ge(unit_done, k + w1 + 1)
                v.tensor_tensor(sq[:, 0, :], ps[:, slot, :], rstd[:, :], ALU.mult).then_inc(taken, 1)
                dve.wait_ge(taken, k + 3 + TAKE["w1"] + 1)
                v.scalar_tensor_tensor(out=at(buf, k), in0=sq[:, 0, :], scalar=0.0, in1=sq[:, 0, :], op0=ALU.max,
                                       op1=ALU.mult).then_inc(s["h1_ready"], 1)
                dve.wait_ge(s["h1_ready"], k + 1)
            for k, slot, _ in units(dve, FIRST["w2"], 32):
                dve.wait_ge(s["h1_hi"], k + 1)
                split_low(alo[:, slot, :], at(buf, k), ahi[:, slot, :], s["h1_split"])
            x2_tok = conv[:, 0:4096].rearrange("p (t d) -> p t d", t=NT)
            gain = sig[:, :, :].rearrange("p a c -> p (a c)")
            dve.wait_ge(unit_done, NU)
            dve.wait_ge(s["f_in"], 16)
            for t in range(NT):
                for half in range(2):
                    part = x2_tok[:, t, half * T:(half + 1) * T]
                    v.tensor_tensor(part, part, ps[:, 2 * t + half, :], ALU.add).then_inc(s["y_ready"], 1)
            for t in range(NT):
                dve.wait_ge(s["y_std"], t + 1)
                done(v.reciprocal(denom[:, 8 + t:9 + t], denom[:, 8 + t:9 + t]))
                v.scalar_tensor_tensor(out=x2_tok[:, t, :], in0=x2_tok[:, t, :], scalar=denom[:, 8 + t:9 + t], in1=gain,
                                       op0=ALU.mult, op1=ALU.mult).then_inc(s["y_out"], 1)


def _blocks(w, first, n):
    k = w.shape[0] // P
    return w[:, first:first + n * P].reshape(k, P, n, P).transpose(2, 1, 0, 3).reshape(n, P, k * P)


def _stream(w_in, w_branch, w_out, wq, wkv, wo, w1, w2):
    conv_at, q_at = 0, 2 * MIX
    gm_at = q_at + 4 * MIX + 2 * HEADS
    pool_at = gm_at + 2 * MIX
    gate_at = pool_at + MIX
    parts = [_blocks(w_in, pool_at, 4), _blocks(w_in, gm_at, 8), _blocks(w_in, q_at, 12),
             _blocks(w_in, conv_at + MIX, 4), _blocks(w_in, conv_at, 4)]

    def merge(b):
        gates = _blocks(w_in, gate_at + b * D, KT)
        proj = w_branch[b].reshape(MT, P, KT // 2, 2, P).transpose(2, 1, 0, 3, 4).reshape(KT // 2, P, 1024)
        return np.stack([gates[0::2], gates[1::2], proj], 1).reshape(12, P, 1024)

    parts += [merge(3), merge(2), _blocks(w_in, q_at + 3 * MIX, 4), merge(1), merge(0)]
    parts += [_blocks(w_out, 0, 8), _blocks(wkv, 0, 16), _blocks(wq, 0, 8), _blocks(wo, 0, 8), _blocks(w1, 0, 32)]
    parts.append(w2.reshape(FFN // P, P, D))
    return np.concatenate(parts, 0)


def _cols(a):
    return a.reshape(-1, P).T


def _constants():
    i = np.arange(P)
    row, colm = i[:, None], i[None, :]
    level = lambda s: (row // (2 * s) == colm // (2 * s)) & (row % (2 * s) < s) & (colm % (2 * s) >= s)
    parts = [row == colm, row <= colm, row > colm, level(1).T] + [level(2 << n) for n in range(6)]
    parts.append(np.ones((P, P)))
    t = np.arange(16)
    head = np.stack([1.0 / np.minimum(t + 1, 2 << g) for g in range(4)]).reshape(1, 64)
    parts.append(np.broadcast_to(head, (P, 64)))
    return np.concatenate([p.astype(np.float32) for p in parts], 1)


def kernel(x, mem, norm_mix, w_in, conv_a_w, conv_a_b, ln_a_g, ln_a_b, dn_conv_w, dn_a_log, dn_dt_bias,
           dn_norm_g, gm_ln_g, gm_ln_b, gm_ws, gm_bs, pool_w, pool_scale, w_branch, w_out, norm_xa, norm_mem,
           xa_wq, xa_wkv, xa_wo, norm_mlp, mlp_w1, mlp_w2, norm_f):
    import concourse.bacc as bacc
    from concourse.bass_utils import run_bass_kernel_spmd as run

    f32 = np.float32
    ar = lambda a: np.asarray(a)
    bd_at = 2 * MIX + 4 * MIX
    conv_w = np.concatenate([np.zeros((1, MIX), f32), ar(conv_a_w)[0]], 0)
    arrays = {
        "wall": _stream(ar(w_in)[0], ar(w_branch)[0], ar(w_out)[0], ar(xa_wq)[0], ar(xa_wkv)[0], ar(xa_wo)[0],
                        ar(mlp_w1)[0], ar(mlp_w2)[0]),
        "x_t": ar(x)[0].T.reshape(KT, P, T).transpose(1, 0, 2),
        "mem_t": ar(mem)[0].T.reshape(KT, P, MEM).transpose(1, 0, 2).reshape(P, KT * MEM),
        "w_bd": ar(w_in)[0][:, bd_at:bd_at + 8].reshape(KT, P, 8).transpose(1, 0, 2).reshape(P, KT * 8),
        "cols_d": np.concatenate([
            _cols(ar(norm_mix)[0]), _cols(ar(norm_xa)[0]), _cols(ar(norm_mem)[0]), _cols(ar(norm_mlp)[0]),
            conv_w.reshape(PADC, 4, P).transpose(2, 1, 0).reshape(P, 4 * PADC), _cols(ar(conv_a_b)[0]),
            _cols(ar(ln_a_g)[0]), _cols(ar(ln_a_b)[0]),
            ar(dn_conv_w)[0].reshape(4, 12, P).transpose(2, 1, 0).reshape(P, 48),
            _cols(ar(dn_norm_g)[0]), _cols(ar(pool_scale)[0]), np.full((P, 1), 1e-6, f32), np.full((P, 1), 1e-5, f32)], 1),
        "rows_d": np.concatenate([ar(dn_a_log)[0], ar(dn_dt_bias)[0]]),
        "gains_d": np.concatenate([ar(gm_ln_g)[0], ar(gm_ln_b)[0], ar(gm_bs)[0].reshape(-1)]),
        "ws_t": ar(gm_ws)[0].transpose(2, 0, 1).reshape(P, 4 * P),
        "pool_w": ar(pool_w)[0].transpose(1, 0, 2).reshape(P, 4 * P),
        "const_d": _constants(),
        "norm_f": ar(norm_f),
    }
    arrays = {n: np.ascontiguousarray(a) for n, a in arrays.items()}
    nc = bacc.Bacc("TRN2", target_bir_lowering=False, num_devices=1)
    args = {n: nc.dram_tensor(n, a.shape, mybir.dt.from_np(a.dtype), kind="ExternalInput").ap() for n, a in arrays.items()}
    args["out"] = nc.dram_tensor("out", (1, T, D), F32, kind="ExternalOutput").ap()
    trunk(nc, **args)
    r = run(nc, [arrays], core_ids=[0])
    return r.results[0]["out"]
```

```python
from contextlib import ExitStack

import numpy as np

import concourse.bass as bass
from concourse import mybir

P = 128
D = 1024
T = 512
MEM = 256
KT = D // P
NT = T // P
MIX = D // 2
MT = MIX // P
HEADS = 4
CK = 31
PADC = 32
FFN = 4 * D
RING = 3

F32 = mybir.dt.float32
F32R = mybir.dt.float32r
ACT = mybir.ActivationFunctionType
ALU = mybir.AluOpType
X = mybir.AxisListType.X

PHASES = [("conv", 8), ("pool", 4), ("gm", 8), ("qkv", 12), ("merge_p", 12), ("merge_c", 12),
          ("dgate", 4), ("merge_o", 12), ("merge_a", 12), ("out", 8), ("kv", 16), ("q", 8),
          ("wo", 8), ("w1", 32), ("w2", 32)]
CONV_LATE = 20
FIRST = {}
NU = 0
for _name, _n in PHASES:
    FIRST[_name] = NU
    NU += _n

TAKE = {"dgate": 0, "out": 4, "kv": 12, "q": 28, "wo": 36, "w1": 44}

COLS = {}
_at = 0
for _name, _n in [("norm_mix", 8), ("norm_xa", 8), ("norm_mem", 8), ("norm_mlp", 8),
                  ("conv_w", 4 * PADC), ("conv_b", 4), ("ln_a_g", 4), ("ln_a_b", 4),
                  ("dn_w", 48), ("dn_g", 1), ("pool_s", 4), ("eps6", 1), ("eps5", 1)]:
    COLS[_name] = _at
    _at += _n
NCOLS = _at

CONST = {}
_at = 0
for _name, _n in [("ident", P), ("tri", P), ("strict", P), ("level0", P), ("levels", 6 * P // 2),
                  ("head", 64)]:
    CONST[_name] = _at
    _at += _n
NCONST = _at


def units(eng, first, count):
    n = count // RING
    if n > 1:
        with eng.Fori(0, n) as i:
            for j in range(RING):
                yield i * RING + j, (first + j) % RING, (first + j) // RING + i
    for k in range(n * RING if n > 1 else 0, count):
        yield k, (first + k) % RING, (first + k) // RING


def turns(eng, after, steps=None, per=0):
    at = 0
    while at < 4:
        end = min([k + 1 for k in after if k >= at] + [4])
        if end - at > 1:
            with eng.Fori(0, end - at) as i:
                if steps:
                    steps.enter(i, per)
                yield i + at
            if steps:
                steps.leave(end - at)
        else:
            yield at
        at = end
        if at - 1 in after:
            after[at - 1]()


class Steps:

    def __init__(self, eng, sem):
        self.eng, self.sem, self.before, self.here, self.turn = eng, sem, 0, 0, None

    def value(self):
        return self.before + self.here + (0 if self.turn is None else self.turn)

    def done(self, ins):
        ins.then_inc(self.sem, 1)
        self.here += 1
        self.eng.wait_ge(self.sem, self.value())

    def enter(self, i, per):
        self.before += self.here
        self.here, self.turn, self.per = 0, i * per, per

    def leave(self, n):
        assert self.here == self.per
        self.before += n * self.per
        self.here, self.turn = 0, None


def trunk(nc, wall, x_t, mem_t, w_bd, cols_d, rows_d, gains_d, ws_t, pool_w, const_d, norm_f, out):
    with ExitStack() as ctx:
        def sb(name, shape, dt=F32):
            return ctx.enter_context(nc.sbuf_tensor(name, shape, dt))

        def sem(name):
            return ctx.enter_context(nc.semaphore(name))

        raw = sb("raw", [P, RING, 1024])
        whi = sb("whi", [P, RING, 1024], F32R)
        wlo = sb("wlo", [P, RING, 1024], F32R)
        ahi = sb("ahi", [P, KT, T], F32R)
        alo = sb("alo", [P, KT, T], F32R)
        bhi = sb("bhi", [P, MT, T], F32R)
        blo = sb("blo", [P, MT, T], F32R)
        bdhi = sb("bdhi", [P, KT * 8], F32R)
        bdlo = sb("bdlo", [P, KT * 8], F32R)
        stream = sb("stream", [P, KT, T])
        buf = sb("buf", [P, 8, 2048])
        conv = sb("conv", [P, 4 * (T + PADC) + 4 * T])
        sig = sb("sig", [P, 2, T])
        sq = sb("sq", [P, 2, T])
        rstd = sb("rstd", [P, T])
        rmem = sb("rmem", [P, MEM])
        state = sb("state", [P, 2, HEADS, P])
        vnew = sb("vnew", [P, HEADS, P])
        cols = sb("cols", [P, NCOLS])
        const = sb("const", [P, NCONST])
        rows = sb("rows", [P, 8])
        wbd = sb("wbd", [P, KT * 8])
        small = sb("small", [P, 16, 16])
        ps = ctx.enter_context(nc.psum_tensor("ps", [P, 8, T], F32))

        def col(name, k=0):
            return cols[:, COLS[name] + k:COLS[name] + k + 1]

        ident, tri, strict, level0 = (const[:, CONST[n]:CONST[n] + P] for n in ("ident", "tri", "strict", "level0"))
        ones = sb("ones", [P, P])[:, :]
        head_inv = const[:, CONST["head"]:CONST["head"] + 64].rearrange("p (g t) -> p g t", g=4)

        def tiles(k, n=1):
            return buf[:, k:k + n, :].rearrange("p a (t c) -> p (a t) c", c=T)

        def mats(k):
            return buf[:, k, :].rearrange("p (h c t) -> p h c t", h=HEADS, c=NT)

        def at(ap, k, n=T):
            flat = ap[:, :, :].rearrange("p a c -> p (a c)")
            return flat[:, k * n:(k + 1) * n] if isinstance(k, int) else flat[:, bass.ds(k * n, n)]

        def right_half(ap, n):
            return ap.rearrange("p (b e c) -> p b e c", e=2, c=n)[:, :, 1, :]

        z = buf[:, :, :].rearrange("p a (t c) -> p (a t) c", c=T)
        zflat = buf[:, :, :].rearrange("p a c -> p (a c)")
        xin = tiles(6, 2)
        a_pad = conv[:, 0:4 * (T + PADC)].rearrange("p (t c) -> p t c", t=4)
        a_acc = conv[:, 4 * (T + PADC):].rearrange("p (t c) -> p t c", t=4)
        tmp_a, tmp_b = tiles(6), tiles(7)
        sq3 = conv[:, 0:3 * T].rearrange("p (s c) -> p s c", s=3)
        sq8 = conv[:, 0:KT * T].rearrange("p (s c) -> p s c", s=KT)
        kbe = (buf[:, 2, 1024:2048].rearrange("p (n t) -> p n t", n=8),
               state[:, :, :, :].rearrange("p a h t -> p (a h) t"))
        head_sq = (state[:, 0], state[:, 1], vnew[:, :, :], rstd[:, :].rearrange("p (c t) -> p c t", c=NT))
        early = stream[:, :, :].rearrange("p a c -> p (a c)")
        gm_g, gm_b, gm_bias = early[:, 0:512], early[:, 512:1024], early[:, 1024:1536]
        ws, pw = early[:, 1536:2048], early[:, 2048:2560]
        gains = early[:, 0:1536]

        beta, g_col, gam, egl = (small[:, n, :] for n in range(4))
        kbe_s, kd_s, s5, s6, s7, s8 = (small[:, n, :] for n in range(4, 10))
        stat = small[:, 10:12, :].rearrange("p a b -> p (a b)")
        mv = small[:, 12, :]
        r_ln = small[:, 13, :]
        negmax, denom = small[:, 14, :], small[:, 15, :]

        raw_in = [sem(f"raw_in{s}") for s in range(RING)]
        hi_ready, lo_ready = sem("hi_ready"), sem("lo_ready")
        unit_done = sem("unit_done")
        z_free = sem("z_free")
        taken = sem("taken")
        gate_free = sem("gate_free")
        merged = sem("merged")
        x_in = [sem(f"x_in{k}") for k in range(4)]
        dve_step = sem("dve_step")
        names = ("const_in params_in h_low_even h_low_odd ones_ready x_sum x_root y_mm x2_in mem_in "
                 "early_in f_in out_sent sq_act sq_dve std_ready bd_mm bd_t taps_done a_ready h_ready h_hi "
                 "bd_hi bd_split bd_ready bd_exp bd_act gelu_ready pooled pool_mm pool_scaled p_hi p_split "
                 "vt_ready vn_ready mix_ready c_ready c_hi c_split conv_q silu_ready qk_sum ln_var ln_std "
                 "sig2_ready qkv_t qkv_tok qk_sq qk_std qk_norm qk_back qk_feat gamrow gb_ready gam_ready "
                 "egr_ready dec_pre dec_exp attn_mm a_mm x0_ready y0_mm lv_t lv_masked lv_p lv_y lv_x "
                 "lv_xt v_tok o_sum kbe_ready wt_mm wt_ready v_mm v_ready s_mm s_ready o_mm o_tok o_sq "
                 "o_std o_norm o_back dg_silu o_feat o_hi o_split ca_ready ca_t ca_norm ca_back ca_silu "
                 "a_hi a_split m_hi m_split mem_sq mem_sum mem_std m_hi2 m_split2 x1_sq x1_sum x1_std "
                 "x1_hi x1_split vt2 vt2_taken score_mm nmax exp_done probs_ready pt_mm pt_ready pv_mm "
                 "ao_hi ao_split x2_sq x2_sum x2_std x2_hi x2_split x2t_mm x2t_ready h1_ready h1_hi "
                 "h1_split y_ready y_sq y_std y_out gram_ready decay_ready mem_added x1_added x2_added "
                 "mem_r x1_r x2_r").split()
        s = {n: sem(n) for n in names}

        block = ctx.enter_context(nc.Block())

        @block.sync
        def _(sp):
            for k in range(4):
                sp.dma_start(xin[:, 2 * k:2 * k + 2, :], x_t[:, 2 * k:2 * k + 2, :]).then_inc(x_in[k], 16)
            for u in range(RING):
                sp.dma_start(raw[:, u, :], wall[u]).then_inc(raw_in[u], 16)
            for k, slot, _ in units(sp, RING, NU - RING):
                sp.wait_ge(lo_ready, k + 1)
                sp.dma_start(raw[:, slot, :], wall[k + RING]).then_inc(raw_in[slot], 16)
            out_v = out[0].rearrange("(t p) d -> p t d", p=P)
            y_out = conv[:, 0:4096].rearrange("p (t d) -> p t d", t=NT)
            for t in range(NT):
                sp.wait_ge(s["y_out"], t + 1)
                sp.dma_start(out_v[:, t, :], y_out[:, t, :]).then_inc(s["out_sent"], 16)
            sp.wait_ge(s["out_sent"], 16 * NT)

        @block.gpsimd
        def _(pool):
            def low(k, slot):
                pool.wait_ge(hi_ready, k + 1)
                nc.gpsimd.tensor_tensor(wlo[:, slot, :], raw[:, slot, :], whi[:, slot, :].bitcast(F32),
                                        ALU.subtract).then_inc(lo_ready, 1)

            low(0, 0)
            for k in range(1, KT, 2):
                pool.wait_ge(s["h_ready"], k + 1)
                nc.gpsimd.tensor_tensor(alo[:, k, :], xin[:, k, :], ahi[:, k, :].bitcast(F32),
                                        ALU.subtract).then_inc(s["h_low_odd"], 1)
                if k == 3:
                    low(1, 1)
            low(2, 2)
            for k, slot, _ in units(pool, RING, NU - RING):
                low(k + RING, slot)

        @block.tensor
        def _(pe):
            def three(dst, st_hi, st_lo, mv_hi, mv_lo, first, last):
                nc.tensor.matmul(dst, st_hi, mv_hi, start=first, stop=False, skip_group_check=True)
                nc.tensor.matmul(dst, st_hi, mv_lo, start=False, stop=False, skip_group_check=True)
                return nc.tensor.matmul(dst, st_lo, mv_hi, start=False, stop=last, skip_group_check=True)

            def unit(slot, bank, ready, n=T, hi=ahi, lo=alo):
                fhi = hi[:, :, :].rearrange("p a c -> p (a c)")
                flo = lo[:, :, :].rearrange("p a c -> p (a c)")
                for k in range(KT):
                    if ready is None:
                        pe.wait_ge(s[("h_low_even", "h_low_odd")[k % 2]], k // 2 + 1)
                    else:
                        pe.wait_ge(ready, k + 1)
                    last = three(ps[:, bank, 0:n], whi[:, slot, k * P:(k + 1) * P], wlo[:, slot, k * P:(k + 1) * P],
                                 fhi[:, k * n:(k + 1) * n], flo[:, k * n:(k + 1) * n], k == 0, k == KT - 1)
                last.then_inc(unit_done, 1)

            def z_units(first, count):
                for k, slot, _ in units(pe, first, count):
                    pe.wait_ge(lo_ready, k + first + 1)
                    pe.wait_ge(z_free, k + first + 1)
                    unit(slot, slot, None)

            def taken_units(name, ready, count=None, skip=0, **how):
                first = FIRST[name] + skip
                for k, slot, _ in units(pe, first, count or dict(PHASES)[name]):
                    pe.wait_ge(lo_ready, k + first + 1)
                    pe.wait_ge(taken, k + TAKE[name] + skip + 1)
                    unit(slot, slot, ready, **how)

            def merge(name, n, ready, after={}):
                first = FIRST[name]
                for i in turns(pe, after):
                    for j in range(2):
                        slot = (first + j) % RING
                        pe.wait_ge(lo_ready, i * 3 + first + j + 1)
                        pe.wait_ge(gate_free, i * 2 + 8 * n + j + 1)
                        unit(slot, j, None)
                    slot = (first + 2) % RING
                    pe.wait_ge(lo_ready, i * 3 + first + 3)
                    pe.wait_ge(merged, i * 2 + 8 * n + 2)
                    pe.wait_ge(ready, MT)
                    for e in range(2):
                        for c in range(MT):
                            at = (c * 2 + e) * P
                            last = three(ps[:, 2 + e, :], whi[:, slot, at:at + P], wlo[:, slot, at:at + P],
                                         bhi[:, c, :], blo[:, c, :], c == 0, c == MT - 1)
                    last.then_inc(unit_done, 1)

            def mean_square(src, n, ready, tell):
                pe.wait_ge(ready, 1)
                nc.tensor.matmul(ps[:, 7, 0:n], ones, src, start=True, stop=True).then_inc(tell, 1)

            pe.wait_ge(s["ones_ready"], 1)
            for k in range(KT):
                pe.wait_ge(s[("sq_act", "sq_dve")[k % 2]], k // 2 + 1)
                last = nc.tensor.matmul(ps[:, 7, :], ones, sq8[:, k, :], start=k == 0, stop=k == KT - 1)
            last.then_inc(s["x_sum"], 1)
            z_units(0, 8)
            pe.wait_ge(s["bd_split"], 1)
            for k in range(KT):
                last = three(ps[0:8, 3, :], bdhi[:, k * 8:k * 8 + 8], bdlo[:, k * 8:k * 8 + 8], ahi[:, k, :], alo[:, k, :],
                             k == 0, k == KT - 1)
            last.then_inc(s["bd_mm"], 1)
            z_units(8, 4)
            pe.wait_ge(s["bd_t"], 1)
            pe.wait_ge(s["const_in"], 16)
            for t in range(NT):
                last = nc.tensor.transpose(ps[:, 4, t * 8:t * 8 + 8], rstd[0:8, t * P:(t + 1) * P], ident[0:8, 0:8])
            last.then_inc(s["bd_ready"], 1)
            z_units(12, 8)
            pe.wait_ge(s["pooled"], 1)
            pe.wait_ge(s["bd_act"], 4)
            pe.wait_ge(s["gb_ready"], 1)
            for g in range(4):
                nc.tensor.matmul(ps[:, 4 + g, :], pw[:, g * P:(g + 1) * P], z[:, g, :],
                                 start=True, stop=True).then_inc(s["pool_mm"], 1)
            z_units(20, 4)
            pe.wait_ge(s["gelu_ready"], 1)
            pe.wait_ge(s["pool_scaled"], 4)
            for t in range(NT):
                for f in range(4):
                    last = nc.tensor.transpose(ps[:, 4 + t, f * P:(f + 1) * P], tiles(2)[:, f, t * P:(t + 1) * P], ident)
                last.then_inc(s["vt_ready"], 1)
            z_units(24, 4)
            pe.wait_ge(s["vn_ready"], 1)
            nc.tensor.matmul(ps[:, 4, 0:16], tri, g_col, start=True, stop=True).then_inc(s["gamrow"], 1)
            z_units(28, 1)
            pe.wait_ge(s["gam_ready"], 1)
            for h in range(HEADS):
                for c in range(NT):
                    n = h * NT + c
                    last = nc.tensor.matmul(ps[:, 4 + h, c * P:(c + 1) * P], g_col[:, n:n + 1].to_broadcast([P, P]),
                                            tri, start=True, stop=True)
                last.then_inc(s["gamrow"], 1)
            z_units(29, 3)
            pe.wait_ge(s["dec_pre"], 4)
            vn = tiles(2)
            for g in range(4):
                for n in range(NT):
                    last = nc.tensor.matmul(ps[:, 4 + g, n * P:(n + 1) * P], vn[:, n, g * P:(g + 1) * P],
                                            ws[:, g * P:(g + 1) * P], start=True, stop=True)
                last.then_inc(s["mix_ready"], 1)
            pe.wait_ge(z_free, 3 + 32)

            def to_tokens(n, src, made, used):
                pe.wait_ge(s["silu_ready"], made)
                for h in range(HEADS):
                    pe.wait_ge(s[used[0]], used[1] + h + 1)
                    for c in range(NT):
                        last = nc.tensor.transpose(ps[:, 4 + h, c * P:(c + 1) * P],
                                                   tiles(src)[:, h, c * P:(c + 1) * P], ident)
                    last.then_inc(s["qkv_t"], 1)

            def to_features(n, src, used):
                pe.wait_ge(s["qk_norm"], n + 1)
                for h in range(HEADS):
                    pe.wait_ge(s[used], h + 1)
                    for c in range(NT):
                        last = nc.tensor.transpose(ps[:, 4 + h, c * P:(c + 1) * P], mats(src)[:, h, c, :], ident)
                    last.then_inc(s["qk_back"], 1)

            merge("merge_p", 0, s["p_split"], after={
                0: lambda: to_tokens(0, 7, 1, ("c_ready", 0)),
                1: lambda: to_tokens(1, 3, 2, ("qk_sq", 0)),
                2: lambda: to_tokens(2, 4, 3, ("qk_sq", 4)),
                3: lambda: to_features(0, 2, "v_tok")})

            qn, kn = mats(4), mats(1)

            def gram(other, used, tell):
                for h in range(HEADS):
                    pe.wait_ge(*used(h))
                    for c in range(NT):
                        last = nc.tensor.matmul(ps[:, 4 + h, c * P:(c + 1) * P], kn[:, h, c, :], other[:, h, c, :],
                                                start=True, stop=True)
                    last.then_inc(s[tell], 1)

            merge("merge_c", 1, s["c_split"], after={
                0: lambda: to_features(1, 7, "qk_feat"),
                1: lambda: gram(kn, lambda h: (s["qk_feat"], 5 + h), "a_mm"),
                2: lambda: gram(qn, lambda h: (s["a_ready"], h + 1), "attn_mm")})
            a_m, x_m, y_m = mats(0), mats(4), mats(1)
            t_m = buf[:, 2, 0:1024].rearrange("p (h c t) -> p h c t", h=HEADS, c=NT)
            pe.wait_ge(s["gram_ready"], 4)
            for h in range(HEADS):
                pe.wait_ge(s["x0_ready"], h + 1)
                for c in range(NT):
                    last = nc.tensor.transpose(ps[:, 4 + h, c * P:(c + 1) * P], x_m[:, h, c, :], ident)
                last.then_inc(s["y0_mm"], 1)
            for lv in range(6):
                n = 2 << lv
                for h in range(HEADS):
                    if lv:
                        pe.wait_ge(s["lv_y"], lv * 4 - 4 + h + 1)
                    pe.wait_ge(s["lv_x"], lv * 4 + h + 1)
                    for c in range(NT):
                        last = nc.tensor.matmul(ps[:, 4 + h, c * 64:(c + 1) * 64], a_m[:, h, c, :],
                                                right_half(y_m[:, h, c, :], n), start=True, stop=True)
                    last.then_inc(s["lv_t"], 1)
                if lv == 0:
                    pe.wait_ge(gate_free, 2 + 16)
                    pe.wait_ge(merged, 2 + 16)
                for h in range(HEADS):
                    pe.wait_ge(s["lv_masked"], lv * 4 + h + 1)
                    for c in range(NT):
                        last = nc.tensor.matmul(ps[:, h, c * 64:(c + 1) * 64], x_m[:, h, c, :], t_m[:, h, c, :],
                                                start=True, stop=True)
                    last.then_inc(s["lv_p"], 1)
                for h in range(HEADS if lv < 5 else 0):
                    pe.wait_ge(s["lv_y"], lv * 4 + h + 1)
                    for c in range(NT):
                        last = nc.tensor.transpose(ps[:, 4 + h, c * P:(c + 1) * P], y_m[:, h, c, :], ident)
                    last.then_inc(s["lv_xt"], 1)
            pe.wait_ge(s["kbe_ready"], 1)
            pe.wait_ge(s["lv_y"], 24)
            for h in range(HEADS):
                for c in range(NT):
                    last = nc.tensor.matmul(ps[:, 4 + h, c * P:(c + 1) * P], kbe[h // 2][:, (h % 2) * 4 + c, :], y_m[:, h, c, :],
                                            start=True, stop=True)
                last.then_inc(s["wt_mm"], 1)
            def gate_unit(k):
                pe.wait_ge(lo_ready, FIRST["dgate"] + k + 1)
                pe.wait_ge(s["wt_ready"], 4)
                unit((FIRST["dgate"] + k) % RING, 4 + k, None)

            wt, qd, at_m, kd, vb = mats(2), mats(6), mats(5), mats(7), mats(3)
            for c in range(NT):
                old, new = state[:, (c + 1) % 2], state[:, c % 2]
                if c == 1:
                    pe.wait_ge(s["wt_ready"], 4)
                if c:
                    pe.wait_ge(s["v_ready"], c)
                    pe.wait_ge(s["s_ready"], c)
                for h in range(HEADS):
                    last = nc.tensor.matmul(ps[:, 0, h * P:(h + 1) * P], y_m[:, h, c, :], vb[:, h, c, :],
                                            start=True, stop=c == 0)
                    if c:
                        last = nc.tensor.matmul(ps[:, 0, h * P:(h + 1) * P], wt[:, h, c, :], old[:, h, :],
                                                start=False, stop=True)
                last.then_inc(s["v_mm"], 1)
                if c in (1, 2):
                    gate_unit(c - 1)
                pe.wait_ge(s["v_ready"], c + 1)
                if c < NT - 1:
                    if c == 0:
                        pe.wait_ge(s["kbe_ready"], 2)
                    for h in range(HEADS):
                        last = nc.tensor.matmul(ps[:, 1, h * P:(h + 1) * P], kd[:, h, c, :], vnew[:, h, :],
                                                start=True, stop=True)
                    last.then_inc(s["s_mm"], 1)
                ob = 2 + c % 2
                if c >= 2:
                    pe.wait_ge(s["o_tok"], c - 1)
                for h in range(HEADS):
                    if c:
                        nc.tensor.matmul(ps[:, ob, h * P:(h + 1) * P], qd[:, h, c, :], old[:, h, :],
                                         start=True, stop=False)
                    last = nc.tensor.matmul(ps[:, ob, h * P:(h + 1) * P], at_m[:, h, c, :], vnew[:, h, :],
                                            start=c == 0, stop=True)
                last.then_inc(s["o_mm"], 1)
            for k in range(2, 4):
                gate_unit(k)
            o_tok = buf[:, 0, :].rearrange("p (c h v) -> p c h v", c=NT, h=HEADS)
            pe.wait_ge(s["o_norm"], 1)
            for h in range(HEADS):
                pe.wait_ge(taken, 3 + h + 1)
                for c in range(NT):
                    last = nc.tensor.transpose(ps[:, 4 + h, c * P:(c + 1) * P], o_tok[:, c, h, :], ident)
                last.then_inc(s["o_back"], 1)
            pe.wait_ge(s["o_tok"], NT)

            def conv_tokens():
                pe.wait_ge(s["ca_ready"], 1)
                pe.wait_ge(s["o_feat"], 4)
                for t in range(NT):
                    for f in range(4):
                        last = nc.tensor.transpose(ps[:, 4 + t, f * P:(f + 1) * P], a_acc[:, f, t * P:(t + 1) * P],
                                                   ident)
                    last.then_inc(s["ca_t"], 1)

            def conv_back():
                pe.wait_ge(s["ca_norm"], 1)
                for f in range(4):
                    for t in range(NT):
                        last = nc.tensor.transpose(ps[:, 4 + f, t * P:(t + 1) * P], tiles(2)[:, t, f * P:(f + 1) * P],
                                                   ident)
                    last.then_inc(s["ca_back"], 1)

            merge("merge_o", 2, s["o_split"], after={0: conv_tokens, 2: conv_back})
            merge("merge_a", 3, s["a_split"])
            pe.wait_ge(gate_free, 2 + 32)
            taken_units("out", s["m_split"])
            mean_square(rstd[:, 0:MEM], MEM, s["mem_added"], s["mem_sum"])
            taken_units("kv", s["m_split2"], n=MEM, hi=bhi, lo=blo)
            pe.wait_ge(s["mem_r"], 1)
            mean_square(sq[:, 0, :], T, s["x1_added"], s["x1_sum"])
            for m in range(2):
                for f in range(KT):
                    pe.wait_ge(taken, 3 + TAKE["kv"] + 8 + f + 1)
                    last = nc.tensor.transpose(ps[:, 3 + 2 * m + f // 4, (f % 4) * P:(f % 4 + 1) * P],
                                               buf[:, 3, f * MEM + m * P:f * MEM + (m + 1) * P], ident)
                last.then_inc(s["vt2"], 1)
            taken_units("q", s["x1_split"])
            q_t, k_t = tiles(0, 2), buf[:, 2, :]
            pe.wait_ge(taken, 3 + TAKE["q"] + 8)
            pe.wait_ge(s["vt2_taken"], 2)
            pe.wait_ge(s["x1_r"], 1)
            for h in range(HEADS):
                for pair in range(2):
                    for e in range(2):
                        t = 2 * pair + e
                        for d in range(2):
                            f = 2 * h + d
                            last = nc.tensor.matmul(ps[:, 2 * h + pair, e * MEM:(e + 1) * MEM],
                                                    q_t[:, f, t * P:(t + 1) * P], k_t[:, f * MEM:(f + 1) * MEM],
                                                    start=d == 0, stop=d == 1)
                    last.then_inc(s["score_mm"], 1)
            probs = buf[:, 5:7, :].rearrange("p a (b c) -> p (a b) c", c=T)
            for b in range(8):
                pe.wait_ge(s["probs_ready"], b + 1)
                for m in range(2):
                    for e in range(2):
                        last = nc.tensor.transpose(ps[:, b, (2 * m + e) * P:(2 * m + e + 1) * P],
                                                   probs[:, b, e * MEM + m * P:e * MEM + (m + 1) * P], ident)
                last.then_inc(s["pt_mm"], 1)
            v_tok = buf[:, 4, :].rearrange("p (m f) -> p m f", m=2)
            p_t = conv[:, 0:4096].rearrange("p (m h t) -> p m h t", m=2, h=HEADS)
            for f in range(KT):
                h = f // 2
                pe.wait_ge(s["pt_ready"], max(2 * h + 2, f + 1))
                for m in range(2):
                    last = nc.tensor.matmul(ps[:, f, :], v_tok[:, m, f * P:(f + 1) * P], p_t[:, m, h, :],
                                            start=m == 0, stop=m == 1)
                last.then_inc(s["pv_mm"], 1)
            pe.wait_ge(s["ao_split"], 3)
            taken_units("wo", s["ao_split"])

            def w1_unit(first, skip, count):
                for k, slot, _ in units(pe, first, count):
                    pe.wait_ge(lo_ready, k + first + 1)
                    pe.wait_ge(taken, k + TAKE["w1"] + skip + 1)
                    for kk in range(KT):
                        hi, lo = (bhi, blo) if kk < 4 else (ahi, alo)
                        pe.wait_ge(s["x2_split"], kk + 1)
                        last = three(ps[:, slot, :], whi[:, slot, kk * P:(kk + 1) * P], wlo[:, slot, kk * P:(kk + 1) * P],
                                     hi[:, kk, :], lo[:, kk, :], kk == 0, kk == KT - 1)
                    last.then_inc(unit_done, 1)

            w1 = FIRST["w1"]
            w1_unit(w1, 0, 1)
            mean_square(sq[:, 0, :], T, s["x2_added"], s["x2_sum"])
            w1_unit(w1 + 1, 1, 11)
            for half in range(2):
                if half:
                    w1_unit(w1 + 12, 12, 12)
                    pe.wait_ge(s["x2t_ready"], 4)
                for t in range(NT):
                    for f in range(4):
                        last = nc.tensor.transpose(ps[:, 3 + t, f * P:(f + 1) * P],
                                                   stream[:, 4 * half + f, t * P:(t + 1) * P], ident)
                    last.then_inc(s["x2t_mm"], 1)
            w1_unit(w1 + 24, 24, 8)
            pe.wait_ge(s["x2t_ready"], 8)
            pe.wait_ge(s["x2_r"], 1)

            def w2_product(slot, t, start, stop):
                for half in range(2):
                    last = three(ps[:, 2 * t + half, :], ahi[:, slot, t * P:(t + 1) * P],
                                 alo[:, slot, t * P:(t + 1) * P], whi[:, slot, half * T:(half + 1) * T],
                                 wlo[:, slot, half * T:(half + 1) * T], start, stop)
                return last

            def w2_unit(k, slot, start):
                pe.wait_ge(lo_ready, k + FIRST["w2"] + 1)
                pe.wait_ge(s["h1_split"], k + 1)
                for t in reversed(range(NT)):
                    if start and t == 1:
                        pe.wait_ge(taken, 3 + TAKE["w1"] + 32)
                    last = w2_product(slot, t, start, False)
                last.then_inc(unit_done, 1)

            w2 = FIRST["w2"]
            w2_unit(0, w2 % RING, True)
            for k, slot, _ in units(pe, w2 + 1, 28):
                w2_unit(k + 1, slot, False)
            pe.wait_ge(lo_ready, NU)
            pe.wait_ge(s["h1_split"], 32)
            for t in range(NT):
                for k in range(29, 32):
                    last = w2_product((w2 + k) % RING, t, False, k == 31)
                last.then_inc(s["y_mm"], 1)

        @block.scalar
        def _(act):
            act.sem_inc(z_free, 3)
            act.sem_inc(gate_free, 2)
            act.dma_start(cols[:, :], cols_d).then_inc(s["params_in"], 16)
            act.dma_start(rows[:, :], rows_d.partition_broadcast(P)).then_inc(s["params_in"], 16)
            act.dma_start(wbd[:, :], w_bd).then_inc(s["params_in"], 16)
            act.dma_start(const[:, :], const_d).then_inc(s["const_in"], 16)
            act.dma_start(gains, gains_d.partition_broadcast(P)).then_inc(s["early_in"], 16)
            act.dma_start(ws, ws_t).then_inc(s["early_in"], 16)
            act.dma_start(pw, pool_w).then_inc(s["early_in"], 16)

            def high(slot, turn):
                act.wait_ge(raw_in[slot], (turn + 1) * 16)
                nc.scalar.activation(whi[:, slot, :], raw[:, slot, :], ACT.Copy).then_inc(hi_ready, 1)

            def feed(first, k, slot, turn):
                act.wait_ge(unit_done, k + first + 1)
                high(slot, turn + 1)

            def feed_units(first, count):
                for k, slot, turn in units(act, first, count):
                    feed(first, k, slot, turn)

            def z_units(first, count, dst):
                for k, slot, turn in units(act, first, count):
                    act.wait_ge(unit_done, k + first + 1)
                    nc.scalar.activation(zflat[:, bass.ds((k + dst) * T, T)], ps[:, slot, :],
                                         ACT.Copy).then_inc(z_free, 1)
                    high(slot, turn + 1)

            def merge(name, n, after={}, inside=None):
                first = FIRST[name]
                for i in turns(act, after):
                    for j in range(RING):
                        if inside is not None and isinstance(i, int) and i == 3 and j == 2:
                            inside()
                        slot, turn = (first + j) % RING, i + (first + j) // RING
                        act.wait_ge(unit_done, i * 3 + first + j + 1)
                        if j < 2:
                            act.wait_ge(merged, i * 2 + 8 * n + 2)
                            nc.scalar.activation(sig[:, j, :], ps[:, j, :], ACT.Sigmoid).then_inc(gate_free, 1)
                        high(slot, turn + 1)

            def split_high(dst, src, tell, scale=1.0):
                nc.scalar.activation(dst, src, ACT.Copy, scale=scale).then_inc(tell, 1)

            for k in range(0, KT, 2):
                act.wait_ge(x_in[k // 2], 16)
                nc.scalar.activation(sq8[:, k, :], xin[:, k, :], ACT.Square).then_inc(s["sq_act"], 1)
            act.wait_ge(s["params_in"], 48)
            high(0, 0)
            act.wait_ge(s["x_sum"], 1)
            nc.scalar.activation(rstd[:, :], ps[:, 7, :], ACT.Sqrt, bias=col("eps6"), scale=1.0 / D).then_inc(s["x_root"], 1)
            high(1, 0)
            for k in range(KT):
                act.wait_ge(s["h_hi"], k + 1)
                split_high(ahi[:, k, :], xin[:, k, :], s["h_ready"])
            high(2, 0)
            nc.scalar.activation(bdhi[:, :], wbd[:, :], ACT.Copy).then_inc(s["bd_hi"], 1)
            z_units(0, 8, 24)
            act.wait_ge(z_free, 3 + 8)
            nc.scalar.activation(buf[:, 6, :], buf[:, 6, :], ACT.Sigmoid).then_inc(s["sig2_ready"], 1)
            act.wait_ge(s["bd_mm"], 1)
            nc.scalar.activation(rstd[0:8, :], ps[0:8, 3, :], ACT.Copy).then_inc(s["bd_t"], 1)
            z_units(8, 4, 0)
            act.wait_ge(s["bd_exp"], 1)
            nc.scalar.activation(s5, s6, ACT.Exp, scale=-1.0).then_inc(s["bd_act"], 1)
            nc.scalar.activation(rows[:, 0:4], rows[:, 0:4], ACT.Exp).then_inc(s["bd_act"], 1)
            act.wait_ge(s["bd_exp"], 2)
            nc.scalar.activation(s6, s5, ACT.Ln).then_inc(s["bd_act"], 1)
            act.wait_ge(s["bd_ready"], 1)
            nc.scalar.activation(beta, ps[:, 4, 0:32].rearrange("p (t e) -> p e t", e=8)[:, 0:4, :],
                                 ACT.Sigmoid).then_inc(s["bd_act"], 1)
            z_units(12, 8, 4)
            act.wait_ge(z_free, 3 + 20)
            for n in (1, 0):
                nc.scalar.activation(buf[:, 1 + n, :], buf[:, 1 + n, :], ACT.Gelu).then_inc(s["gelu_ready"], 1)
            act.wait_ge(s["pool_mm"], 4)
            for g in range(4):
                nc.scalar.activation(z[:, g, :], ps[:, 4 + g, :], ACT.Copy, scale=col("pool_s", g)).then_inc(s["pool_scaled"], 1)
            act.wait_ge(s["pool_scaled"], 4)
            for g in range(4):
                split_high(bhi[:, g, :], z[:, g, :], s["p_hi"])
            z_units(20, 4, 12)
            z_units(24, 1, 16)
            act.wait_ge(s["ln_var"], 1)
            nc.scalar.activation(r_ln[:, 0:4], r_ln[:, 0:4], ACT.Sqrt, bias=col("eps5")).then_inc(s["ln_std"], 1)
            z_units(25, 4, 17)
            for h in range(HEADS):
                act.wait_ge(s["gamrow"], h + 2)
                nc.scalar.activation(tiles(6)[:, h, :], ps[:, 4 + h, :], ACT.Exp).then_inc(s["egr_ready"], 1)
            z_units(29, 3, 21)
            def silu(n, at_):
                act.wait_ge(s["conv_q"], n + 1)
                nc.scalar.activation(buf[:, at_, :], buf[:, at_, :], ACT.Silu).then_inc(s["silu_ready"], 1)

            silu(0, 7)
            silu(1, 3)

            def to_tokens(n, dst):
                for h in range(HEADS):
                    act.wait_ge(s["qkv_t"], 4 * n + h + 1)
                    nc.scalar.activation(tiles(dst)[:, h, :], ps[:, 4 + h, :], ACT.Copy).then_inc(s["qkv_tok"], 1)
                    if n:
                        act.wait_ge(s["qk_sum"], h + 1)
                    nc.scalar.activation(head_sq[h].rearrange("p c t -> p (c t)"), ps[:, 4 + h, :],
                                         ACT.Square).then_inc(s["qk_sq"], 1)

            def root(n):
                act.wait_ge(s["qk_std"], n + 1)
                nc.scalar.activation((s7, s8)[n], (s7, s8)[n], ACT.Sqrt).then_inc(s["std_ready"], 1)

            def decays():
                act.wait_ge(s["decay_ready"], 1)
                nc.scalar.activation(kbe_s, gam, ACT.Exp).then_inc(s["bd_act"], 1)
                nc.scalar.activation(kd_s, kd_s, ACT.Exp).then_inc(s["bd_act"], 1)
                nc.scalar.activation(egl, egl, ACT.Exp).then_inc(s["bd_act"], 1)
                nc.scalar.activation(buf[:, 0, :], buf[:, 0, :], ACT.Exp, scale=-1.0).then_inc(s["dec_exp"], 1)
                nc.scalar.activation(buf[:, 5, :], buf[:, 5, :], ACT.Exp).then_inc(s["dec_exp"], 1)

            def to_features(n, dst):
                for h in range(HEADS):
                    act.wait_ge(s["qk_back"], 4 * n + h + 1)
                    nc.scalar.activation(tiles(dst)[:, h, :], ps[:, 4 + h, :], ACT.Copy).then_inc(s["qk_feat"], 1)

            merge("merge_p", 0, after={0: lambda: to_tokens(0, 2), 1: lambda: (root(0), to_tokens(1, 7), silu(2, 4)),
                                       2: lambda: (root(1), decays())})
            act.wait_ge(unit_done, FIRST["merge_c"])
            for g in range(4):
                split_high(bhi[:, g, :], tiles(1)[:, g, :], s["c_hi"])
            to_features(0, 4)
            act.wait_ge(s["c_split"], 4)
            merge("merge_c", 1, after={0: lambda: to_features(1, 1)})
            for h in range(HEADS):
                act.wait_ge(s["y0_mm"], h + 1)
                nc.scalar.activation(tiles(1)[:, h, :], ps[:, 4 + h, :], ACT.Copy).then_inc(s["lv_x"], 1)
            with act.Fori(0, 5) as lv:
                for h in range(HEADS):
                    act.wait_ge(s["lv_xt"], lv * 4 + h + 1)
                    nc.scalar.activation(tiles(4)[:, h, :], ps[:, 4 + h, :], ACT.Copy).then_inc(s["lv_x"], 1)
            for h in range(HEADS):
                act.wait_ge(s["wt_mm"], h + 1)
                nc.scalar.activation(tiles(2)[:, h, :], ps[:, 4 + h, :], ACT.Copy, scale=-1.0).then_inc(s["wt_ready"], 1)
            for c in range(NT):
                act.wait_ge(s["o_mm"], c + 1)
                nc.scalar.activation(tiles(0)[:, c, :], ps[:, 2 + c % 2, :], ACT.Copy).then_inc(s["o_tok"], 1)
                if c < 2:
                    slot_ = (FIRST["dgate"] + c) % RING
                    feed(FIRST["dgate"], c, slot_, (FIRST["dgate"] + c) // RING)
            act.wait_ge(s["o_tok"], NT)
            nc.scalar.activation(buf[:, 4, :], buf[:, 0, :], ACT.Square).then_inc(s["o_sq"], 1)
            act.wait_ge(s["o_sum"], 1)
            nc.scalar.activation(s5, s5, ACT.Sqrt, bias=col("eps6"), scale=1.0 / P).then_inc(s["o_std"], 1)
            feed_units(FIRST["dgate"] + 2, 2)
            for h in range(HEADS):
                act.wait_ge(taken, 3 + h + 1)
                nc.scalar.activation(tiles(6)[:, h, :], tiles(6)[:, h, :], ACT.Silu).then_inc(s["dg_silu"], 1)
            for h in range(HEADS):
                act.wait_ge(s["o_feat"], h + 1)
                split_high(bhi[:, h, :], tiles(1)[:, h, :], s["o_hi"])

            def conv_root():
                act.wait_ge(s["ln_var"], 2)
                nc.scalar.activation(r_ln[:, 0:4], r_ln[:, 0:4], ACT.Sqrt, bias=col("eps5")).then_inc(s["ln_std"], 1)

            def conv_back():
                for f in range(4):
                    act.wait_ge(s["ca_back"], f + 1)
                    nc.scalar.activation(tiles(3)[:, f, :], ps[:, 4 + f, :], ACT.Silu, bias=col("ln_a_b", f),
                                         scale=col("ln_a_g", f)).then_inc(s["ca_silu"], 1)

            merge("merge_o", 2, after={0: conv_root, 2: conv_back})
            act.wait_ge(s["ca_silu"], 4)
            act.wait_ge(unit_done, FIRST["merge_a"])
            for f in range(4):
                split_high(bhi[:, f, :], tiles(3)[:, f, :], s["a_hi"])
            act.wait_ge(s["o_feat"], 4)
            act.dma_start(xin, x_t).then_inc(s["x2_in"], 16)
            act.dma_start(buf[:, 4, :], mem_t).then_inc(s["mem_in"], 16)

            def mem_squares():
                act.wait_ge(s["mem_in"], 16)
                nc.scalar.activation(buf[:, 5, :], buf[:, 4, :], ACT.Square).then_inc(s["mem_sq"], 1)

            def merged_high():
                act.wait_ge(unit_done, FIRST["out"] - 1)
                for k in range(6):
                    act.wait_ge(merged, 2 + 24 + k + 1)
                    split_high(ahi[:, k, :], stream[:, k, :], s["m_hi"])

            merge("merge_a", 3, after={0: mem_squares, 2: lambda: None}, inside=merged_high)
            for k in range(6, KT):
                act.wait_ge(merged, 2 + 24 + k + 1)
                split_high(ahi[:, k, :], stream[:, k, :], s["m_hi"])
            act.dma_start(sig[:, :, :].rearrange("p a c -> p (a c)"), norm_f.partition_broadcast(P)).then_inc(s["f_in"], 16)
            act.wait_ge(unit_done, FIRST["out"])
            for k in range(KT):
                split_high(bhi[:, k // 2, (k % 2) * MEM:(k % 2 + 1) * MEM], buf[:, 4, k * MEM:(k + 1) * MEM],
                           s["m_hi2"], col("norm_mem", k))

            def residual_units(name, tell, late=None):
                first = FIRST[name]
                act.sem_inc(tell, 1)
                for k, slot, turn in units(act, first, 8):
                    if late is not None and isinstance(k, int) and k == 6:
                        late()
                    feed(first, k, slot, turn)
                    act.wait_ge(taken, k + 3 + TAKE[name] + 1)
                    nc.scalar.activation(sq3[:, slot, :], at(stream, k), ACT.Square).then_inc(tell, 1)

            residual_units("out", s["x1_sq"])
            act.wait_ge(s["mem_sum"], 1)
            nc.scalar.activation(rstd[:, 0:MEM], ps[:, 7, 0:MEM], ACT.Sqrt, bias=col("eps6"), scale=1.0 / D).then_inc(s["mem_std"], 1)
            for k, slot, turn in units(act, FIRST["kv"], 8):
                feed(FIRST["kv"], k, slot, turn)
                nc.scalar.activation(at(ahi, k), at(stream, k), ACT.Copy,
                                     scale=cols[:, bass.ds(k + COLS["norm_xa"], 1)]).then_inc(s["x1_hi"], 1)
            feed_units(FIRST["kv"] + 8, 8)
            act.wait_ge(s["x1_sum"], 1)
            nc.scalar.activation(sq[:, 1, :], ps[:, 7, :], ACT.Sqrt, bias=col("eps6"), scale=1.0 / D).then_inc(s["x1_std"], 1)
            for m in range(2):
                act.wait_ge(s["vt2"], m + 1)
                nc.scalar.activation(buf[:, 4, m * 1024:(m + 1) * 1024].rearrange("p (a c) -> p a c", a=2),
                                     ps[:, 3 + 2 * m:5 + 2 * m, :], ACT.Copy).then_inc(s["vt2_taken"], 1)
            feed_units(FIRST["q"], 8)
            probs = buf[:, 5:7, :].rearrange("p a (b c) -> p (a b) c", c=T)
            p_t = conv[:, 0:4096].rearrange("p (m h t) -> p m h t", m=2, h=HEADS)
            for b in range(8):
                act.wait_ge(s["nmax"], b + 1)
                for e in range(2):
                    n = 2 * b + e
                    nc.scalar.activation(probs[:, b, e * MEM:(e + 1) * MEM], ps[:, b, e * MEM:(e + 1) * MEM], ACT.Exp,
                                         bias=negmax[:, n:n + 1], scale=1.0 / 16.0,
                                         accum_out=denom[:, n:n + 1]).then_inc(s["exp_done"], 1)
            for b in range(8):
                act.wait_ge(s["pt_mm"], b + 1)
                h, pair = b // 2, b % 2
                nc.scalar.activation(p_t[:, :, h, pair * MEM:(pair + 1) * MEM],
                                     ps[:, b, :].rearrange("p (m t) -> p m t", m=2), ACT.Copy).then_inc(s["pt_ready"], 1)
            for f in range(KT):
                act.wait_ge(s["pv_mm"], f + 1)
                split_high(ahi[:, f, :], ps[:, f, :], s["ao_hi"])
            act.wait_ge(s["pv_mm"], 8)

            def x2_high(tiles_):
                for k in tiles_:
                    dst = bhi if k < 4 else ahi
                    split_high(dst[:, k, :], stream[:, k, :], s["x2_hi"], col("norm_mlp", k))

            residual_units("wo", s["x2_sq"], late=lambda: x2_high(range(4)))
            act.wait_ge(unit_done, FIRST["w1"])
            x2_high(range(4, KT))
            feed_units(FIRST["w1"], 1)
            act.wait_ge(s["x2_sum"], 1)
            nc.scalar.activation(sq[:, 1, :], ps[:, 7, :], ACT.Sqrt, bias=col("eps6"), scale=1.0 / D).then_inc(s["x2_std"], 1)
            w1 = FIRST["w1"]
            x2_tok = conv[:, 0:4096].rearrange("p (t d) -> p t d", t=NT)
            feed_units(w1 + 1, 11)
            for half in range(2):
                if half:
                    feed_units(w1 + 12, 12)
                for t in range(NT):
                    act.wait_ge(s["x2t_mm"], 4 * half + t + 1)
                    nc.scalar.activation(x2_tok[:, t, half * T:(half + 1) * T], ps[:, 3 + t, :],
                                         ACT.Copy).then_inc(s["x2t_ready"], 1)
            w2 = FIRST["w2"]

            def h1_high(k, slot):
                act.wait_ge(s["h1_ready"], k + 1)
                nc.scalar.activation(ahi[:, slot, :], zflat[:, bass.ds(k * T, T)] if not isinstance(k, int) else z[:, k, :],
                                     ACT.Copy).then_inc(s["h1_hi"], 1)

            for k in range(RING):
                h1_high(k, (w2 + k) % RING)
            feed_units(w1 + 24, 8)
            for k, slot, turn in units(act, w2, 27):
                act.wait_ge(unit_done, k + w2 + 1)
                high(slot, turn + 1)
                h1_high(k + RING, slot)
            for k in range(27, 29):
                slot = (w2 + k) % RING
                act.wait_ge(unit_done, w2 + k + 1)
                high(slot, (w2 + k) // RING + 1)
                h1_high(k + RING, slot)
            for t in range(NT):
                act.wait_ge(s["y_ready"], t + 1)
                nc.scalar.activation(stream[:, 2 * t:2 * t + 2, :], x2_tok[:, t, :].rearrange("p (a c) -> p a c", a=2),
                                     ACT.Square, accum_out=denom[:, t:t + 1]).then_inc(s["y_sq"], 1)
                act.wait_ge(s["y_sq"], t + 1)
                nc.scalar.activation(denom[:, 8 + t:9 + t], denom[:, t:t + 1], ACT.Sqrt, bias=col("eps6"),
                                     scale=1.0 / D).then_inc(s["y_std"], 1)

        @block.vector
        def _(dve):
            v = nc.vector
            steps = Steps(dve, dve_step)
            done = steps.done
            dve.sem_inc(taken, 3)
            dve.sem_inc(merged, 2)
            dve.sem_inc(s["taps_done"], 4)

            def split_low(dst, src, hi, tell, scale=None):
                if scale is None:
                    v.tensor_tensor(dst, src, hi.bitcast(F32), ALU.subtract).then_inc(tell, 1)
                else:
                    v.scalar_tensor_tensor(out=dst, in0=src, scalar=scale, in1=hi.bitcast(F32), op0=ALU.mult,
                                           op1=ALU.subtract).then_inc(tell, 1)

            def take(name, fn):
                first = FIRST[name]
                for k, slot, _ in units(dve, first, dict(PHASES)[name]):
                    dve.wait_ge(unit_done, k + first + 1)
                    fn(k, slot).then_inc(taken, 1)

            v.memset(ones, 1.0).then_inc(s["ones_ready"], 1)
            for k in range(1, KT, 2):
                dve.wait_ge(x_in[k // 2], 16)
                v.tensor_tensor(sq8[:, k, :], xin[:, k, :], xin[:, k, :], ALU.mult).then_inc(s["sq_dve"], 1)
            dve.wait_ge(s["params_in"], 48)
            dve.wait_ge(s["x_root"], 1)
            done(v.reciprocal(rstd[:, :], rstd[:, :]))

            def h_low(k):
                dve.wait_ge(s["h_ready"], k + 1)
                split_low(alo[:, k, :], xin[:, k, :], ahi[:, k, :], s["h_low_even"])

            for k in range(KT):
                v.scalar_tensor_tensor(out=xin[:, k, :], in0=xin[:, k, :], scalar=col("norm_mix", k), in1=rstd[:, :],
                                       op0=ALU.mult, op1=ALU.mult).then_inc(s["h_hi"], 1)
                if k and k % 2 == 0:
                    h_low(k - 2)
            h_low(6)
            dve.wait_ge(s["bd_hi"], 1)
            split_low(bdlo[:, :], wbd[:, :], bdhi[:, :], s["bd_split"])
            done(v.memset(conv[:, :], 0.0))
            for t in range(4):
                done(v.tensor_scalar(a_acc[:, t, :], a_acc[:, t, :], col("conv_b", t), None, ALU.add))
            dve.wait_ge(s["sig2_ready"], 1)
            done(v.tensor_tensor(a_pad[:, :, PADC - 1:PADC - 1 + T], tiles(7), tiles(6), ALU.mult))

            def conv_step(tap):
                for t in range(4):
                    dve.wait_ge(s["taps_done"], tap * 4 + t + 1)
                    v.scalar_tensor_tensor(out=a_acc[:, t, :], in0=a_pad[:, t, bass.ds(tap, T)],
                                           scalar=cols[:, bass.ds(tap + (COLS["conv_w"] + t * PADC), 1)],
                                           in1=a_acc[:, t, :], op0=ALU.mult, op1=ALU.add).then_inc(s["taps_done"], 1)

            def conv_taps(first, n):
                with dve.Fori(0, n) as i:
                    conv_step(i + first)

            conv_taps(0, 6)
            dve.wait_ge(s["bd_ready"], 1)
            da = ps[:, 4, 0:32].rearrange("p (t e) -> p e t", e=8)[:, 4:8, :]
            v4 = lambda ap: ap.rearrange("p (h c) -> p h c", h=HEADS)
            done(v.tensor_tensor(v4(g_col), da, rows[:, 4:8].unsqueeze(2).to_broadcast([P, 4, 4]), ALU.add))
            v.scalar_tensor_tensor(out=s6, in0=g_col, scalar=-1.0, in1=g_col, op0=ALU.mult, op1=ALU.max).then_inc(s["bd_exp"], 1)
            done(v.tensor_scalar(g_col, g_col, 0.0, None, ALU.max))
            dve.wait_ge(s["bd_act"], 1)
            v.tensor_scalar(s5, s5, 1.0, None, ALU.add).then_inc(s["bd_exp"], 1)
            dve.wait_ge(s["bd_act"], 3)
            done(v.tensor_tensor(g_col, g_col, s6, ALU.add))
            v.scalar_tensor_tensor(out=v4(g_col), in0=v4(g_col), scalar=-1.0,
                                   in1=rows[:, 0:4].unsqueeze(2).to_broadcast([P, 4, 4]), op0=ALU.mult,
                                   op1=ALU.mult).then_inc(s["gb_ready"], 1)

            dve.wait_ge(z_free, 3 + 12)
            dve.wait_ge(s["early_in"], 48)
            dve.wait_ge(s["const_in"], 16)
            src = z[:, 0:4, :]
            for lv, dst in enumerate((tmp_a, tmp_b, tmp_a, tmp_b)):
                sh = 1 << lv
                done(v.tensor_copy(dst[:, lv:4, 0:sh], src[:, lv:4, 0:sh]))
                done(v.tensor_tensor(dst[:, lv:4, sh:T], src[:, lv:4, sh:T], src[:, lv:4, 0:T - sh], ALU.add))
                src = dst
            first16 = small[:, 8:12, :]
            for g in range(4):
                sums = (tmp_a, tmp_b)[g % 2][:, g, :]
                done(v.tensor_tensor(first16[:, g, :], sums[:, 0:16], head_inv[:, g, :], ALU.mult))
                done(v.tensor_tensor(first16[:, g, :], first16[:, g, :], z[:, g, 0:16], ALU.subtract))
                done(v.scalar_tensor_tensor(out=z[:, g, :], in0=sums, scalar=1.0 / (2 << g), in1=z[:, g, :],
                                            op0=ALU.mult, op1=ALU.subtract))
                ins = v.tensor_copy(z[:, g, 0:16], first16[:, g, :])
                if g < 3:
                    done(ins)
                else:
                    ins.then_inc(s["pooled"], 1)
            done(v.tensor_tensor(ws.rearrange("p (g t) -> p g t", g=4), ws.rearrange("p (g t) -> p g t", g=4),
                                 tri.unsqueeze(1).to_broadcast([P, 4, P]), ALU.mult))

            conv_taps(6, CONV_LATE - 6)

            def short_conv(dst, srcs, n, last_tell):
                for h in range(4):
                    w = lambda j: col("dn_w", (n * 4 + h) * 4 + j)
                    done(v.tensor_scalar(dst[:, h, :], srcs[:, h, :], w(3), None, ALU.mult))
                    for j in range(3):
                        sh = 3 - j
                        ins = v.scalar_tensor_tensor(out=dst[:, h, sh:T], in0=srcs[:, h, 0:T - sh], scalar=w(j),
                                                     in1=dst[:, h, sh:T], op0=ALU.mult, op1=ALU.add)
                        if last_tell is not None and h == 3 and j == 2:
                            ins.then_inc(last_tell, 1)
                        else:
                            done(ins)

            def layer_norm(ready, dst, n, tell=None):
                for t in range(NT):
                    dve.wait_ge(ready, t + 1)
                    done(v.bn_stats(stat[:, 0:6], ps[:, 4 + t, :]))
                    done(v.bn_aggr(mv[:, 2 * t:2 * t + 2], stat[:, 0:6]))
                v.tensor_copy(r_ln[:, 0:4], mv[:, 0:8].rearrange("p (t e) -> p t e", e=2)[:, :, 1]).then_inc(s["ln_var"], 1)
                dve.wait_ge(s["ln_std"], n)
                done(v.reciprocal(r_ln[:, 0:4], r_ln[:, 0:4]))
                for t in range(NT):
                    ins = v.tensor_scalar(dst[:, t, :], ps[:, 4 + t, :], mv[:, 2 * t:2 * t + 1], r_ln[:, t:t + 1],
                                          ALU.subtract, ALU.mult)
                    if t == NT - 1 and tell is not None:
                        ins.then_inc(tell, 1)
                    else:
                        done(ins)

            for g in range(4):
                dve.wait_ge(s["p_hi"], g + 1)
                split_low(blo[:, g, :], z[:, g, :], bhi[:, g, :], s["p_split"])
            layer_norm(s["vt_ready"], tiles(2), 1)
            b2 = tiles(2)
            done(v.tensor_tensor(b2, b2, gm_g.unsqueeze(1).to_broadcast([P, 4, T]), ALU.mult))
            v.tensor_tensor(b2, b2, gm_b.unsqueeze(1).to_broadcast([P, 4, T]), ALU.add).then_inc(s["vn_ready"], 1)
            dve.wait_ge(z_free, 3 + 24)
            short_conv(tmp_b, tiles(3), 0, s["conv_q"])
            bcol = lambda ap, h: ap[:, 4 * h:4 * h + 4].unsqueeze(2).to_broadcast([P, 4, P])
            b16 = lambda ap: ap.unsqueeze(2).to_broadcast([P, 16, P])
            m3 = lambda k: buf[:, k, :].rearrange("p (n t) -> p n t", n=16)
            dve.wait_ge(s["gamrow"], 1)
            v.tensor_copy(gam, ps[:, 4, 0:16]).then_inc(s["gam_ready"], 1)
            dve.wait_ge(z_free, 3 + 28)
            short_conv(tiles(3), tiles(4), 1, s["conv_q"])
            dve.wait_ge(s["gam_ready"], 1)
            dve.wait_ge(s["bd_act"], 4)
            for h in range(HEADS):
                dve.wait_ge(s["egr_ready"], h + 1)
                row = ps[:, 4 + h, :].rearrange("p (c t) -> p c t", c=4)
                done(v.tensor_copy(egl[:, 4 * h:4 * h + 4], row[:, :, P - 1]))
                v.tensor_tensor(mats(0)[:, h], row, bcol(gam, h), ALU.subtract).then_inc(s["dec_pre"], 1)
            dve.wait_ge(s["gelu_ready"], 2)
            for g in range(4):
                dve.wait_ge(s["mix_ready"], g + 1)
                bias = gm_bias[:, g * P:(g + 1) * P].unsqueeze(1).to_broadcast([P, 4, P])
                v.tensor_tensor(sq[:, g % 2, :].rearrange("p (n t) -> p n t", n=4),
                                ps[:, 4 + g, :].rearrange("p (n t) -> p n t", n=4), bias, ALU.add).then_inc(s["c_ready"], 1)
                dve.wait_ge(s["c_ready"], g + 1)
                done(v.tensor_tensor(tiles(1)[:, g, :], tiles(1)[:, g, :], sq[:, g % 2, :], ALU.mult))
            dve.wait_ge(z_free, 3 + 32)
            short_conv(tiles(4), tiles(5), 2, s["conv_q"])
            dve.wait_ge(s["dec_pre"], 4)
            dve.wait_ge(s["conv_q"], 3)
            done(v.tensor_scalar(buf[:, 5, :], buf[:, 0, :], 0.0, None, ALU.min))
            done(v.tensor_scalar(buf[:, 0, :], buf[:, 0, :], 0.0, None, ALU.max))
            v.tensor_tensor(kd_s, egl, gam, ALU.subtract).then_inc(s["decay_ready"], 1)

            def merge(name, n, taps=0, after={}):
                first = FIRST[name]
                for i in turns(dve, after, steps, 0 if n == 0 else 2):
                    for j in range(taps):
                        conv_step(i * taps + CONV_LATE + 8 * n + j)
                    dve.wait_ge(unit_done, i * 3 + first + 3)
                    dve.wait_ge(gate_free, i * 2 + 8 * n + 4)
                    for e in range(2):
                        dst = stream[:, :, :].rearrange("p a c -> p (a c)")
                        at_ = i * 2 * T + e * T
                        dst = dst[:, at_:at_ + T] if isinstance(at_, int) else dst[:, bass.ds(at_, T)]
                        if n == 0:
                            v.tensor_tensor(dst, sig[:, e, :], ps[:, 2 + e, :], ALU.mult).then_inc(merged, 1)
                        else:
                            done(v.tensor_tensor(sq[:, e, :], sig[:, e, :], ps[:, 2 + e, :], ALU.mult))
                            v.tensor_tensor(dst, dst, sq[:, e, :], ALU.add).then_inc(merged, 1)
                    dve.wait_ge(merged, i * 2 + 8 * n + 4)

            def head_sums(n):
                r = (s7, s8)[n]
                for h in range(HEADS):
                    dve.wait_ge(s["qk_sq"], 4 * n + h + 1)
                    v.tensor_reduce(r[:, 4 * h:4 * h + 4], head_sq[h], X, ALU.add).then_inc(s["qk_sum"], 1)
                dve.wait_ge(s["qk_sum"], 4 * n + 4)
                v.tensor_scalar(r, r, 1e-6, None, ALU.add).then_inc(s["qk_std"], 1)

            def normalise(n, at_):
                r = (s7, s8)[n]
                dve.wait_ge(s["std_ready"], 1 + n)
                done(v.reciprocal(r, r))
                if n == 0:
                    done(v.tensor_scalar(r, r, float(P) ** -0.5, None, ALU.mult))
                dve.wait_ge(s["qkv_tok"], 4 * n + 4)
                v.tensor_tensor(m3(at_), m3(at_), b16(r), ALU.mult).then_inc(s["qk_norm"], 1)

            def v_tokens():
                for h in range(HEADS):
                    dve.wait_ge(s["qkv_t"], 8 + h + 1)
                    v.tensor_tensor(mats(3)[:, h], ps[:, 4 + h, :].rearrange("p (c t) -> p c t", c=4), bcol(beta, h),
                                    ALU.mult).then_inc(s["v_tok"], 1)

            def decay_masks():
                dve.wait_ge(s["dec_exp"], 2)
                done(v.tensor_tensor(m3(0), m3(0), strict.unsqueeze(1).to_broadcast([P, 16, P]), ALU.mult))
                done(v.tensor_tensor(m3(0), m3(0), b16(beta), ALU.mult))
                done(v.tensor_tensor(m3(5), m3(5), tri.unsqueeze(1).to_broadcast([P, 16, P]), ALU.mult))
                done(v.tensor_tensor(kbe_s, kbe_s, beta, ALU.mult))

            merge("merge_p", 0, 2, after={0: lambda: head_sums(0), 1: lambda: (normalise(0, 2), head_sums(1)),
                                          2: lambda: (v_tokens(), normalise(1, 7))})
            for g in range(4):
                dve.wait_ge(s["c_hi"], g + 1)
                split_low(blo[:, g, :], tiles(1)[:, g, :], bhi[:, g, :], s["c_split"])

            def lower():
                dve.wait_ge(s["qk_back"], 8)
                b8 = lambda e: kbe_s[:, 8 * e:8 * e + 8].unsqueeze(2).to_broadcast([P, 8, P])
                done(v.tensor_tensor(kbe[0], m3(7)[:, 0:8], b8(0), ALU.mult))
                v.tensor_tensor(kbe[1], m3(7)[:, 8:16], b8(1), ALU.mult).then_inc(s["kbe_ready"], 1)
                for h in range(HEADS):
                    dve.wait_ge(s["a_mm"], h + 1)
                    v.tensor_tensor(mats(0)[:, h], mats(0)[:, h], ps[:, 4 + h, :].rearrange("p (c t) -> p c t", c=4),
                                    ALU.mult).then_inc(s["a_ready"], 1)
                done(v.tensor_tensor(buf[:, 6, :], buf[:, 6, :], buf[:, 4, :], ALU.mult))
                dve.wait_ge(s["kbe_ready"], 1)
                v.tensor_tensor(m3(7), m3(7), b16(kd_s), ALU.mult).then_inc(s["kbe_ready"], 1)

            def first_inverse():
                for h in range(HEADS):
                    dve.wait_ge(s["attn_mm"], h + 1)
                    v.tensor_tensor(mats(5)[:, h], mats(5)[:, h], ps[:, 4 + h, :].rearrange("p (c t) -> p c t", c=4),
                                    ALU.mult).then_inc(s["gram_ready"], 1)
                dve.wait_ge(s["a_ready"], 4)
                for h in range(HEADS):
                    done(v.tensor_tensor(mats(4)[:, h], mats(0)[:, h], level0.unsqueeze(1).to_broadcast([P, 4, P]), ALU.mult))
                    v.tensor_tensor(mats(4)[:, h], ident.unsqueeze(1).to_broadcast([P, 4, P]), mats(4)[:, h],
                                    ALU.subtract).then_inc(s["x0_ready"], 1)

            merge("merge_c", 1, 1, after={0: decay_masks, 1: lower, 2: first_inverse})
            t_m = buf[:, 2, 0:1024].rearrange("p (h c t) -> p h c t", h=HEADS, c=NT)
            for lv in range(6):
                mask = const[:, CONST["levels"] + lv * 64:CONST["levels"] + (lv + 1) * 64].unsqueeze(1).to_broadcast([P, 4, 64])
                for h in range(HEADS):
                    dve.wait_ge(s["lv_t"], lv * 4 + h + 1)
                    v.tensor_tensor(t_m[:, h], ps[:, 4 + h, 0:256].rearrange("p (c t) -> p c t", c=4), mask,
                                    ALU.mult).then_inc(s["lv_masked"], 1)
                for h in range(HEADS):
                    dve.wait_ge(s["lv_p"], lv * 4 + h + 1)
                    half = right_half(tiles(1)[:, h, :], 2 << lv)
                    got = ps[:, h, 0:256].rearrange("p (b c) -> p b c", c=2 << lv)
                    v.tensor_tensor(half, half, got, ALU.subtract).then_inc(s["lv_y"], 1)
            egl_hc = egl.rearrange("p (h c) -> p h c", h=HEADS)
            for c in range(NT):
                old, new = state[:, (c + 1) % 2], state[:, c % 2]
                dve.wait_ge(s["v_mm"], c + 1)
                if c:
                    dve.wait_ge(s["o_mm"], c)
                v.tensor_copy(vnew[:, :, :], ps[:, 0, :].rearrange("p (h t) -> p h t", h=4)).then_inc(s["v_ready"], 1)
                if c < NT - 1:
                    if c:
                        done(v.tensor_tensor(new, old, egl_hc[:, :, c:c + 1].to_broadcast([P, 4, P]), ALU.mult))
                    dve.wait_ge(s["s_mm"], c + 1)
                    upd = ps[:, 1, :].rearrange("p (h t) -> p h t", h=4)
                    if c:
                        v.tensor_tensor(new, new, upd, ALU.add).then_inc(s["s_ready"], 1)
                    else:
                        v.tensor_copy(new, upd).then_inc(s["s_ready"], 1)
            dve.wait_ge(s["taps_done"], 4 + 4 * PADC)
            dve.sem_inc(s["ca_ready"], 1)
            dve.wait_ge(s["o_sq"], 1)
            done(v.tensor_reduce(s5, m3(4), X, ALU.add))
            dve.sem_inc(s["o_sum"], 1)
            dve.wait_ge(s["o_std"], 1)
            done(v.reciprocal(s5, s5))
            v.tensor_tensor(m3(0), m3(0), b16(s5), ALU.mult).then_inc(s["o_norm"], 1)
            for k in range(4):
                dve.wait_ge(unit_done, FIRST["dgate"] + k + 1)
                v.tensor_copy(tiles(6)[:, k, :], ps[:, 4 + k, :]).then_inc(taken, 1)
            for h in range(HEADS):
                dve.wait_ge(s["dg_silu"], h + 1)
                dve.wait_ge(s["o_back"], h + 1)
                v.scalar_tensor_tensor(out=tiles(1)[:, h, :], in0=ps[:, 4 + h, :], scalar=col("dn_g"), in1=tiles(6)[:, h, :],
                                       op0=ALU.mult, op1=ALU.mult).then_inc(s["o_feat"], 1)
            for h in range(HEADS):
                dve.wait_ge(s["o_hi"], h + 1)
                split_low(blo[:, h, :], tiles(1)[:, h, :], bhi[:, h, :], s["o_split"])
            merge("merge_o", 2, after={0: lambda: layer_norm(s["ca_t"], tiles(2), 2, s["ca_norm"])})
            for f in range(4):
                dve.wait_ge(s["a_hi"], f + 1)
                split_low(blo[:, f, :], tiles(3)[:, f, :], bhi[:, f, :], s["a_split"])

            def merged_low(tiles_):
                for k in tiles_:
                    dve.wait_ge(s["m_hi"], k + 1)
                    split_low(alo[:, k, :], stream[:, k, :], ahi[:, k, :], s["m_split"])

            def mem_sum():
                dve.wait_ge(s["mem_sq"], 1)
                v.tensor_reduce(rstd[:, 0:MEM], buf[:, 5, :].rearrange("p (k t) -> p t k", k=KT), X,
                                ALU.add).then_inc(s["mem_added"], 1)

            merge("merge_a", 3, after={1: mem_sum, 2: lambda: merged_low(range(6))})
            merged_low(range(6, KT))
            for k in range(KT):
                dve.wait_ge(s["m_hi2"], k + 1)
                split_low(blo[:, k // 2, (k % 2) * MEM:(k % 2 + 1) * MEM], buf[:, 4, k * MEM:(k + 1) * MEM],
                          bhi[:, k // 2, (k % 2) * MEM:(k % 2 + 1) * MEM], s["m_split2"], col("norm_mem", k))
            dve.wait_ge(s["x2_in"], 16)

            def residual(name, fn, squares, added, late=None):
                first = FIRST[name]
                done(v.memset(sq3, 0.0))
                done(v.memset(sq[:, 0, :], 0.0))
                with dve.Fori(0, 2) as i:
                    steps.enter(i, RING)
                    for j in range(RING):
                        residual_tile(first, i * RING + j, j, fn, squares, name)
                steps.leave(2)
                if late is not None:
                    late()
                for k in range(6, 8):
                    residual_tile(first, k, k, fn, squares, name)
                dve.wait_ge(squares, 9)
                v.tensor_tensor(sq[:, 0, :], sq[:, 0, :], sq3[:, (first + 7) % RING, :], ALU.add).then_inc(added, 1)

            def residual_tile(first, k, j, fn, squares, name):
                dve.wait_ge(unit_done, k + first + 1)
                fn(k, (first + j) % RING).then_inc(taken, 1)
                dve.wait_ge(squares, k + 1)
                done(v.tensor_tensor(sq[:, 0, :], sq[:, 0, :], sq3[:, (first + j - 1) % RING, :], ALU.add))

            residual("out", lambda k, slot: v.tensor_tensor(at(stream, k), ps[:, slot, :], at(buf[:, 6:8, :], k), ALU.add),
                     s["x1_sq"], s["x1_added"])
            dve.wait_ge(s["mem_std"], 1)
            v.reciprocal(rmem[:, :], rstd[:, 0:MEM]).then_inc(s["mem_r"], 1)
            dve.wait_ge(s["mem_r"], 1)
            first = FIRST["kv"]
            for k, slot, _ in units(dve, first, 16):
                dve.wait_ge(unit_done, k + first + 1)
                v.tensor_tensor(at(buf[:, 2:4, :], k, MEM), ps[:, slot, 0:MEM], rmem[:, :], ALU.mult).then_inc(taken, 1)
            for k in range(KT):
                dve.wait_ge(s["x1_hi"], k + 1)
                split_low(alo[:, k, :], stream[:, k, :], ahi[:, k, :], s["x1_split"], col("norm_xa", k))
            dve.wait_ge(taken, 3 + TAKE["q"])
            dve.wait_ge(s["x1_std"], 1)
            v.reciprocal(rstd[:, :], sq[:, 1, :]).then_inc(s["x1_r"], 1)
            dve.wait_ge(s["x1_r"], 1)
            take("q", lambda k, slot: v.tensor_tensor(at(buf[:, 0:2, :], k), ps[:, slot, :], rstd[:, :], ALU.mult))
            probs = buf[:, 5:7, :].rearrange("p a (b c) -> p (a b) c", c=T)
            for b in range(8):
                dve.wait_ge(s["score_mm"], b + 1)
                done(v.reduce_max(negmax[:, 2 * b:2 * b + 2], ps[:, b, :].rearrange("p (e m) -> p e m", e=2), X))
                v.tensor_scalar(negmax[:, 2 * b:2 * b + 2], negmax[:, 2 * b:2 * b + 2], -1.0 / 16.0, None,
                                ALU.mult).then_inc(s["nmax"], 1)
            for b in range(8):
                dve.wait_ge(s["exp_done"], 2 * b + 2)
                done(v.reciprocal(denom[:, 2 * b:2 * b + 2], denom[:, 2 * b:2 * b + 2]))
                pb = probs[:, b, :].rearrange("p (e m) -> p e m", e=2)
                v.tensor_tensor(pb, pb, denom[:, 2 * b:2 * b + 2].unsqueeze(2).to_broadcast([P, 2, MEM]),
                                ALU.mult).then_inc(s["probs_ready"], 1)
            for f in range(KT):
                dve.wait_ge(s["ao_hi"], f + 1)
                split_low(alo[:, f, :], ps[:, f, :], ahi[:, f, :], s["ao_split"])
            def x2_low(tiles_):
                for k in tiles_:
                    dve.wait_ge(s["x2_hi"], k + 1)
                    hi, lo = (bhi, blo) if k < 4 else (ahi, alo)
                    split_low(lo[:, k, :], stream[:, k, :], hi[:, k, :], s["x2_split"], col("norm_mlp", k))

            residual("wo", lambda k, slot: v.tensor_tensor(at(stream, k), at(stream, k), ps[:, slot, :], ALU.add),
                     s["x2_sq"], s["x2_added"], late=lambda: x2_low(range(4)))
            x2_low(range(4, KT))
            dve.wait_ge(s["x2_std"], 1)
            v.reciprocal(rstd[:, :], sq[:, 1, :]).then_inc(s["x2_r"], 1)
            dve.wait_ge(s["x2_r"], 1)
            w1 = FIRST["w1"]
            def hidden(skip, count):
                for k_, slot, _ in units(dve, w1 + skip, count):
                    k = k_ + skip
                    dve.wait_ge(unit_done, k + w1 + 1)
                    v.tensor_tensor(sq[:, 0, :], ps[:, slot, :], rstd[:, :], ALU.mult).then_inc(taken, 1)
                    dve.wait_ge(taken, k + 3 + TAKE["w1"] + 1)
                    v.scalar_tensor_tensor(out=at(buf, k), in0=sq[:, 0, :], scalar=0.0, in1=sq[:, 0, :], op0=ALU.max,
                                           op1=ALU.mult).then_inc(s["h1_ready"], 1)
                    dve.wait_ge(s["h1_ready"], k + 1)

            def hidden_low(skip, count):
                for k_, slot, _ in units(dve, FIRST["w2"] + skip, count):
                    dve.wait_ge(s["h1_hi"], k_ + skip + 1)
                    split_low(alo[:, slot, :], at(buf, k_ + skip), ahi[:, slot, :], s["h1_split"])

            hidden(0, 27)
            hidden_low(0, 3)
            hidden(27, 5)
            hidden_low(3, 29)
            x2_tok = conv[:, 0:4096].rearrange("p (t d) -> p t d", t=NT)
            gain = sig[:, :, :].rearrange("p a c -> p (a c)")
            dve.wait_ge(s["f_in"], 16)
            for t in range(NT):
                dve.wait_ge(s["y_mm"], t + 1)
                rows2 = x2_tok[:, t, :].rearrange("p (a c) -> p a c", a=2)
                v.tensor_tensor(rows2, rows2, ps[:, 2 * t:2 * t + 2, :], ALU.add).then_inc(s["y_ready"], 1)
                dve.wait_ge(s["y_std"], t + 1)
                done(v.reciprocal(denom[:, 8 + t:9 + t], denom[:, 8 + t:9 + t]))
                v.scalar_tensor_tensor(out=x2_tok[:, t, :], in0=x2_tok[:, t, :], scalar=denom[:, 8 + t:9 + t], in1=gain,
                                       op0=ALU.mult, op1=ALU.mult).then_inc(s["y_out"], 1)


def _blocks(w, first, n):
    k = w.shape[0] // P
    return w[:, first:first + n * P].reshape(k, P, n, P).transpose(2, 1, 0, 3).reshape(n, P, k * P)


def _stream(w_in, w_branch, w_out, wq, wkv, wo, w1, w2):
    conv_at, q_at = 0, 2 * MIX
    gm_at = q_at + 4 * MIX + 2 * HEADS
    pool_at = gm_at + 2 * MIX
    gate_at = pool_at + MIX
    parts = [_blocks(w_in, conv_at + MIX, 4), _blocks(w_in, conv_at, 4), _blocks(w_in, pool_at, 4),
             _blocks(w_in, gm_at, 8), _blocks(w_in, q_at, 12)]

    def merge(b):
        gates = _blocks(w_in, gate_at + b * D, KT)
        proj = w_branch[b].reshape(MT, P, KT // 2, 2, P).transpose(2, 1, 0, 3, 4).reshape(KT // 2, P, 1024)
        return np.stack([gates[0::2], gates[1::2], proj], 1).reshape(12, P, 1024)

    parts += [merge(3), merge(2), _blocks(w_in, q_at + 3 * MIX, 4), merge(1), merge(0)]
    parts += [_blocks(w_out, 0, 8), _blocks(wkv, 0, 16), _blocks(wq, 0, 8), _blocks(wo, 0, 8), _blocks(w1, 0, 32)]
    parts.append(w2.reshape(FFN // P, P, D))
    return np.concatenate(parts, 0)


def _cols(a):
    return a.reshape(-1, P).T


def _constants():
    i = np.arange(P)
    row, colm = i[:, None], i[None, :]
    level = lambda s: (row // (2 * s) == colm // (2 * s)) & (row % (2 * s) < s) & (colm % (2 * s) >= s)
    parts = [row == colm, row <= colm, row > colm, level(1).T]
    parts += [level(2 << n).reshape(P, -1, 2, 2 << n)[:, :, 1].reshape(P, 64) for n in range(6)]
    t = np.arange(16)
    head = np.stack([1.0 / np.minimum(t + 1, 2 << g) for g in range(4)]).reshape(1, 64)
    parts.append(np.broadcast_to(head, (P, 64)))
    return np.concatenate([p.astype(np.float32) for p in parts], 1)


def kernel(x, mem, norm_mix, w_in, conv_a_w, conv_a_b, ln_a_g, ln_a_b, dn_conv_w, dn_a_log, dn_dt_bias,
           dn_norm_g, gm_ln_g, gm_ln_b, gm_ws, gm_bs, pool_w, pool_scale, w_branch, w_out, norm_xa, norm_mem,
           xa_wq, xa_wkv, xa_wo, norm_mlp, mlp_w1, mlp_w2, norm_f):
    import concourse.bacc as bacc
    from concourse.bass_utils import run_bass_kernel_spmd as run

    f32 = np.float32
    ar = lambda a: np.asarray(a)
    bd_at = 2 * MIX + 4 * MIX
    conv_w = np.concatenate([np.zeros((1, MIX), f32), ar(conv_a_w)[0]], 0)
    arrays = {
        "wall": _stream(ar(w_in)[0], ar(w_branch)[0], ar(w_out)[0], ar(xa_wq)[0], ar(xa_wkv)[0], ar(xa_wo)[0],
                        ar(mlp_w1)[0], ar(mlp_w2)[0]),
        "x_t": ar(x)[0].T.reshape(KT, P, T).transpose(1, 0, 2),
        "mem_t": ar(mem)[0].T.reshape(KT, P, MEM).transpose(1, 0, 2).reshape(P, KT * MEM),
        "w_bd": ar(w_in)[0][:, bd_at:bd_at + 8].reshape(KT, P, 8).transpose(1, 0, 2).reshape(P, KT * 8),
        "cols_d": np.concatenate([
            _cols(ar(norm_mix)[0]), _cols(ar(norm_xa)[0]), _cols(ar(norm_mem)[0]), _cols(ar(norm_mlp)[0]),
            conv_w.reshape(PADC, 4, P).transpose(2, 1, 0).reshape(P, 4 * PADC), _cols(ar(conv_a_b)[0]),
            _cols(ar(ln_a_g)[0]), _cols(ar(ln_a_b)[0]),
            ar(dn_conv_w)[0].reshape(4, 12, P).transpose(2, 1, 0).reshape(P, 48),
            _cols(ar(dn_norm_g)[0]), _cols(ar(pool_scale)[0]), np.full((P, 1), 1e-6, f32), np.full((P, 1), 1e-5, f32)], 1),
        "rows_d": np.concatenate([ar(dn_a_log)[0], ar(dn_dt_bias)[0]]),
        "gains_d": np.concatenate([ar(gm_ln_g)[0], ar(gm_ln_b)[0], ar(gm_bs)[0].reshape(-1)]),
        "ws_t": ar(gm_ws)[0].transpose(2, 0, 1).reshape(P, 4 * P),
        "pool_w": ar(pool_w)[0].transpose(1, 0, 2).reshape(P, 4 * P),
        "const_d": _constants(),
        "norm_f": ar(norm_f),
    }
    arrays = {n: np.ascontiguousarray(a) for n, a in arrays.items()}
    nc = bacc.Bacc("TRN2", target_bir_lowering=False, num_devices=1)
    args = {n: nc.dram_tensor(n, a.shape, mybir.dt.from_np(a.dtype), kind="ExternalInput").ap() for n, a in arrays.items()}
    args["out"] = nc.dram_tensor("out", (1, T, D), F32, kind="ExternalOutput").ap()
    trunk(nc, **args)
    r = run(nc, [arrays], core_ids=[0])
    return r.results[0]["out"]
```

```python
from contextlib import ExitStack

import numpy as np

import concourse.bass as bass
from concourse import mybir

P = 128
D = 1024
T = 512
MEM = 256
KT = D // P
NT = T // P
MIX = D // 2
MT = MIX // P
HEADS = 4
CK = 31
PADC = 32
FFN = 4 * D
RING = 3

F32 = mybir.dt.float32
F32R = mybir.dt.float32r
ACT = mybir.ActivationFunctionType
ALU = mybir.AluOpType
X = mybir.AxisListType.X

PHASES = [("conv", 8), ("pool", 4), ("gm", 8), ("qkv", 12), ("merge_p", 12), ("merge_c", 12),
          ("dgate", 4), ("merge_o", 12), ("merge_a", 12), ("out", 8), ("kv", 16), ("q", 8),
          ("wo", 8), ("w1", 32), ("w2", 32)]
CONV_LATE = 20
FIRST = {}
NU = 0
for _name, _n in PHASES:
    FIRST[_name] = NU
    NU += _n

TAKE = {"conv": 0, "dgate": 8, "out": 12, "kv": 20, "q": 36, "wo": 44, "w1": 52}

COLS = {}
_at = 0
for _name, _n in [("norm_mix", 8), ("norm_xa", 8), ("norm_mem", 8), ("norm_mlp", 8),
                  ("conv_w", 4 * PADC), ("conv_b", 4), ("ln_a_g", 4), ("ln_a_b", 4),
                  ("dn_w", 48), ("dn_g", 1), ("pool_s", 4), ("eps6", 1), ("eps5", 1)]:
    COLS[_name] = _at
    _at += _n
NCOLS = _at

CONST = {}
_at = 0
for _name, _n in [("ident", P), ("tri", P), ("strict", P), ("level0", P), ("levels", 6 * P // 2),
                  ("head", 64)]:
    CONST[_name] = _at
    _at += _n
NCONST = _at


def units(eng, first, count):
    n = count // RING
    if n > 1:
        with eng.Fori(0, n) as i:
            for j in range(RING):
                yield i * RING + j, (first + j) % RING, (first + j) // RING + i
    for k in range(n * RING if n > 1 else 0, count):
        yield k, (first + k) % RING, (first + k) // RING


def turns(eng, after, steps=None, per=0):
    at = 0
    while at < 4:
        end = min([k + 1 for k in after if k >= at] + [4])
        if end - at > 1:
            with eng.Fori(0, end - at) as i:
                if steps:
                    steps.enter(i, per)
                yield i + at
            if steps:
                steps.leave(end - at)
        else:
            yield at
        at = end
        if at - 1 in after:
            after[at - 1]()


class Steps:

    def __init__(self, eng, sem):
        self.eng, self.sem, self.before, self.here, self.turn = eng, sem, 0, 0, None

    def value(self):
        return self.before + self.here + (0 if self.turn is None else self.turn)

    def done(self, ins):
        ins.then_inc(self.sem, 1)
        self.here += 1
        self.eng.wait_ge(self.sem, self.value())

    def enter(self, i, per):
        self.before += self.here
        self.here, self.turn, self.per = 0, i * per, per

    def leave(self, n):
        assert self.here == self.per
        self.before += n * self.per
        self.here, self.turn = 0, None


def trunk(nc, wall, x_t, mem_t, w_bd, cols_d, rows_d, gains_d, ws_t, pool_w, const_d, norm_f, out):
    with ExitStack() as ctx:
        def sb(name, shape, dt=F32):
            return ctx.enter_context(nc.sbuf_tensor(name, shape, dt))

        def sem(name):
            return ctx.enter_context(nc.semaphore(name))

        raw = sb("raw", [P, RING, 1024])
        whi = sb("whi", [P, RING, 1024], F32R)
        wlo = sb("wlo", [P, RING, 1024], F32R)
        ahi = sb("ahi", [P, KT, T], F32R)
        alo = sb("alo", [P, KT, T], F32R)
        bhi = sb("bhi", [P, MT, T], F32R)
        blo = sb("blo", [P, MT, T], F32R)
        bdhi = sb("bdhi", [P, KT * 8], F32R)
        bdlo = sb("bdlo", [P, KT * 8], F32R)
        stream = sb("stream", [P, KT, T])
        buf = sb("buf", [P, 8, 2048])
        conv = sb("conv", [P, 4 * (T + PADC) + 4 * T])
        sig = sb("sig", [P, 2, T])
        sq = sb("sq", [P, 2, T])
        rstd = sb("rstd", [P, T])
        rmem = sb("rmem", [P, MEM])
        state = sb("state", [P, 2, HEADS, P])
        vnew = sb("vnew", [P, HEADS, P])
        cols = sb("cols", [P, NCOLS])
        const = sb("const", [P, NCONST])
        rows = sb("rows", [P, 8])
        wbd = sb("wbd", [P, KT * 8])
        small = sb("small", [P, 16, 16])
        ps = ctx.enter_context(nc.psum_tensor("ps", [P, 8, T], F32))

        def col(name, k=0):
            return cols[:, COLS[name] + k:COLS[name] + k + 1]

        ident, tri, strict, level0 = (const[:, CONST[n]:CONST[n] + P] for n in ("ident", "tri", "strict", "level0"))
        ones = sb("ones", [P, P])[:, :]
        head_inv = const[:, CONST["head"]:CONST["head"] + 64].rearrange("p (g t) -> p g t", g=4)

        def tiles(k, n=1):
            return buf[:, k:k + n, :].rearrange("p a (t c) -> p (a t) c", c=T)

        def mats(k):
            return buf[:, k, :].rearrange("p (h c t) -> p h c t", h=HEADS, c=NT)

        def at(ap, k, n=T):
            flat = ap[:, :, :].rearrange("p a c -> p (a c)")
            return flat[:, k * n:(k + 1) * n] if isinstance(k, int) else flat[:, bass.ds(k * n, n)]

        def right_half(ap, n):
            return ap.rearrange("p (b e c) -> p b e c", e=2, c=n)[:, :, 1, :]

        z = buf[:, :, :].rearrange("p a (t c) -> p (a t) c", c=T)
        zflat = buf[:, :, :].rearrange("p a c -> p (a c)")
        xin = tiles(6, 2)
        a_pad = conv[:, 0:4 * (T + PADC)].rearrange("p (t c) -> p t c", t=4)
        a_acc = conv[:, 4 * (T + PADC):].rearrange("p (t c) -> p t c", t=4)
        tmp_a, tmp_b = tiles(6), tiles(7)
        sq3 = conv[:, 0:3 * T].rearrange("p (s c) -> p s c", s=3)
        sq8 = conv[:, 0:KT * T].rearrange("p (s c) -> p s c", s=KT)
        level_t = state[:, :, :, :].rearrange("p a h t -> p (a h t)").rearrange("p (h c t) -> p h c t", h=HEADS, c=NT)
        head_sq = (state[:, 0], state[:, 1], vnew[:, :, :], rstd[:, :].rearrange("p (c t) -> p c t", c=NT))
        early = stream[:, :, :].rearrange("p a c -> p (a c)")
        gm_g, gm_b, gm_bias = early[:, 0:512], early[:, 512:1024], early[:, 1024:1536]
        ws, pw = early[:, 1536:2048], early[:, 2048:2560]
        gains = early[:, 0:1536]

        beta, g_col, gam, egl = (small[:, n, :] for n in range(4))
        kbe_s, kd_s, s5, s6, s7, s8 = (small[:, n, :] for n in range(4, 10))
        stat = small[:, 10:12, :].rearrange("p a b -> p (a b)")
        mv = small[:, 12, :]
        r_ln = small[:, 13, :]
        negmax, denom = small[:, 14, :], small[:, 15, :]

        raw_in = [sem(f"raw_in{s}") for s in range(RING)]
        hi_ready, lo_ready = sem("hi_ready"), sem("lo_ready")
        unit_done = sem("unit_done")
        z_free = sem("z_free")
        taken = sem("taken")
        gate_free = sem("gate_free")
        merged = sem("merged")
        x_in = [sem(f"x_in{k}") for k in range(4)]
        dve_step = sem("dve_step")
        names = ("const_in params_in h_low_even h_low_odd x_sum x_added x_root y_mm x2_in mem_in early_in "
                 "f_in out_sent sq_act sq_pool cols_in x_split h_read std_ready bd_mm bd_t taps_done "
                 "a_ready h_ready h_hi bd_hi bd_split bd_ready bd_exp bd_act gelu_ready pooled pool_mm "
                 "pool_scaled p_hi p_split vt_ready vn_ready mix_ready c_ready c_hi c_split conv_q "
                 "silu_ready qk_sum ln_var ln_std sig2_ready qkv_t qkv_tok qk_sq qk_std qk_norm qk_back "
                 "qk_feat gamrow gb_ready gam_ready egr_ready dec_pre dec_exp attn_mm a_mm x0_ready y0_mm "
                 "lv_t lv_masked lv_p lv_y lv_x lv_xt v_tok o_sum kd_ready ks_mm rhs_ready v_mm v_ready "
                 "s_mm s_ready o_mm o_tok o_sq o_std o_norm o_back dg_silu o_feat o_hi o_split ca_t "
                 "ca_norm ca_back ca_silu a_hi a_split m_hi m_split mem_sq mem_sum mem_std m_hi2 m_split2 "
                 "x1_sq x1_sum x1_std x1_hi x1_split vt2 vt2_hi vt2_taken score_mm nmax exp_done "
                 "probs_ready pt_mm pt_ready pv_mm ao_hi ao_split x2_sq x2_sum x2_std x2_hi x2_split "
                 "x2t_mm x2t_ready h1_ready h1_hi h1_split y_ready y_sq y_std y_out gram_ready decay_ready "
                 "mem_added x1_added x2_added mem_r x1_r x2_r").split()
        s = {n: sem(n) for n in names}

        block = ctx.enter_context(nc.Block())

        @block.sync
        def _(sp):
            sp.dma_start(raw[:, 0, :], wall[0]).then_inc(raw_in[0], 16)
            for k in range(4):
                sp.dma_start(xin[:, 2 * k:2 * k + 2, :], x_t[:, 2 * k:2 * k + 2, :]).then_inc(x_in[k], 16)
            for u in range(1, RING):
                sp.dma_start(raw[:, u, :], wall[u]).then_inc(raw_in[u], 16)
            for k, slot, _ in units(sp, RING, NU - RING):
                sp.wait_ge(lo_ready, k + 1)
                sp.dma_start(raw[:, slot, :], wall[k + RING]).then_inc(raw_in[slot], 16)
            out_v = out[0].rearrange("(t p) d -> p t d", p=P)
            y_out = conv[:, 0:4096].rearrange("p (t d) -> p t d", t=NT)
            for t in range(NT - 1):
                sp.wait_ge(s["y_out"], t + 1)
                sp.dma_start(out_v[:, t, :], y_out[:, t, :]).then_inc(s["out_sent"], 16)
            for half in range(2):
                sp.wait_ge(s["y_out"], NT + half)
                sp.dma_start(out_v[:, NT - 1, half * T:(half + 1) * T],
                             y_out[:, NT - 1, half * T:(half + 1) * T]).then_inc(s["out_sent"], 16)
            sp.wait_ge(s["out_sent"], 16 * (NT + 1))

        @block.gpsimd
        def _(pool):
            def low(k, slot):
                pool.wait_ge(hi_ready, k + 1)
                nc.gpsimd.tensor_tensor(wlo[:, slot, :], raw[:, slot, :], whi[:, slot, :].bitcast(F32),
                                        ALU.subtract).then_inc(lo_ready, 1)

            low(0, 0)
            for k in range(1, KT, 2):
                if k == 7:
                    low(1, 1)
                pool.wait_ge(x_in[k // 2], 16)
                nc.gpsimd.tensor_tensor(sq8[:, k, :], xin[:, k, :], xin[:, k, :], ALU.mult).then_inc(s["sq_pool"], 1)
            for k, slot, _ in units(pool, 2, 8):
                low(k + 2, slot)
            for k in range(1, KT, 2):
                pool.wait_ge(s["h_ready"], KT + k + 1)
                nc.gpsimd.tensor_tensor(alo[:, k, :], xin[:, k, :], ahi[:, k, :].bitcast(F32),
                                        ALU.subtract).then_inc(s["h_low_odd"], 1)
            for k, slot, _ in units(pool, 10, NU - 10):
                low(k + 10, slot)

        @block.tensor
        def _(pe):
            def three(dst, st_hi, st_lo, mv_hi, mv_lo, first, last):
                nc.tensor.matmul(dst, st_hi, mv_hi, start=first, stop=False, skip_group_check=True)
                nc.tensor.matmul(dst, st_hi, mv_lo, start=False, stop=False, skip_group_check=True)
                return nc.tensor.matmul(dst, st_lo, mv_hi, start=False, stop=last, skip_group_check=True)

            def unit(slot, bank, ready, n=T, hi=ahi, lo=alo, tell=None):
                fhi = hi[:, :, :].rearrange("p a c -> p (a c)")
                flo = lo[:, :, :].rearrange("p a c -> p (a c)")
                for k in range(KT):
                    if ready is None:
                        pe.wait_ge(s[("h_low_even", "h_low_odd")[k % 2]], k // 2 + 1)
                    else:
                        pe.wait_ge(ready, k + 1)
                    last = three(ps[:, bank, 0:n], whi[:, slot, k * P:(k + 1) * P], wlo[:, slot, k * P:(k + 1) * P],
                                 fhi[:, k * n:(k + 1) * n], flo[:, k * n:(k + 1) * n], k == 0, k == KT - 1)
                    if tell is not None and k < KT - 1:
                        last.then_inc(tell, 1)
                last.then_inc(unit_done, 1)

            def z_units(first, count):
                for k, slot, _ in units(pe, first, count):
                    pe.wait_ge(lo_ready, k + first + 1)
                    pe.wait_ge(z_free, k + first + 1)
                    unit(slot, slot, None)

            def taken_units(name, ready, count=None, skip=0, **how):
                first = FIRST[name] + skip
                for k, slot, _ in units(pe, first, count or dict(PHASES)[name]):
                    pe.wait_ge(lo_ready, k + first + 1)
                    pe.wait_ge(taken, k + TAKE[name] + skip + 1)
                    unit(slot, slot, ready, **how)

            def merge(name, n, ready, after={}):
                first = FIRST[name]
                for i in turns(pe, after):
                    for j in range(2):
                        slot = (first + j) % RING
                        pe.wait_ge(lo_ready, i * 3 + first + j + 1)
                        pe.wait_ge(gate_free, i * 2 + 8 * n + j + 1)
                        unit(slot, j, None)
                    slot = (first + 2) % RING
                    pe.wait_ge(lo_ready, i * 3 + first + 3)
                    pe.wait_ge(merged, i * 2 + 8 * n + 2)
                    pe.wait_ge(ready, MT)
                    for e in range(2):
                        for c in range(MT):
                            at = (c * 2 + e) * P
                            last = three(ps[:, 2 + e, :], whi[:, slot, at:at + P], wlo[:, slot, at:at + P],
                                         bhi[:, c, :], blo[:, c, :], c == 0, c == MT - 1)
                    last.then_inc(unit_done, 1)

            def mean_square(src, n, ready, tell):
                pe.wait_ge(ready, 1)
                nc.tensor.matmul(ps[:, 7, 0:n], ones, src, start=True, stop=True).then_inc(tell, 1)

            def x_unit(k, slot, tell=None):
                pe.wait_ge(lo_ready, k + 1)
                pe.wait_ge(taken, k + 1)
                unit(slot, slot, s["x_split"], tell=tell)

            x_unit(0, 0)
            x_unit(1, 1)
            mean_square(sq8[:, 0, :], T, s["x_added"], s["x_sum"])
            for k, slot, _ in units(pe, 2, 5):
                x_unit(k + 2, slot)
            pe.wait_ge(s["bd_split"], 1)
            for k in range(KT):
                last = three(ps[0:8, 3, :], bdhi[:, k * 8:k * 8 + 8], bdlo[:, k * 8:k * 8 + 8], ahi[:, k, :], alo[:, k, :],
                             k == 0, k == KT - 1)
            last.then_inc(s["bd_mm"], 1)
            x_unit(7, 7 % RING, tell=s["h_read"])
            pe.wait_ge(taken, 3 + 8)
            z_units(8, 4)
            pe.wait_ge(s["bd_t"], 1)
            pe.wait_ge(s["const_in"], 16)
            for t in range(NT):
                last = nc.tensor.transpose(ps[:, 4, t * 8:t * 8 + 8], sq[0:8, 0, t * P:(t + 1) * P], ident[0:8, 0:8])
            last.then_inc(s["bd_ready"], 1)
            z_units(12, 8)
            pe.wait_ge(s["pooled"], 1)
            pe.wait_ge(s["bd_act"], 4)
            pe.wait_ge(s["gb_ready"], 1)
            for g in range(4):
                nc.tensor.matmul(ps[:, 4 + g, :], pw[:, g * P:(g + 1) * P], z[:, g, :],
                                 start=True, stop=True).then_inc(s["pool_mm"], 1)
            z_units(20, 4)
            pe.wait_ge(s["gelu_ready"], 1)
            pe.wait_ge(s["pool_scaled"], 4)
            for t in range(NT):
                for f in range(4):
                    last = nc.tensor.transpose(ps[:, 4 + t, f * P:(f + 1) * P], tiles(2)[:, f, t * P:(t + 1) * P], ident)
                last.then_inc(s["vt_ready"], 1)
            z_units(24, 4)
            pe.wait_ge(s["vn_ready"], 1)
            nc.tensor.matmul(ps[:, 4, 0:16], tri, g_col, start=True, stop=True).then_inc(s["gamrow"], 1)
            z_units(28, 2)
            pe.wait_ge(s["gam_ready"], 1)
            for h in range(HEADS):
                for c in range(NT):
                    n = h * NT + c
                    last = nc.tensor.matmul(ps[:, 4 + h, c * P:(c + 1) * P], g_col[:, n:n + 1].to_broadcast([P, P]),
                                            tri, start=True, stop=True)
                last.then_inc(s["gamrow"], 1)
            z_units(30, 2)
            pe.wait_ge(s["dec_pre"], 4)
            vn = tiles(2)
            for g in range(4):
                for n in range(NT):
                    last = nc.tensor.matmul(ps[:, 4 + g, n * P:(n + 1) * P], vn[:, n, g * P:(g + 1) * P],
                                            ws[:, g * P:(g + 1) * P], start=True, stop=True)
                last.then_inc(s["mix_ready"], 1)
            pe.wait_ge(z_free, 3 + 32)

            def to_tokens(n, src, made, used):
                pe.wait_ge(s["silu_ready"], made)
                for h in range(HEADS):
                    pe.wait_ge(s[used[0]], used[1] + h + 1)
                    for c in range(NT):
                        last = nc.tensor.transpose(ps[:, 4 + h, c * P:(c + 1) * P],
                                                   tiles(src)[:, h, c * P:(c + 1) * P], ident)
                    last.then_inc(s["qkv_t"], 1)

            def to_features(n, src, used):
                pe.wait_ge(s["qk_norm"], n + 1)
                for h in range(HEADS):
                    pe.wait_ge(s[used], h + 1)
                    for c in range(NT):
                        last = nc.tensor.transpose(ps[:, 4 + h, c * P:(c + 1) * P], mats(src)[:, h, c, :], ident)
                    last.then_inc(s["qk_back"], 1)

            merge("merge_p", 0, s["p_split"], after={
                0: lambda: to_tokens(0, 7, 1, ("c_ready", 0)),
                1: lambda: to_tokens(1, 3, 2, ("qk_sq", 0)),
                2: lambda: to_tokens(2, 4, 3, ("qk_sq", 4)),
                3: lambda: to_features(0, 2, "v_tok")})

            qn, kn = mats(4), mats(1)

            def gram(other, used, tell):
                for h in range(HEADS):
                    pe.wait_ge(*used(h))
                    for c in range(NT):
                        last = nc.tensor.matmul(ps[:, 4 + h, c * P:(c + 1) * P], kn[:, h, c, :], other[:, h, c, :],
                                                start=True, stop=True)
                    last.then_inc(s[tell], 1)

            merge("merge_c", 1, s["c_split"], after={
                0: lambda: to_features(1, 7, "qk_feat"),
                1: lambda: gram(kn, lambda h: (s["qk_feat"], 5 + h), "a_mm"),
                2: lambda: gram(qn, lambda h: (s["a_ready"], h + 1), "attn_mm")})
            a_m, x_m, y_m = mats(0), mats(4), mats(2)
            pe.wait_ge(s["gram_ready"], 4)
            for h in range(HEADS):
                pe.wait_ge(s["x0_ready"], h + 1)
                for c in range(NT):
                    last = nc.tensor.transpose(ps[:, 4 + h, c * P:(c + 1) * P], x_m[:, h, c, :], ident)
                last.then_inc(s["y0_mm"], 1)
            for lv in range(6):
                n = 2 << lv
                for h in range(HEADS):
                    if lv:
                        pe.wait_ge(s["lv_y"], lv * 4 - 4 + h + 1)
                    pe.wait_ge(s["lv_x"], lv * 4 + h + 1)
                    for c in range(NT):
                        last = nc.tensor.matmul(ps[:, 4 + h, c * 64:(c + 1) * 64], a_m[:, h, c, :],
                                                right_half(y_m[:, h, c, :], n), start=True, stop=True)
                    last.then_inc(s["lv_t"], 1)
                if lv == 0:
                    pe.wait_ge(gate_free, 2 + 16)
                    pe.wait_ge(merged, 2 + 16)
                for h in range(HEADS):
                    pe.wait_ge(s["lv_masked"], lv * 4 + h + 1)
                    for c in range(NT):
                        last = nc.tensor.matmul(ps[:, h, c * 64:(c + 1) * 64], x_m[:, h, c, :], level_t[:, h, c, :],
                                                start=True, stop=True)
                    last.then_inc(s["lv_p"], 1)
                for h in range(HEADS if lv < 5 else 0):
                    pe.wait_ge(s["lv_y"], lv * 4 + h + 1)
                    for c in range(NT):
                        last = nc.tensor.transpose(ps[:, 4 + h, c * P:(c + 1) * P], y_m[:, h, c, :], ident)
                    last.then_inc(s["lv_xt"], 1)
            def gate_unit(k):
                pe.wait_ge(lo_ready, FIRST["dgate"] + k + 1)
                unit((FIRST["dgate"] + k) % RING, 4 + k, None)

            k_t, qd, at_m, kd, vb = mats(1), mats(6), mats(5), mats(7), mats(3)
            pe.wait_ge(s["lv_y"], 24)
            for c in range(NT):
                old = state[:, (c + 1) % 2]
                ob = 2 + c % 2
                if c:
                    pe.wait_ge(s["s_ready"], c)
                    for h in range(HEADS):
                        last = nc.tensor.matmul(ps[:, 1, h * P:(h + 1) * P], k_t[:, h, c, :], old[:, h, :],
                                                start=True, stop=True)
                    last.then_inc(s["ks_mm"], 1)
                    if c >= 2:
                        pe.wait_ge(s["o_tok"], c - 1)
                    for h in range(HEADS):
                        nc.tensor.matmul(ps[:, ob, h * P:(h + 1) * P], qd[:, h, c, :], old[:, h, :],
                                         start=h == 0, stop=False, skip_group_check=True)
                    pe.wait_ge(s["rhs_ready"], 4 * c)
                    pe.wait_ge(s["v_ready"], c)
                for h in range(HEADS):
                    last = nc.tensor.matmul(ps[:, 0, h * P:(h + 1) * P], y_m[:, h, c, :], vb[:, h, c, :],
                                            start=True, stop=True)
                last.then_inc(s["v_mm"], 1)
                if c in (1, 2):
                    gate_unit(c - 1)
                pe.wait_ge(s["v_ready"], c + 1)
                if c < NT - 1:
                    if c == 0:
                        pe.wait_ge(s["kd_ready"], 1)
                    for h in range(HEADS):
                        last = nc.tensor.matmul(ps[:, 1, h * P:(h + 1) * P], kd[:, h, c, :], vnew[:, h, :],
                                                start=True, stop=True)
                    last.then_inc(s["s_mm"], 1)
                for h in range(HEADS):
                    last = nc.tensor.matmul(ps[:, ob, h * P:(h + 1) * P], at_m[:, h, c, :], vnew[:, h, :],
                                            start=c == 0, stop=True, skip_group_check=True)
                last.then_inc(s["o_mm"], 1)
            for k in range(2, 4):
                gate_unit(k)
            o_tok = buf[:, 0, :].rearrange("p (c h v) -> p c h v", c=NT, h=HEADS)
            pe.wait_ge(s["o_norm"], 1)
            for h in range(HEADS):
                pe.wait_ge(taken, 3 + TAKE["dgate"] + h + 1)
                for c in range(NT):
                    last = nc.tensor.transpose(ps[:, 4 + h, c * P:(c + 1) * P], o_tok[:, c, h, :], ident)
                last.then_inc(s["o_back"], 1)
            pe.wait_ge(s["o_tok"], NT)

            def conv_tokens():
                pe.wait_ge(s["taps_done"], 4 + 4 * PADC)
                pe.wait_ge(s["o_feat"], 4)
                for t in range(NT):
                    for f in range(4):
                        last = nc.tensor.transpose(ps[:, 4 + t, f * P:(f + 1) * P], a_acc[:, f, t * P:(t + 1) * P],
                                                   ident)
                    last.then_inc(s["ca_t"], 1)

            def conv_back():
                pe.wait_ge(s["ca_norm"], 1)
                for f in range(4):
                    for t in range(NT):
                        last = nc.tensor.transpose(ps[:, 4 + f, t * P:(t + 1) * P], tiles(2)[:, t, f * P:(f + 1) * P],
                                                   ident)
                    last.then_inc(s["ca_back"], 1)

            merge("merge_o", 2, s["o_split"], after={0: conv_tokens, 2: conv_back})
            merge("merge_a", 3, s["a_split"])
            pe.wait_ge(gate_free, 2 + 32)
            taken_units("out", s["m_split"])
            mean_square(rstd[:, 0:MEM], MEM, s["mem_added"], s["mem_sum"])
            taken_units("kv", s["m_split2"], n=MEM, hi=bhi, lo=blo)
            pe.wait_ge(s["mem_r"], 1)
            mean_square(sq[:, 0, :], T, s["x1_added"], s["x1_sum"])
            for m in range(2):
                for f in range(KT):
                    pe.wait_ge(taken, 3 + TAKE["kv"] + 8 + f + 1)
                    last = nc.tensor.transpose(ps[:, 3 + 2 * m + f // 4, (f % 4) * P:(f % 4 + 1) * P],
                                               buf[:, 3, f * MEM + m * P:f * MEM + (m + 1) * P], ident)
                last.then_inc(s["vt2"], 1)
            taken_units("q", s["x1_split"])
            q_t, k_t = tiles(0, 2), buf[:, 2, :]
            pe.wait_ge(taken, 3 + TAKE["q"] + 8)
            pe.wait_ge(s["vt2_taken"], 2)
            pe.wait_ge(s["x1_r"], 1)
            for h in range(HEADS):
                for pair in range(2):
                    for e in range(2):
                        t = 2 * pair + e
                        for d in range(2):
                            f = 2 * h + d
                            last = nc.tensor.matmul(ps[:, 2 * h + pair, e * MEM:(e + 1) * MEM],
                                                    q_t[:, f, t * P:(t + 1) * P], k_t[:, f * MEM:(f + 1) * MEM],
                                                    start=d == 0, stop=d == 1)
                    last.then_inc(s["score_mm"], 1)
            probs = buf[:, 5:7, :].rearrange("p a (b c) -> p (a b) c", c=T)
            for b in range(8):
                pe.wait_ge(s["probs_ready"], b + 1)
                for m in range(2):
                    for e in range(2):
                        last = nc.tensor.transpose(ps[:, b, (2 * m + e) * P:(2 * m + e + 1) * P],
                                                   probs[:, b, e * MEM + m * P:e * MEM + (m + 1) * P], ident)
                last.then_inc(s["pt_mm"], 1)
            v_hi, v_lo = (b[:, :, :].rearrange("p a c -> p (a c)") for b in (bhi, blo))
            for f in range(KT):
                h = f // 2
                pe.wait_ge(s["pt_ready"], max(2 * h + 2, f + 1))
                for m in range(2):
                    at_ = m * D + f * P
                    last = three(ps[:, f, :], v_hi[:, at_:at_ + P], v_lo[:, at_:at_ + P], ahi[:, 2 * h + m, :],
                                 alo[:, 2 * h + m, :], m == 0, m == 1)
                last.then_inc(s["pv_mm"], 1)
            pe.wait_ge(s["ao_split"], 3)
            taken_units("wo", s["ao_split"])

            def w1_unit(first, skip, count):
                for k, slot, _ in units(pe, first, count):
                    pe.wait_ge(lo_ready, k + first + 1)
                    pe.wait_ge(taken, k + TAKE["w1"] + skip + 1)
                    for kk in range(KT):
                        hi, lo = (bhi, blo) if kk < 4 else (ahi, alo)
                        pe.wait_ge(s["x2_split"], kk + 1)
                        last = three(ps[:, slot, :], whi[:, slot, kk * P:(kk + 1) * P], wlo[:, slot, kk * P:(kk + 1) * P],
                                     hi[:, kk, :], lo[:, kk, :], kk == 0, kk == KT - 1)
                    last.then_inc(unit_done, 1)

            w1 = FIRST["w1"]
            w1_unit(w1, 0, 1)
            mean_square(sq[:, 0, :], T, s["x2_added"], s["x2_sum"])
            w1_unit(w1 + 1, 1, 11)
            for half in range(2):
                if half:
                    w1_unit(w1 + 12, 12, 12)
                    pe.wait_ge(s["x2t_ready"], 4)
                for t in range(NT):
                    for f in range(4):
                        last = nc.tensor.transpose(ps[:, 3 + t, f * P:(f + 1) * P],
                                                   stream[:, 4 * half + f, t * P:(t + 1) * P], ident)
                    last.then_inc(s["x2t_mm"], 1)
            w1_unit(w1 + 24, 24, 8)
            pe.wait_ge(s["x2t_ready"], 8)
            pe.wait_ge(s["x2_r"], 1)

            def w2_product(slot, t, start, stop, halves=(0, 1)):
                for half in halves:
                    last = three(ps[:, 2 * t + half, :], ahi[:, slot, t * P:(t + 1) * P],
                                 alo[:, slot, t * P:(t + 1) * P], whi[:, slot, half * T:(half + 1) * T],
                                 wlo[:, slot, half * T:(half + 1) * T], start, stop)
                return last

            def w2_unit(k, slot, start):
                pe.wait_ge(lo_ready, k + FIRST["w2"] + 1)
                pe.wait_ge(s["h1_split"], k + 1)
                for t in reversed(range(NT)):
                    if start and t == 1:
                        pe.wait_ge(taken, 3 + TAKE["w1"] + 32)
                    last = w2_product(slot, t, start, False)
                last.then_inc(unit_done, 1)

            w2 = FIRST["w2"]
            w2_unit(0, w2 % RING, True)
            for k, slot, _ in units(pe, w2 + 1, 28):
                w2_unit(k + 1, slot, False)
            def w2_rest(t, first, end, halves=(0, 1)):
                for k in range(first, end):
                    last = w2_product((w2 + k) % RING, t, False, k == 31, halves)
                return last

            pe.wait_ge(lo_ready, NU - 1)
            pe.wait_ge(s["h1_split"], 31)
            for t in range(2):
                w2_rest(t, 29, 31)
            pe.wait_ge(lo_ready, NU)
            pe.wait_ge(s["h1_split"], 32)
            for t in range(NT - 1):
                w2_rest(t, 31 if t < 2 else 29, 32).then_inc(s["y_mm"], 1)
            for half in range(2):
                w2_rest(NT - 1, 29, 32, (half,)).then_inc(s["y_mm"], 1)

        @block.scalar
        def _(act):
            act.sem_inc(z_free, 3 + 8)
            act.sem_inc(gate_free, 2)
            act.dma_start(cols[:, :], cols_d).then_inc(s["cols_in"], 16)

            def high(slot, turn):
                act.wait_ge(raw_in[slot], (turn + 1) * 16)
                nc.scalar.activation(whi[:, slot, :], raw[:, slot, :], ACT.Copy).then_inc(hi_ready, 1)

            def feed(first, k, slot, turn):
                act.wait_ge(unit_done, k + first + 1)
                high(slot, turn + 1)

            def feed_units(first, count):
                for k, slot, turn in units(act, first, count):
                    feed(first, k, slot, turn)

            def z_units(first, count, dst):
                for k, slot, turn in units(act, first, count):
                    act.wait_ge(unit_done, k + first + 1)
                    nc.scalar.activation(zflat[:, bass.ds((k + dst) * T, T)], ps[:, slot, :],
                                         ACT.Copy).then_inc(z_free, 1)
                    high(slot, turn + 1)

            def merge(name, n, after={}, inside=None):
                first = FIRST[name]
                for i in turns(act, after):
                    for j in range(RING):
                        if inside is not None and isinstance(i, int) and i == 3 and j == 2:
                            inside()
                        slot, turn = (first + j) % RING, i + (first + j) // RING
                        act.wait_ge(unit_done, i * 3 + first + j + 1)
                        if j < 2:
                            act.wait_ge(merged, i * 2 + 8 * n + 2)
                            nc.scalar.activation(sig[:, j, :], ps[:, j, :], ACT.Sigmoid).then_inc(gate_free, 1)
                        high(slot, turn + 1)

            def split_high(dst, src, tell, scale=1.0):
                nc.scalar.activation(dst, src, ACT.Copy, scale=scale).then_inc(tell, 1)

            high(0, 0)
            act.wait_ge(s["cols_in"], 16)
            for k in range(KT):
                act.wait_ge(x_in[k // 2], 16)
                split_high(ahi[:, k, :], xin[:, k, :], s["h_ready"], col("norm_mix", k))
            high(1, 0)
            for k in range(0, KT, 2):
                nc.scalar.activation(sq8[:, k, :], xin[:, k, :], ACT.Square).then_inc(s["sq_act"], 1)
            act.dma_start(rows[:, :], rows_d.partition_broadcast(P)).then_inc(s["params_in"], 16)
            act.dma_start(wbd[:, :], w_bd).then_inc(s["params_in"], 16)
            high(2, 0)
            act.dma_start(const[:, :], const_d).then_inc(s["const_in"], 16)
            act.dma_start(gains, gains_d.partition_broadcast(P)).then_inc(s["early_in"], 16)
            act.dma_start(ws, ws_t).then_inc(s["early_in"], 16)
            act.dma_start(pw, pool_w).then_inc(s["early_in"], 16)
            feed(0, 0, 0, 0)
            act.wait_ge(s["x_sum"], 1)
            nc.scalar.activation(rstd[:, :], ps[:, 7, :], ACT.Sqrt, bias=col("eps6"), scale=1.0 / D).then_inc(s["x_root"], 1)
            feed(0, 1, 1, 0)
            act.wait_ge(s["params_in"], 32)
            nc.scalar.activation(bdhi[:, :], wbd[:, :], ACT.Copy).then_inc(s["bd_hi"], 1)
            feed_units(2, 5)
            act.wait_ge(s["h_hi"], KT)
            for k in range(KT):
                if k < KT - 1:
                    act.wait_ge(s["h_read"], k + 1)
                else:
                    act.wait_ge(unit_done, 8)
                split_high(ahi[:, k, :], xin[:, k, :], s["h_ready"])
            feed(0, 7, 7 % RING, 7 // RING)
            act.wait_ge(taken, 3 + 8)
            nc.scalar.activation(buf[:, 3, :], buf[:, 3, :], ACT.Sigmoid).then_inc(s["sig2_ready"], 1)
            z_units(8, 4, 0)
            act.wait_ge(s["bd_exp"], 1)
            nc.scalar.activation(s5, s6, ACT.Exp, scale=-1.0).then_inc(s["bd_act"], 1)
            nc.scalar.activation(rows[:, 0:4], rows[:, 0:4], ACT.Exp).then_inc(s["bd_act"], 1)
            act.wait_ge(s["bd_exp"], 2)
            nc.scalar.activation(s6, s5, ACT.Ln).then_inc(s["bd_act"], 1)
            act.wait_ge(s["bd_ready"], 1)
            nc.scalar.activation(beta, ps[:, 4, 0:32].rearrange("p (t e) -> p e t", e=8)[:, 0:4, :],
                                 ACT.Sigmoid).then_inc(s["bd_act"], 1)
            z_units(12, 8, 4)
            act.wait_ge(z_free, 3 + 20)
            for n in (1, 0):
                nc.scalar.activation(buf[:, 1 + n, :], buf[:, 1 + n, :], ACT.Gelu).then_inc(s["gelu_ready"], 1)
            act.wait_ge(s["pool_mm"], 4)
            for g in range(4):
                nc.scalar.activation(z[:, g, :], ps[:, 4 + g, :], ACT.Copy, scale=col("pool_s", g)).then_inc(s["pool_scaled"], 1)
            act.wait_ge(s["pool_scaled"], 4)
            for g in range(4):
                split_high(bhi[:, g, :], z[:, g, :], s["p_hi"])
            z_units(20, 4, 12)
            z_units(24, 1, 16)
            act.wait_ge(s["ln_var"], 1)
            nc.scalar.activation(r_ln[:, 0:4], r_ln[:, 0:4], ACT.Sqrt, bias=col("eps5")).then_inc(s["ln_std"], 1)
            z_units(25, 5, 17)
            for h in range(HEADS):
                act.wait_ge(s["gamrow"], h + 2)
                nc.scalar.activation(tiles(6)[:, h, :], ps[:, 4 + h, :], ACT.Exp).then_inc(s["egr_ready"], 1)
            z_units(30, 2, 22)
            def silu(n, at_):
                act.wait_ge(s["conv_q"], n + 1)
                nc.scalar.activation(buf[:, at_, :], buf[:, at_, :], ACT.Silu).then_inc(s["silu_ready"], 1)

            silu(0, 7)
            silu(1, 3)

            def to_tokens(n, dst):
                for h in range(HEADS):
                    act.wait_ge(s["qkv_t"], 4 * n + h + 1)
                    nc.scalar.activation(tiles(dst)[:, h, :], ps[:, 4 + h, :], ACT.Copy).then_inc(s["qkv_tok"], 1)
                    if n:
                        act.wait_ge(s["qk_sum"], h + 1)
                    nc.scalar.activation(head_sq[h].rearrange("p c t -> p (c t)"), ps[:, 4 + h, :],
                                         ACT.Square).then_inc(s["qk_sq"], 1)

            def root(n):
                act.wait_ge(s["qk_std"], n + 1)
                nc.scalar.activation((s7, s8)[n], (s7, s8)[n], ACT.Sqrt).then_inc(s["std_ready"], 1)

            def decays():
                act.wait_ge(s["decay_ready"], 1)
                nc.scalar.activation(kbe_s, gam, ACT.Exp).then_inc(s["bd_act"], 1)
                nc.scalar.activation(kd_s, kd_s, ACT.Exp).then_inc(s["bd_act"], 1)
                nc.scalar.activation(egl, egl, ACT.Exp).then_inc(s["bd_act"], 1)
                nc.scalar.activation(buf[:, 0, :], buf[:, 0, :], ACT.Exp, scale=-1.0).then_inc(s["dec_exp"], 1)
                nc.scalar.activation(buf[:, 5, :], buf[:, 5, :], ACT.Exp).then_inc(s["dec_exp"], 1)

            def to_features(n, dst):
                for h in range(HEADS):
                    act.wait_ge(s["qk_back"], 4 * n + h + 1)
                    nc.scalar.activation(tiles(dst)[:, h, :], ps[:, 4 + h, :], ACT.Copy).then_inc(s["qk_feat"], 1)

            merge("merge_p", 0, after={0: lambda: to_tokens(0, 2), 1: lambda: (root(0), to_tokens(1, 7), silu(2, 4)),
                                       2: lambda: (root(1), decays())})
            act.wait_ge(unit_done, FIRST["merge_c"])
            for g in range(4):
                split_high(bhi[:, g, :], tiles(1)[:, g, :], s["c_hi"])
            to_features(0, 4)
            act.wait_ge(s["c_split"], 4)
            merge("merge_c", 1, after={0: lambda: to_features(1, 1)})
            for h in range(HEADS):
                act.wait_ge(s["y0_mm"], h + 1)
                nc.scalar.activation(tiles(2)[:, h, :], ps[:, 4 + h, :], ACT.Copy).then_inc(s["lv_x"], 1)
            with act.Fori(0, 5) as lv:
                for h in range(HEADS):
                    act.wait_ge(s["lv_xt"], lv * 4 + h + 1)
                    nc.scalar.activation(tiles(4)[:, h, :], ps[:, 4 + h, :], ACT.Copy).then_inc(s["lv_x"], 1)
            for c in range(NT):
                act.wait_ge(s["o_mm"], c + 1)
                nc.scalar.activation(tiles(0)[:, c, :], ps[:, 2 + c % 2, :], ACT.Copy).then_inc(s["o_tok"], 1)
                if c < 2:
                    slot_ = (FIRST["dgate"] + c) % RING
                    feed(FIRST["dgate"], c, slot_, (FIRST["dgate"] + c) // RING)
            act.wait_ge(s["o_tok"], NT)
            nc.scalar.activation(buf[:, 4, :], buf[:, 0, :], ACT.Square).then_inc(s["o_sq"], 1)
            act.wait_ge(s["o_sum"], 1)
            nc.scalar.activation(s5, s5, ACT.Sqrt, bias=col("eps6"), scale=1.0 / P).then_inc(s["o_std"], 1)
            feed_units(FIRST["dgate"] + 2, 2)
            for h in range(HEADS):
                act.wait_ge(taken, 3 + TAKE["dgate"] + h + 1)
                nc.scalar.activation(tiles(6)[:, h, :], tiles(6)[:, h, :], ACT.Silu).then_inc(s["dg_silu"], 1)
            for h in range(HEADS):
                act.wait_ge(s["o_feat"], h + 1)
                split_high(bhi[:, h, :], tiles(1)[:, h, :], s["o_hi"])

            def conv_root():
                act.wait_ge(s["ln_var"], 2)
                nc.scalar.activation(r_ln[:, 0:4], r_ln[:, 0:4], ACT.Sqrt, bias=col("eps5")).then_inc(s["ln_std"], 1)

            def conv_back():
                for f in range(4):
                    act.wait_ge(s["ca_back"], f + 1)
                    nc.scalar.activation(tiles(3)[:, f, :], ps[:, 4 + f, :], ACT.Silu, bias=col("ln_a_b", f),
                                         scale=col("ln_a_g", f)).then_inc(s["ca_silu"], 1)

            merge("merge_o", 2, after={0: conv_root, 2: conv_back})
            act.wait_ge(s["ca_silu"], 4)
            act.wait_ge(unit_done, FIRST["merge_a"])
            for f in range(4):
                split_high(bhi[:, f, :], tiles(3)[:, f, :], s["a_hi"])
            act.wait_ge(s["o_feat"], 4)
            act.dma_start(xin, x_t).then_inc(s["x2_in"], 16)
            act.dma_start(buf[:, 4, :], mem_t).then_inc(s["mem_in"], 16)

            def mem_squares():
                act.wait_ge(s["mem_in"], 16)
                nc.scalar.activation(buf[:, 5, :], buf[:, 4, :], ACT.Square).then_inc(s["mem_sq"], 1)

            def merged_high():
                act.wait_ge(unit_done, FIRST["out"] - 1)
                for k in range(6):
                    act.wait_ge(merged, 2 + 24 + k + 1)
                    split_high(ahi[:, k, :], stream[:, k, :], s["m_hi"])

            merge("merge_a", 3, after={0: mem_squares, 2: lambda: None}, inside=merged_high)
            for k in range(6, KT):
                act.wait_ge(merged, 2 + 24 + k + 1)
                split_high(ahi[:, k, :], stream[:, k, :], s["m_hi"])
            act.dma_start(sig[:, :, :].rearrange("p a c -> p (a c)"), norm_f.partition_broadcast(P)).then_inc(s["f_in"], 16)
            act.wait_ge(unit_done, FIRST["out"])
            for k in range(KT):
                split_high(bhi[:, k // 2, (k % 2) * MEM:(k % 2 + 1) * MEM], buf[:, 4, k * MEM:(k + 1) * MEM],
                           s["m_hi2"], col("norm_mem", k))

            def residual_units(name, tell, late=None):
                first = FIRST[name]
                act.sem_inc(tell, 1)
                for k, slot, turn in units(act, first, 8):
                    if late is not None and isinstance(k, int) and k == 6:
                        late()
                    feed(first, k, slot, turn)
                    act.wait_ge(taken, k + 3 + TAKE[name] + 1)
                    nc.scalar.activation(sq3[:, slot, :], at(stream, k), ACT.Square).then_inc(tell, 1)

            residual_units("out", s["x1_sq"])
            act.wait_ge(s["mem_sum"], 1)
            nc.scalar.activation(rstd[:, 0:MEM], ps[:, 7, 0:MEM], ACT.Sqrt, bias=col("eps6"), scale=1.0 / D).then_inc(s["mem_std"], 1)
            for k, slot, turn in units(act, FIRST["kv"], 8):
                feed(FIRST["kv"], k, slot, turn)
                nc.scalar.activation(at(ahi, k), at(stream, k), ACT.Copy,
                                     scale=cols[:, bass.ds(k + COLS["norm_xa"], 1)]).then_inc(s["x1_hi"], 1)
            feed_units(FIRST["kv"] + 8, 8)
            act.wait_ge(s["x1_sum"], 1)
            nc.scalar.activation(sq[:, 1, :], ps[:, 7, :], ACT.Sqrt, bias=col("eps6"), scale=1.0 / D).then_inc(s["x1_std"], 1)
            for m in range(2):
                act.wait_ge(s["vt2"], m + 1)
                split_high(bhi[:, 2 * m:2 * m + 2, :], ps[:, 3 + 2 * m:5 + 2 * m, :], s["vt2_hi"])
            feed_units(FIRST["q"], 8)
            probs = buf[:, 5:7, :].rearrange("p a (b c) -> p (a b) c", c=T)
            for b in range(8):
                act.wait_ge(s["nmax"], b + 1)
                for e in range(2):
                    n = 2 * b + e
                    nc.scalar.activation(probs[:, b, e * MEM:(e + 1) * MEM], ps[:, b, e * MEM:(e + 1) * MEM], ACT.Exp,
                                         bias=negmax[:, n:n + 1], scale=1.0 / 16.0,
                                         accum_out=denom[:, n:n + 1]).then_inc(s["exp_done"], 1)
            for b in range(8):
                act.wait_ge(s["pt_mm"], b + 1)
                h, pair = b // 2, b % 2
                split_high(ahi[:, 2 * h:2 * h + 2, pair * MEM:(pair + 1) * MEM],
                           ps[:, b, :].rearrange("p (m t) -> p m t", m=2), s["ao_hi"])
            for f in range(KT):
                act.wait_ge(s["pv_mm"], f + 2 - f % 2)
                split_high(ahi[:, f, :], ps[:, f, :], s["ao_hi"])

            def x2_high(tiles_):
                for k in tiles_:
                    dst = bhi if k < 4 else ahi
                    split_high(dst[:, k, :], stream[:, k, :], s["x2_hi"], col("norm_mlp", k))

            residual_units("wo", s["x2_sq"], late=lambda: x2_high(range(4)))
            act.wait_ge(unit_done, FIRST["w1"])
            x2_high(range(4, KT))
            feed_units(FIRST["w1"], 1)
            act.wait_ge(s["x2_sum"], 1)
            nc.scalar.activation(sq[:, 1, :], ps[:, 7, :], ACT.Sqrt, bias=col("eps6"), scale=1.0 / D).then_inc(s["x2_std"], 1)
            w1 = FIRST["w1"]
            x2_tok = conv[:, 0:4096].rearrange("p (t d) -> p t d", t=NT)
            feed_units(w1 + 1, 11)
            for half in range(2):
                if half:
                    feed_units(w1 + 12, 12)
                for t in range(NT):
                    act.wait_ge(s["x2t_mm"], 4 * half + t + 1)
                    nc.scalar.activation(x2_tok[:, t, half * T:(half + 1) * T], ps[:, 3 + t, :],
                                         ACT.Copy).then_inc(s["x2t_ready"], 1)
            w2 = FIRST["w2"]

            def h1_high(k, slot):
                act.wait_ge(s["h1_ready"], k + 1)
                nc.scalar.activation(ahi[:, slot, :], zflat[:, bass.ds(k * T, T)] if not isinstance(k, int) else z[:, k, :],
                                     ACT.Copy).then_inc(s["h1_hi"], 1)

            for k in range(RING):
                h1_high(k, (w2 + k) % RING)
            feed_units(w1 + 24, 8)
            for k, slot, turn in units(act, w2, 27):
                act.wait_ge(unit_done, k + w2 + 1)
                high(slot, turn + 1)
                h1_high(k + RING, slot)
            for k in range(27, 29):
                slot = (w2 + k) % RING
                act.wait_ge(unit_done, w2 + k + 1)
                high(slot, (w2 + k) // RING + 1)
                h1_high(k + RING, slot)
            for t in range(NT):
                act.wait_ge(s["y_ready"], t + 1 if t < NT - 1 else NT + 1)
                nc.scalar.activation(stream[:, 2 * t:2 * t + 2, :], x2_tok[:, t, :].rearrange("p (a c) -> p a c", a=2),
                                     ACT.Square, accum_out=denom[:, t:t + 1]).then_inc(s["y_sq"], 1)
                act.wait_ge(s["y_sq"], t + 1)
                nc.scalar.activation(denom[:, 8 + t:9 + t], denom[:, t:t + 1], ACT.Sqrt, bias=col("eps6"),
                                     scale=1.0 / D).then_inc(s["y_std"], 1)

        @block.vector
        def _(dve):
            v = nc.vector
            steps = Steps(dve, dve_step)
            done = steps.done
            dve.sem_inc(taken, 3)
            dve.sem_inc(merged, 2)
            dve.sem_inc(s["taps_done"], 4)

            def split_low(dst, src, hi, tell, scale=None):
                if scale is None:
                    v.tensor_tensor(dst, src, hi.bitcast(F32), ALU.subtract).then_inc(tell, 1)
                else:
                    v.scalar_tensor_tensor(out=dst, in0=src, scalar=scale, in1=hi.bitcast(F32), op0=ALU.mult,
                                           op1=ALU.subtract).then_inc(tell, 1)

            def take(name, fn):
                first = FIRST[name]
                for k, slot, _ in units(dve, first, dict(PHASES)[name]):
                    dve.wait_ge(unit_done, k + first + 1)
                    fn(k, slot).then_inc(taken, 1)

            done(v.memset(ones, 1.0))
            dve.wait_ge(s["cols_in"], 16)
            for k in range(KT):
                dve.wait_ge(s["h_ready"], k + 1)
                split_low(alo[:, k, :], xin[:, k, :], ahi[:, k, :], s["x_split"], col("norm_mix", k))
            dve.wait_ge(s["sq_act"], 4)
            dve.wait_ge(s["sq_pool"], 4)
            for n in (4, 2):
                done(v.tensor_tensor(sq8[:, 0:n, :], sq8[:, 0:n, :], sq8[:, n:2 * n, :], ALU.add))
            v.tensor_tensor(sq8[:, 0, :], sq8[:, 0, :], sq8[:, 1, :], ALU.add).then_inc(s["x_added"], 1)
            dve.wait_ge(s["x_root"], 1)
            done(v.reciprocal(rstd[:, :], rstd[:, :]))

            def take_conv(k):
                dve.wait_ge(unit_done, k + 1)
                v.tensor_tensor(tiles(3, 2)[:, k, :], ps[:, k % RING, :], rstd[:, :], ALU.mult).then_inc(taken, 1)

            take_conv(0)
            take_conv(1)
            for k in range(KT):
                v.scalar_tensor_tensor(out=xin[:, k, :], in0=xin[:, k, :], scalar=col("norm_mix", k), in1=rstd[:, :],
                                       op0=ALU.mult, op1=ALU.mult).then_inc(s["h_hi"], 1)
            take_conv(2)
            dve.wait_ge(s["bd_hi"], 1)
            split_low(bdlo[:, :], wbd[:, :], bdhi[:, :], s["bd_split"])
            done(v.memset(conv[:, :], 0.0))
            for t in range(4):
                done(v.tensor_scalar(a_acc[:, t, :], a_acc[:, t, :], col("conv_b", t), None, ALU.add))
            for k in range(3, 7):
                take_conv(k)
            dve.wait_ge(s["bd_mm"], 1)
            v.tensor_tensor(sq[0:8, 0, :], ps[0:8, 3, :], rstd[0:8, :], ALU.mult).then_inc(s["bd_t"], 1)
            for k in range(0, KT, 2):
                dve.wait_ge(s["h_ready"], KT + k + 1)
                split_low(alo[:, k, :], xin[:, k, :], ahi[:, k, :], s["h_low_even"])
            take_conv(7)
            dve.wait_ge(s["sig2_ready"], 1)
            done(v.tensor_tensor(a_pad[:, :, PADC - 1:PADC - 1 + T], tiles(4), tiles(3), ALU.mult))

            def conv_step(tap):
                for t in range(4):
                    dve.wait_ge(s["taps_done"], tap * 4 + t + 1)
                    v.scalar_tensor_tensor(out=a_acc[:, t, :], in0=a_pad[:, t, bass.ds(tap, T)],
                                           scalar=cols[:, bass.ds(tap + (COLS["conv_w"] + t * PADC), 1)],
                                           in1=a_acc[:, t, :], op0=ALU.mult, op1=ALU.add).then_inc(s["taps_done"], 1)

            def conv_taps(first, n):
                with dve.Fori(0, n) as i:
                    conv_step(i + first)

            conv_taps(0, 6)
            dve.wait_ge(s["bd_ready"], 1)
            da = ps[:, 4, 0:32].rearrange("p (t e) -> p e t", e=8)[:, 4:8, :]
            v4 = lambda ap: ap.rearrange("p (h c) -> p h c", h=HEADS)
            done(v.tensor_tensor(v4(g_col), da, rows[:, 4:8].unsqueeze(2).to_broadcast([P, 4, 4]), ALU.add))
            v.scalar_tensor_tensor(out=s6, in0=g_col, scalar=-1.0, in1=g_col, op0=ALU.mult, op1=ALU.max).then_inc(s["bd_exp"], 1)
            done(v.tensor_scalar(g_col, g_col, 0.0, None, ALU.max))
            dve.wait_ge(s["bd_act"], 1)
            v.tensor_scalar(s5, s5, 1.0, None, ALU.add).then_inc(s["bd_exp"], 1)
            dve.wait_ge(s["bd_act"], 3)
            done(v.tensor_tensor(g_col, g_col, s6, ALU.add))
            v.scalar_tensor_tensor(out=v4(g_col), in0=v4(g_col), scalar=-1.0,
                                   in1=rows[:, 0:4].unsqueeze(2).to_broadcast([P, 4, 4]), op0=ALU.mult,
                                   op1=ALU.mult).then_inc(s["gb_ready"], 1)

            dve.wait_ge(z_free, 3 + 12)
            dve.wait_ge(s["early_in"], 48)
            dve.wait_ge(s["const_in"], 16)
            src = z[:, 0:4, :]
            for lv, dst in enumerate((tmp_a, tmp_b, tmp_a, tmp_b)):
                sh = 1 << lv
                done(v.tensor_copy(dst[:, lv:4, 0:sh], src[:, lv:4, 0:sh]))
                done(v.tensor_tensor(dst[:, lv:4, sh:T], src[:, lv:4, sh:T], src[:, lv:4, 0:T - sh], ALU.add))
                src = dst
            first16 = small[:, 8:12, :]
            for g in range(4):
                sums = (tmp_a, tmp_b)[g % 2][:, g, :]
                done(v.tensor_tensor(first16[:, g, :], sums[:, 0:16], head_inv[:, g, :], ALU.mult))
                done(v.tensor_tensor(first16[:, g, :], first16[:, g, :], z[:, g, 0:16], ALU.subtract))
                done(v.scalar_tensor_tensor(out=z[:, g, :], in0=sums, scalar=1.0 / (2 << g), in1=z[:, g, :],
                                            op0=ALU.mult, op1=ALU.subtract))
                ins = v.tensor_copy(z[:, g, 0:16], first16[:, g, :])
                if g < 3:
                    done(ins)
                else:
                    ins.then_inc(s["pooled"], 1)
            done(v.tensor_tensor(ws.rearrange("p (g t) -> p g t", g=4), ws.rearrange("p (g t) -> p g t", g=4),
                                 tri.unsqueeze(1).to_broadcast([P, 4, P]), ALU.mult))

            conv_taps(6, CONV_LATE - 6)

            def short_conv(dst, srcs, n, last_tell):
                for h in range(4):
                    w = lambda j: col("dn_w", (n * 4 + h) * 4 + j)
                    done(v.tensor_scalar(dst[:, h, :], srcs[:, h, :], w(3), None, ALU.mult))
                    for j in range(3):
                        sh = 3 - j
                        ins = v.scalar_tensor_tensor(out=dst[:, h, sh:T], in0=srcs[:, h, 0:T - sh], scalar=w(j),
                                                     in1=dst[:, h, sh:T], op0=ALU.mult, op1=ALU.add)
                        if h == 3 and j == 2:
                            ins.then_inc(last_tell, 1)
                        else:
                            done(ins)

            def layer_norm(ready, dst, n, tell=None):
                for t in range(NT):
                    dve.wait_ge(ready, t + 1)
                    done(v.bn_stats(stat[:, 0:6], ps[:, 4 + t, :]))
                    done(v.bn_aggr(mv[:, 2 * t:2 * t + 2], stat[:, 0:6]))
                v.tensor_copy(r_ln[:, 0:4], mv[:, 0:8].rearrange("p (t e) -> p t e", e=2)[:, :, 1]).then_inc(s["ln_var"], 1)
                dve.wait_ge(s["ln_std"], n)
                done(v.reciprocal(r_ln[:, 0:4], r_ln[:, 0:4]))
                for t in range(NT):
                    ins = v.tensor_scalar(dst[:, t, :], ps[:, 4 + t, :], mv[:, 2 * t:2 * t + 1], r_ln[:, t:t + 1],
                                          ALU.subtract, ALU.mult)
                    if t == NT - 1 and tell is not None:
                        ins.then_inc(tell, 1)
                    else:
                        done(ins)

            for g in range(4):
                dve.wait_ge(s["p_hi"], g + 1)
                split_low(blo[:, g, :], z[:, g, :], bhi[:, g, :], s["p_split"])
            layer_norm(s["vt_ready"], tiles(2), 1)
            b2 = tiles(2)
            done(v.tensor_tensor(b2, b2, gm_g.unsqueeze(1).to_broadcast([P, 4, T]), ALU.mult))
            v.tensor_tensor(b2, b2, gm_b.unsqueeze(1).to_broadcast([P, 4, T]), ALU.add).then_inc(s["vn_ready"], 1)
            dve.wait_ge(z_free, 3 + 24)
            short_conv(tmp_b, tiles(3), 0, s["conv_q"])
            bcol = lambda ap, h: ap[:, 4 * h:4 * h + 4].unsqueeze(2).to_broadcast([P, 4, P])
            b16 = lambda ap: ap.unsqueeze(2).to_broadcast([P, 16, P])
            m3 = lambda k: buf[:, k, :].rearrange("p (n t) -> p n t", n=16)
            dve.wait_ge(s["gamrow"], 1)
            v.tensor_copy(gam, ps[:, 4, 0:16]).then_inc(s["gam_ready"], 1)
            dve.wait_ge(z_free, 3 + 28)
            short_conv(tiles(3), tiles(4), 1, s["conv_q"])
            dve.wait_ge(s["gam_ready"], 1)
            dve.wait_ge(s["bd_act"], 4)
            for h in range(HEADS):
                dve.wait_ge(s["egr_ready"], h + 1)
                row = ps[:, 4 + h, :].rearrange("p (c t) -> p c t", c=4)
                done(v.tensor_copy(egl[:, 4 * h:4 * h + 4], row[:, :, P - 1]))
                v.tensor_tensor(mats(0)[:, h], row, bcol(gam, h), ALU.subtract).then_inc(s["dec_pre"], 1)
            dve.wait_ge(s["gelu_ready"], 2)
            for g in range(4):
                dve.wait_ge(s["mix_ready"], g + 1)
                bias = gm_bias[:, g * P:(g + 1) * P].unsqueeze(1).to_broadcast([P, 4, P])
                v.tensor_tensor(sq[:, g % 2, :].rearrange("p (n t) -> p n t", n=4),
                                ps[:, 4 + g, :].rearrange("p (n t) -> p n t", n=4), bias, ALU.add).then_inc(s["c_ready"], 1)
                dve.wait_ge(s["c_ready"], g + 1)
                done(v.tensor_tensor(tiles(1)[:, g, :], tiles(1)[:, g, :], sq[:, g % 2, :], ALU.mult))
            dve.wait_ge(z_free, 3 + 32)
            short_conv(tiles(4), tiles(5), 2, s["conv_q"])
            dve.wait_ge(s["dec_pre"], 4)
            dve.wait_ge(s["conv_q"], 3)
            done(v.tensor_scalar(buf[:, 5, :], buf[:, 0, :], 0.0, None, ALU.min))
            done(v.tensor_scalar(buf[:, 0, :], buf[:, 0, :], 0.0, None, ALU.max))
            v.tensor_tensor(kd_s, egl, gam, ALU.subtract).then_inc(s["decay_ready"], 1)

            def merge(name, n, taps=0, after={}):
                first = FIRST[name]
                for i in turns(dve, after, steps, 0 if n == 0 else 2):
                    for j in range(taps):
                        conv_step(i * taps + CONV_LATE + 8 * n + j)
                    dve.wait_ge(unit_done, i * 3 + first + 3)
                    dve.wait_ge(gate_free, i * 2 + 8 * n + 4)
                    for e in range(2):
                        dst = stream[:, :, :].rearrange("p a c -> p (a c)")
                        at_ = i * 2 * T + e * T
                        dst = dst[:, at_:at_ + T] if isinstance(at_, int) else dst[:, bass.ds(at_, T)]
                        if n == 0:
                            v.tensor_tensor(dst, sig[:, e, :], ps[:, 2 + e, :], ALU.mult).then_inc(merged, 1)
                        else:
                            done(v.tensor_tensor(sq[:, e, :], sig[:, e, :], ps[:, 2 + e, :], ALU.mult))
                            v.tensor_tensor(dst, dst, sq[:, e, :], ALU.add).then_inc(merged, 1)
                    dve.wait_ge(merged, i * 2 + 8 * n + 4)

            def head_sums(n):
                r = (s7, s8)[n]
                for h in range(HEADS):
                    dve.wait_ge(s["qk_sq"], 4 * n + h + 1)
                    v.tensor_reduce(r[:, 4 * h:4 * h + 4], head_sq[h], X, ALU.add).then_inc(s["qk_sum"], 1)
                dve.wait_ge(s["qk_sum"], 4 * n + 4)
                v.tensor_scalar(r, r, 1e-6, None, ALU.add).then_inc(s["qk_std"], 1)

            def normalise(n, at_):
                r = (s7, s8)[n]
                dve.wait_ge(s["std_ready"], 1 + n)
                done(v.reciprocal(r, r))
                if n == 0:
                    done(v.tensor_scalar(r, r, float(P) ** -0.5, None, ALU.mult))
                dve.wait_ge(s["qkv_tok"], 4 * n + 4)
                v.tensor_tensor(m3(at_), m3(at_), b16(r), ALU.mult).then_inc(s["qk_norm"], 1)

            def v_tokens():
                for h in range(HEADS):
                    dve.wait_ge(s["qkv_t"], 8 + h + 1)
                    v.tensor_tensor(mats(3)[:, h], ps[:, 4 + h, :].rearrange("p (c t) -> p c t", c=4), bcol(beta, h),
                                    ALU.mult).then_inc(s["v_tok"], 1)

            def decay_masks():
                dve.wait_ge(s["dec_exp"], 2)
                done(v.tensor_tensor(m3(0), m3(0), strict.unsqueeze(1).to_broadcast([P, 16, P]), ALU.mult))
                done(v.tensor_tensor(m3(0), m3(0), b16(beta), ALU.mult))
                done(v.tensor_tensor(m3(5), m3(5), tri.unsqueeze(1).to_broadcast([P, 16, P]), ALU.mult))
                done(v.scalar_tensor_tensor(out=kbe_s, in0=kbe_s, scalar=-1.0, in1=beta, op0=ALU.mult, op1=ALU.mult))

            merge("merge_p", 0, 2, after={0: lambda: head_sums(0), 1: lambda: (normalise(0, 2), head_sums(1)),
                                          2: lambda: (v_tokens(), normalise(1, 7))})
            for g in range(4):
                dve.wait_ge(s["c_hi"], g + 1)
                split_low(blo[:, g, :], tiles(1)[:, g, :], bhi[:, g, :], s["c_split"])

            def lower():
                for h in range(HEADS):
                    dve.wait_ge(s["a_mm"], h + 1)
                    v.tensor_tensor(mats(0)[:, h], mats(0)[:, h], ps[:, 4 + h, :].rearrange("p (c t) -> p c t", c=4),
                                    ALU.mult).then_inc(s["a_ready"], 1)
                done(v.tensor_tensor(buf[:, 6, :], buf[:, 6, :], buf[:, 4, :], ALU.mult))
                v.tensor_tensor(m3(7), m3(7), b16(kd_s), ALU.mult).then_inc(s["kd_ready"], 1)

            def first_inverse():
                for h in range(HEADS):
                    dve.wait_ge(s["attn_mm"], h + 1)
                    v.tensor_tensor(mats(5)[:, h], mats(5)[:, h], ps[:, 4 + h, :].rearrange("p (c t) -> p c t", c=4),
                                    ALU.mult).then_inc(s["gram_ready"], 1)
                dve.wait_ge(s["a_ready"], 4)
                for h in range(HEADS):
                    done(v.tensor_tensor(mats(4)[:, h], mats(0)[:, h], level0.unsqueeze(1).to_broadcast([P, 4, P]), ALU.mult))
                    v.tensor_tensor(mats(4)[:, h], ident.unsqueeze(1).to_broadcast([P, 4, P]), mats(4)[:, h],
                                    ALU.subtract).then_inc(s["x0_ready"], 1)

            merge("merge_c", 1, 1, after={0: decay_masks, 1: lower, 2: first_inverse})
            for lv in range(6):
                mask = const[:, CONST["levels"] + lv * 64:CONST["levels"] + (lv + 1) * 64].unsqueeze(1).to_broadcast([P, 4, 64])
                for h in range(HEADS):
                    dve.wait_ge(s["lv_t"], lv * 4 + h + 1)
                    v.tensor_tensor(level_t[:, h], ps[:, 4 + h, 0:256].rearrange("p (c t) -> p c t", c=4), mask,
                                    ALU.mult).then_inc(s["lv_masked"], 1)
                for h in range(HEADS):
                    dve.wait_ge(s["lv_p"], lv * 4 + h + 1)
                    half = right_half(tiles(2)[:, h, :], 2 << lv)
                    got = ps[:, h, 0:256].rearrange("p (b c) -> p b c", c=2 << lv)
                    v.tensor_tensor(half, half, got, ALU.subtract).then_inc(s["lv_y"], 1)
            egl_hc = egl.rearrange("p (h c) -> p h c", h=HEADS)
            for c in range(NT):
                old, new = state[:, (c + 1) % 2], state[:, c % 2]
                if c:
                    dve.wait_ge(s["ks_mm"], c)
                    for h in range(HEADS):
                        n = h * NT + c
                        v.scalar_tensor_tensor(out=mats(3)[:, h, c, :], in0=ps[:, 1, h * P:(h + 1) * P],
                                               scalar=kbe_s[:, n:n + 1], in1=mats(3)[:, h, c, :], op0=ALU.mult,
                                               op1=ALU.add).then_inc(s["rhs_ready"], 1)
                dve.wait_ge(s["v_mm"], c + 1)
                if c:
                    dve.wait_ge(s["o_mm"], c)
                v.tensor_copy(vnew[:, :, :], ps[:, 0, :].rearrange("p (h t) -> p h t", h=4)).then_inc(s["v_ready"], 1)
                if c < NT - 1:
                    if c:
                        done(v.tensor_tensor(new, old, egl_hc[:, :, c:c + 1].to_broadcast([P, 4, P]), ALU.mult))
                    dve.wait_ge(s["s_mm"], c + 1)
                    upd = ps[:, 1, :].rearrange("p (h t) -> p h t", h=4)
                    if c:
                        v.tensor_tensor(new, new, upd, ALU.add).then_inc(s["s_ready"], 1)
                    else:
                        v.tensor_copy(new, upd).then_inc(s["s_ready"], 1)
            dve.wait_ge(s["o_sq"], 1)
            done(v.tensor_reduce(s5, m3(4), X, ALU.add))
            dve.sem_inc(s["o_sum"], 1)
            dve.wait_ge(s["o_std"], 1)
            done(v.reciprocal(s5, s5))
            v.tensor_tensor(m3(0), m3(0), b16(s5), ALU.mult).then_inc(s["o_norm"], 1)
            for k in range(4):
                dve.wait_ge(unit_done, FIRST["dgate"] + k + 1)
                v.tensor_copy(tiles(6)[:, k, :], ps[:, 4 + k, :]).then_inc(taken, 1)
            for h in range(HEADS):
                dve.wait_ge(s["dg_silu"], h + 1)
                dve.wait_ge(s["o_back"], h + 1)
                v.scalar_tensor_tensor(out=tiles(1)[:, h, :], in0=ps[:, 4 + h, :], scalar=col("dn_g"), in1=tiles(6)[:, h, :],
                                       op0=ALU.mult, op1=ALU.mult).then_inc(s["o_feat"], 1)
            for h in range(HEADS):
                dve.wait_ge(s["o_hi"], h + 1)
                split_low(blo[:, h, :], tiles(1)[:, h, :], bhi[:, h, :], s["o_split"])
            merge("merge_o", 2, after={0: lambda: layer_norm(s["ca_t"], tiles(2), 2, s["ca_norm"])})
            for f in range(4):
                dve.wait_ge(s["a_hi"], f + 1)
                split_low(blo[:, f, :], tiles(3)[:, f, :], bhi[:, f, :], s["a_split"])

            def merged_low(tiles_):
                for k in tiles_:
                    dve.wait_ge(s["m_hi"], k + 1)
                    split_low(alo[:, k, :], stream[:, k, :], ahi[:, k, :], s["m_split"])

            def mem_sum():
                dve.wait_ge(s["mem_sq"], 1)
                v.tensor_reduce(rstd[:, 0:MEM], buf[:, 5, :].rearrange("p (k t) -> p t k", k=KT), X,
                                ALU.add).then_inc(s["mem_added"], 1)

            merge("merge_a", 3, after={1: mem_sum, 2: lambda: merged_low(range(6))})
            merged_low(range(6, KT))
            for k in range(KT):
                dve.wait_ge(s["m_hi2"], k + 1)
                split_low(blo[:, k // 2, (k % 2) * MEM:(k % 2 + 1) * MEM], buf[:, 4, k * MEM:(k + 1) * MEM],
                          bhi[:, k // 2, (k % 2) * MEM:(k % 2 + 1) * MEM], s["m_split2"], col("norm_mem", k))
            dve.wait_ge(s["x2_in"], 16)

            def residual(name, fn, squares, added, late=None):
                first = FIRST[name]
                done(v.memset(sq3, 0.0))
                done(v.memset(sq[:, 0, :], 0.0))
                with dve.Fori(0, 2) as i:
                    steps.enter(i, RING)
                    for j in range(RING):
                        residual_tile(first, i * RING + j, j, fn, squares, name)
                steps.leave(2)
                if late is not None:
                    late()
                for k in range(6, 8):
                    residual_tile(first, k, k, fn, squares, name)
                dve.wait_ge(squares, 9)
                v.tensor_tensor(sq[:, 0, :], sq[:, 0, :], sq3[:, (first + 7) % RING, :], ALU.add).then_inc(added, 1)

            def residual_tile(first, k, j, fn, squares, name):
                dve.wait_ge(unit_done, k + first + 1)
                fn(k, (first + j) % RING).then_inc(taken, 1)
                dve.wait_ge(squares, k + 1)
                done(v.tensor_tensor(sq[:, 0, :], sq[:, 0, :], sq3[:, (first + j - 1) % RING, :], ALU.add))

            residual("out", lambda k, slot: v.tensor_tensor(at(stream, k), ps[:, slot, :], at(buf[:, 6:8, :], k), ALU.add),
                     s["x1_sq"], s["x1_added"])
            dve.wait_ge(s["mem_std"], 1)
            v.reciprocal(rmem[:, :], rstd[:, 0:MEM]).then_inc(s["mem_r"], 1)
            dve.wait_ge(s["mem_r"], 1)
            first = FIRST["kv"]
            for k, slot, _ in units(dve, first, 16):
                dve.wait_ge(unit_done, k + first + 1)
                v.tensor_tensor(at(buf[:, 2:4, :], k, MEM), ps[:, slot, 0:MEM], rmem[:, :], ALU.mult).then_inc(taken, 1)
            for k in range(KT):
                dve.wait_ge(s["x1_hi"], k + 1)
                split_low(alo[:, k, :], stream[:, k, :], ahi[:, k, :], s["x1_split"], col("norm_xa", k))
            dve.wait_ge(taken, 3 + TAKE["q"])
            dve.wait_ge(s["x1_std"], 1)
            v.reciprocal(rstd[:, :], sq[:, 1, :]).then_inc(s["x1_r"], 1)
            dve.wait_ge(s["x1_r"], 1)
            for m in range(2):
                dve.wait_ge(s["vt2_hi"], m + 1)
                split_low(blo[:, 2 * m:2 * m + 2, :], ps[:, 3 + 2 * m:5 + 2 * m, :], bhi[:, 2 * m:2 * m + 2, :],
                          s["vt2_taken"])
            take("q", lambda k, slot: v.tensor_tensor(at(buf[:, 0:2, :], k), ps[:, slot, :], rstd[:, :], ALU.mult))
            probs = buf[:, 5:7, :].rearrange("p a (b c) -> p (a b) c", c=T)
            def normalise_probs(b):
                dve.wait_ge(s["exp_done"], 2 * b + 2)
                done(v.reciprocal(denom[:, 2 * b:2 * b + 2], denom[:, 2 * b:2 * b + 2]))
                pb = probs[:, b, :].rearrange("p (e m) -> p e m", e=2)
                v.tensor_tensor(pb, pb, denom[:, 2 * b:2 * b + 2].unsqueeze(2).to_broadcast([P, 2, MEM]),
                                ALU.mult).then_inc(s["probs_ready"], 1)

            for b in range(8):
                dve.wait_ge(s["score_mm"], b + 1)
                done(v.reduce_max(negmax[:, 2 * b:2 * b + 2], ps[:, b, :].rearrange("p (e m) -> p e m", e=2), X))
                v.tensor_scalar(negmax[:, 2 * b:2 * b + 2], negmax[:, 2 * b:2 * b + 2], -1.0 / 16.0, None,
                                ALU.mult).then_inc(s["nmax"], 1)
                if b:
                    normalise_probs(b - 1)
            normalise_probs(7)
            for b in range(8):
                dve.wait_ge(s["ao_hi"], b + 1)
                at_ = slice(2 * (b // 2), 2 * (b // 2) + 2), slice((b % 2) * MEM, (b % 2 + 1) * MEM)
                split_low(alo[:, at_[0], at_[1]], ps[:, b, :].rearrange("p (m t) -> p m t", m=2),
                          ahi[:, at_[0], at_[1]], s["pt_ready"])
            for f in range(KT):
                dve.wait_ge(s["ao_hi"], 8 + f + 1)
                split_low(alo[:, f, :], ps[:, f, :], ahi[:, f, :], s["ao_split"])
            def x2_low(tiles_):
                for k in tiles_:
                    dve.wait_ge(s["x2_hi"], k + 1)
                    hi, lo = (bhi, blo) if k < 4 else (ahi, alo)
                    split_low(lo[:, k, :], stream[:, k, :], hi[:, k, :], s["x2_split"], col("norm_mlp", k))

            residual("wo", lambda k, slot: v.tensor_tensor(at(stream, k), at(stream, k), ps[:, slot, :], ALU.add),
                     s["x2_sq"], s["x2_added"], late=lambda: x2_low(range(4)))
            x2_low(range(4, KT))
            dve.wait_ge(s["x2_std"], 1)
            v.reciprocal(rstd[:, :], sq[:, 1, :]).then_inc(s["x2_r"], 1)
            dve.wait_ge(s["x2_r"], 1)
            w1 = FIRST["w1"]
            def hidden(skip, count):
                for k_, slot, _ in units(dve, w1 + skip, count):
                    k = k_ + skip
                    dve.wait_ge(unit_done, k + w1 + 1)
                    v.tensor_tensor(sq[:, 0, :], ps[:, slot, :], rstd[:, :], ALU.mult).then_inc(taken, 1)
                    dve.wait_ge(taken, k + 3 + TAKE["w1"] + 1)
                    v.scalar_tensor_tensor(out=at(buf, k), in0=sq[:, 0, :], scalar=0.0, in1=sq[:, 0, :], op0=ALU.max,
                                           op1=ALU.mult).then_inc(s["h1_ready"], 1)
                    dve.wait_ge(s["h1_ready"], k + 1)

            def hidden_low(skip, count):
                for k_, slot, _ in units(dve, FIRST["w2"] + skip, count):
                    dve.wait_ge(s["h1_hi"], k_ + skip + 1)
                    split_low(alo[:, slot, :], at(buf, k_ + skip), ahi[:, slot, :], s["h1_split"])

            hidden(0, 27)
            hidden_low(0, 3)
            hidden(27, 5)
            hidden_low(3, 29)
            x2_tok = conv[:, 0:4096].rearrange("p (t d) -> p t d", t=NT)
            gain = sig[:, :, :].rearrange("p a c -> p (a c)")
            dve.wait_ge(s["f_in"], 16)
            def add_tile(t, halves=(0, 2), mm=0):
                dve.wait_ge(s["y_mm"], t + 1 + mm)
                rows2 = x2_tok[:, t, :].rearrange("p (a c) -> p a c", a=2)[:, halves[0]:halves[1], :]
                v.tensor_tensor(rows2, rows2, ps[:, 2 * t + halves[0]:2 * t + halves[1], :], ALU.add).then_inc(s["y_ready"], 1)

            def finish_tile(t):
                dve.wait_ge(s["y_std"], t + 1)
                done(v.reciprocal(denom[:, 8 + t:9 + t], denom[:, 8 + t:9 + t]))
                for cut in (slice(0, D),) if t < NT - 1 else (slice(0, T), slice(T, D)):
                    v.scalar_tensor_tensor(out=x2_tok[:, t, cut], in0=x2_tok[:, t, cut], scalar=denom[:, 8 + t:9 + t],
                                           in1=gain[:, cut], op0=ALU.mult, op1=ALU.mult).then_inc(s["y_out"], 1)

            add_tile(0)
            add_tile(1)
            finish_tile(0)
            add_tile(2)
            finish_tile(1)
            add_tile(3, (0, 1))
            finish_tile(2)
            add_tile(3, (1, 2), 1)
            finish_tile(3)


def _blocks(w, first, n):
    k = w.shape[0] // P
    return w[:, first:first + n * P].reshape(k, P, n, P).transpose(2, 1, 0, 3).reshape(n, P, k * P)


def _stream(w_in, w_branch, w_out, wq, wkv, wo, w1, w2):
    conv_at, q_at = 0, 2 * MIX
    gm_at = q_at + 4 * MIX + 2 * HEADS
    pool_at = gm_at + 2 * MIX
    gate_at = pool_at + MIX
    parts = [_blocks(w_in, conv_at + MIX, 4), _blocks(w_in, conv_at, 4), _blocks(w_in, pool_at, 4),
             _blocks(w_in, gm_at, 8), _blocks(w_in, q_at, 12)]

    def merge(b):
        gates = _blocks(w_in, gate_at + b * D, KT)
        proj = w_branch[b].reshape(MT, P, KT // 2, 2, P).transpose(2, 1, 0, 3, 4).reshape(KT // 2, P, 1024)
        return np.stack([gates[0::2], gates[1::2], proj], 1).reshape(12, P, 1024)

    parts += [merge(3), merge(2), _blocks(w_in, q_at + 3 * MIX, 4), merge(1), merge(0)]
    parts += [_blocks(w_out, 0, 8), _blocks(wkv, 0, 16), _blocks(wq, 0, 8), _blocks(wo, 0, 8), _blocks(w1, 0, 32)]
    parts.append(w2.reshape(FFN // P, P, D))
    return np.concatenate(parts, 0)


def _cols(a):
    return a.reshape(-1, P).T


def _constants():
    i = np.arange(P)
    row, colm = i[:, None], i[None, :]
    level = lambda s: (row // (2 * s) == colm // (2 * s)) & (row % (2 * s) < s) & (colm % (2 * s) >= s)
    parts = [row == colm, row <= colm, row > colm, level(1).T]
    parts += [level(2 << n).reshape(P, -1, 2, 2 << n)[:, :, 1].reshape(P, 64) for n in range(6)]
    t = np.arange(16)
    head = np.stack([1.0 / np.minimum(t + 1, 2 << g) for g in range(4)]).reshape(1, 64)
    parts.append(np.broadcast_to(head, (P, 64)))
    return np.concatenate([p.astype(np.float32) for p in parts], 1)


def kernel(x, mem, norm_mix, w_in, conv_a_w, conv_a_b, ln_a_g, ln_a_b, dn_conv_w, dn_a_log, dn_dt_bias,
           dn_norm_g, gm_ln_g, gm_ln_b, gm_ws, gm_bs, pool_w, pool_scale, w_branch, w_out, norm_xa, norm_mem,
           xa_wq, xa_wkv, xa_wo, norm_mlp, mlp_w1, mlp_w2, norm_f):
    import concourse.bacc as bacc
    from concourse.bass_utils import run_bass_kernel_spmd as run

    f32 = np.float32
    ar = lambda a: np.asarray(a)
    bd_at = 2 * MIX + 4 * MIX
    conv_w = np.concatenate([np.zeros((1, MIX), f32), ar(conv_a_w)[0]], 0)
    arrays = {
        "wall": _stream(ar(w_in)[0], ar(w_branch)[0], ar(w_out)[0], ar(xa_wq)[0], ar(xa_wkv)[0], ar(xa_wo)[0],
                        ar(mlp_w1)[0], ar(mlp_w2)[0]),
        "x_t": ar(x)[0].T.reshape(KT, P, T).transpose(1, 0, 2),
        "mem_t": ar(mem)[0].T.reshape(KT, P, MEM).transpose(1, 0, 2).reshape(P, KT * MEM),
        "w_bd": ar(w_in)[0][:, bd_at:bd_at + 8].reshape(KT, P, 8).transpose(1, 0, 2).reshape(P, KT * 8),
        "cols_d": np.concatenate([
            _cols(ar(norm_mix)[0]), _cols(ar(norm_xa)[0]), _cols(ar(norm_mem)[0]), _cols(ar(norm_mlp)[0]),
            conv_w.reshape(PADC, 4, P).transpose(2, 1, 0).reshape(P, 4 * PADC), _cols(ar(conv_a_b)[0]),
            _cols(ar(ln_a_g)[0]), _cols(ar(ln_a_b)[0]),
            ar(dn_conv_w)[0].reshape(4, 12, P).transpose(2, 1, 0).reshape(P, 48),
            _cols(ar(dn_norm_g)[0]), _cols(ar(pool_scale)[0]), np.full((P, 1), 1e-6, f32), np.full((P, 1), 1e-5, f32)], 1),
        "rows_d": np.concatenate([ar(dn_a_log)[0], ar(dn_dt_bias)[0]]),
        "gains_d": np.concatenate([ar(gm_ln_g)[0], ar(gm_ln_b)[0], ar(gm_bs)[0].reshape(-1)]),
        "ws_t": ar(gm_ws)[0].transpose(2, 0, 1).reshape(P, 4 * P),
        "pool_w": ar(pool_w)[0].transpose(1, 0, 2).reshape(P, 4 * P),
        "const_d": _constants(),
        "norm_f": ar(norm_f),
    }
    arrays = {n: np.ascontiguousarray(a) for n, a in arrays.items()}
    nc = bacc.Bacc("TRN2", target_bir_lowering=False, num_devices=1)
    args = {n: nc.dram_tensor(n, a.shape, mybir.dt.from_np(a.dtype), kind="ExternalInput").ap() for n, a in arrays.items()}
    args["out"] = nc.dram_tensor("out", (1, T, D), F32, kind="ExternalOutput").ap()
    trunk(nc, **args)
    r = run(nc, [arrays], core_ids=[0])
    return r.results[0]["out"]
```
